# Optimizing a Trainium2 kernel written in Bass

```python
import math
import jax, jax.numpy as jnp
from jax import lax
import numpy as np

D_MODEL = 1024
BATCH = 1
SEQ = 128
DEPTH = 2
DEC_BATCH = 1
DEC_SEQ = 256
PAST_LEN = 128

GRID_W = 64
BRANCH_W = 512
N_BRANCH = 4
H_M = 4
DK_M = 128
DV_M = 128
H_D = 4
DQK_D = 64
DV_D = 128
H_G = 4
DK_G = 64
DV_G = 128
GATE_RANK = 16
GLA_TAU = 16.0
CONV_W = 31
N_GROUPS = 4
EXPERTS_PER_GROUP = 4
TOP_K = 2
D_EXPERT = 512
CHUNK = 64
QBLOCK = 128
ROPE_BASE = 10000.0
EPS = 1e-6
N_MOD = 6

IN_SIZES = (H_M * DK_M, H_M * DK_M, H_M * DV_M, H_M * DV_M, 2 * H_M, 2 * H_M,
            H_D * 2 * DQK_D, H_D * 2 * DQK_D, H_D * DV_D,
            H_G * DK_G, H_G * DK_G, H_G * DV_G, 2 * GATE_RANK, H_G * DV_G,
            BRANCH_W, BRANCH_W,
            N_BRANCH * D_MODEL)
N_IN = sum(IN_SIZES)

kernel_name = 'hybrid_mlstm_diffattn_gla_conv_hmoe_dit_step'

def _split_offsets():
    out, acc = [], 0
    for s in IN_SIZES[:-1]:
        acc += s
        out.append(acc)
    return out

def _rms(x, g):
    xf = x.astype(jnp.float32)
    y = xf * lax.rsqrt(jnp.mean(xf * xf, axis=-1, keepdims=True) + EPS)
    return (y * g.astype(jnp.float32)).astype(x.dtype)

def _layernorm(x, g, b):
    xf = x.astype(jnp.float32)
    mu = jnp.mean(xf, axis=-1, keepdims=True)
    xc = xf - mu
    y = xc * lax.rsqrt(jnp.mean(xc * xc, axis=-1, keepdims=True) + EPS)
    return (y * g.astype(jnp.float32) + b.astype(jnp.float32)).astype(x.dtype)

def _grid_angles(S):
    rows = S // GRID_W
    r, col = jnp.meshgrid(jnp.arange(rows, dtype=jnp.float32), jnp.arange(GRID_W, dtype=jnp.float32), indexing='ij')
    r, col = r.reshape(-1), col.reshape(-1)
    n_freq = DQK_D // 4
    inv = ROPE_BASE ** (-jnp.arange(n_freq, dtype=jnp.float32) / n_freq)
    ang = jnp.concatenate([r[:, None] * inv, col[:, None] * inv], axis=-1)
    return jnp.cos(ang), jnp.sin(ang)

def _rope(x, cos, sin):
    half = x.shape[-1] // 2
    x1, x2 = x[..., :half], x[..., half:]
    shape = (1, cos.shape[0]) + (1,) * (x.ndim - 3) + (half,)
    cs, sn = cos.reshape(shape).astype(x.dtype), sin.reshape(shape).astype(x.dtype)
    return jnp.concatenate([x1 * cs - x2 * sn, x1 * sn + x2 * cs], axis=-1)

def _chunks(a):
    B, H, S = a.shape[:3]
    return jnp.moveaxis(a.reshape((B, H, S // CHUNK, CHUNK) + a.shape[3:]), 2, 0)

def _unchunk(a):
    a = jnp.moveaxis(a, 0, 2)
    return a.reshape((a.shape[0], a.shape[1], -1) + a.shape[4:])

def _mlstm_chunkwise(q, k, v, ig, lf, C0, n0, m0):
    causal = jnp.tril(jnp.ones((CHUNK, CHUNK), bool))

    def step(carry, inp):
        C, n, m = carry
        qc, kc, vc, ic, fc = inp
        b = jnp.cumsum(fc, axis=-1)
        log_d = jnp.where(causal, b[..., :, None] - b[..., None, :] + ic[..., None, :], -jnp.inf)
        log_inter = b + m[..., None]
        m_t = jnp.maximum(log_inter, jnp.max(log_d, axis=-1))
        a_inter = jnp.exp(log_inter - m_t)
        s = jnp.einsum('bhtd,bhsd->bhts', qc, kc) * jnp.exp(log_d - m_t[..., None])
        num = a_inter[..., None] * jnp.einsum('bhtd,bhde->bhte', qc, C) + jnp.einsum('bhts,bhse->bhte', s, vc)
        den = a_inter * jnp.einsum('bhtd,bhd->bht', qc, n) + jnp.sum(s, axis=-1)
        h = num / jnp.maximum(jnp.abs(den), jnp.exp(-m_t))[..., None]
        b_last = b[..., -1]
        log_src = b_last[..., None] - b + ic
        m_new = jnp.maximum(b_last + m, jnp.max(log_src, axis=-1))
        a_c = jnp.exp(b_last + m - m_new)
        w = jnp.exp(log_src - m_new[..., None])
        C = a_c[..., None, None] * C + jnp.einsum('bhs,bhsd,bhse->bhde', w, kc, vc)
        n = a_c[..., None] * n + jnp.einsum('bhs,bhsd->bhd', w, kc)
        return (C, n, m_new), h

    init = (C0.astype(jnp.float32), n0.astype(jnp.float32), m0.astype(jnp.float32))
    (C, n, m), hs = lax.scan(step, init, (_chunks(q), _chunks(k), _chunks(v), _chunks(ig), _chunks(lf)))
    return _unchunk(hs), C, n, m

def _gla_chunkwise(q, k, v, la, S0):
    causal = jnp.tril(jnp.ones((CHUNK, CHUNK), bool))[:, :, None]

    def step(st, inp):
        qc, kc, vc, lc = inp
        g = jnp.cumsum(lc, axis=2)
        dec = jnp.exp(jnp.where(causal, g[:, :, :, None, :] - g[:, :, None, :, :], -jnp.inf))
        att = jnp.einsum('bhtd,bhsd,bhtsd->bhts', qc, kc, dec)
        o = jnp.einsum('bhtd,bhde->bhte', qc * jnp.exp(g), st) + jnp.einsum('bhts,bhse->bhte', att, vc)
        g_last = g[:, :, -1:, :]
        st = jnp.exp(g_last[:, :, 0, :, None]) * st + jnp.einsum('bhsd,bhse->bhde', kc * jnp.exp(g_last - g), vc)
        return st, o

    S_fin, o = lax.scan(step, S0.astype(jnp.float32), (_chunks(q), _chunks(k), _chunks(v), _chunks(la)))
    return _unchunk(o), S_fin

def _diff_attention(q, k, v, lam):
    B, Sq, H = q.shape[:3]
    nb = Sq // QBLOCK
    qb = jnp.moveaxis(q.reshape(B, nb, QBLOCK, H, 2, DQK_D), 1, 0)
    scale = DQK_D ** -0.5

    def block(qi):
        s = jnp.einsum('bqhcd,bkhcd->bhcqk', qi, k).astype(jnp.float32) * scale
        pr = jax.nn.softmax(s, axis=-1)
        w = (pr[:, :, 0] - lam * pr[:, :, 1]).astype(v.dtype)
        return jnp.einsum('bhqk,bkhe->bqhe', w, v)

    o = lax.map(block, qb)
    return jnp.moveaxis(o, 0, 1).reshape(B, Sq, H, DV_D)

def _mixer(h, p, lam_init, ctx):
    B, S, _ = h.shape
    dt = h.dtype
    proj = h @ p['w_in']
    (m_q, m_k, m_v, m_o, m_i, m_f, d_q, d_k, d_v,
     g_q, g_k, g_v, g_a, g_r, c_a, c_b, gate) = jnp.split(proj, _split_offsets(), axis=-1)
    flip = lambda a: jnp.flip(a, axis=2)
    heads = lambda a, n: a.reshape(B, S, n, -1).transpose(0, 2, 1, 3).astype(jnp.float32)

    mq = heads(m_q, H_M)
    mk = heads(m_k, H_M) * DK_M ** -0.5
    mv = heads(m_v, H_M)
    mi = (m_i.reshape(B, S, 2, H_M) + p['b_m_i'].reshape(2, H_M)).astype(jnp.float32).transpose(0, 2, 3, 1)
    mf = jax.nn.log_sigmoid((m_f.reshape(B, S, 2, H_M) + p['b_m_f'].reshape(2, H_M)).astype(jnp.float32)).transpose(0, 2, 3, 1)
    if ctx is None:
        C0 = jnp.zeros((B, 2, H_M, DK_M, DV_M), jnp.float32)
        n0 = jnp.zeros((B, 2, H_M, DK_M), jnp.float32)
        m0 = jnp.zeros((B, 2, H_M), jnp.float32)
        S0 = jnp.zeros((B, 2, H_G, DK_G, DV_G), jnp.float32)
    else:
        C0, n0, m0, S0 = ctx['C'], ctx['n'], ctx['m'], ctx['S']
    hf, Cf, nf, mf_fin = _mlstm_chunkwise(mq, mk, mv, mi[:, 0], mf[:, 0], C0[:, 0], n0[:, 0], m0[:, 0])
    hb, Cb, nb, mb_fin = _mlstm_chunkwise(flip(mq), flip(mk), flip(mv), flip(mi[:, 1]), flip(mf[:, 1]),
                                          C0[:, 1], n0[:, 1], m0[:, 1])
    hm = (hf + flip(hb)).transpose(0, 2, 1, 3)
    y_m = _rms(hm, p['hnorm_m'].reshape(H_M, DV_M)).reshape(B, S, BRANCH_W).astype(dt) * jax.nn.sigmoid(m_o)

    dq = d_q.reshape(B, S, H_D, 2, DQK_D)
    dk = d_k.reshape(B, S, H_D, 2, DQK_D)
    dv = d_v.reshape(B, S, H_D, DV_D)
    if ctx is None:
        k_all, v_all = dk, dv
    else:
        cos, sin = _grid_angles(S)
        dq = _rope(dq, cos, sin)
        n_ctx = ctx['k'].shape[1]
        k_all = jnp.concatenate([_rope(dk, cos, sin), ctx['k'].reshape(B, n_ctx, H_D, 2, DQK_D).astype(dk.dtype)], axis=1)
        v_all = jnp.concatenate([dv, ctx['v'].astype(dv.dtype)], axis=1)
    lq1, lk1 = p['lam_q1'].astype(jnp.float32), p['lam_k1'].astype(jnp.float32)
    lq2, lk2 = p['lam_q2'].astype(jnp.float32), p['lam_k2'].astype(jnp.float32)
    lam = jnp.exp(jnp.sum(lq1 * lk1)) - jnp.exp(jnp.sum(lq2 * lk2)) + lam_init
    od = _diff_attention(dq, k_all, v_all, lam)
    y_d = (_rms(od, p['hnorm_d'].reshape(H_D, DV_D)) * (1.0 - lam_init)).reshape(B, S, BRANCH_W).astype(dt)

    gq = heads(g_q, H_G) * DK_G ** -0.5
    gk = heads(g_k, H_G)
    gv = heads(g_v, H_G)
    la = jnp.einsum('bsjr,jrk->bsjk', g_a.reshape(B, S, 2, GATE_RANK), p['w_gla_up']) + p['b_gla_gate']
    la = jax.nn.log_sigmoid(la.astype(jnp.float32)) / GLA_TAU
    la = la.reshape(B, S, 2, H_G, DK_G).transpose(0, 2, 3, 1, 4)
    of, Sf = _gla_chunkwise(gq, gk, gv, la[:, 0], S0[:, 0])
    ob, Sb = _gla_chunkwise(flip(gq), flip(gk), flip(gv), flip(la[:, 1]), S0[:, 1])
    og = (of + flip(ob)).transpose(0, 2, 1, 3)
    y_g = _rms(og, p['hnorm_g'].reshape(H_G, DV_G)).reshape(B, S, BRANCH_W).astype(dt) * jax.nn.silu(g_r)

    u = c_a * jax.nn.sigmoid(c_b)
    u = lax.conv_general_dilated(u, p['w_dw'][:, None, :].astype(u.dtype), window_strides=(1,),
                                 padding=[(CONV_W // 2, CONV_W // 2)],
                                 dimension_numbers=('NWC', 'WIO', 'NWC'), feature_group_count=BRANCH_W)
    y_c = jax.nn.silu(_layernorm(u, p['conv_ln_g'], p['conv_ln_b'])).astype(dt)

    ys = jnp.stack([y_m, y_d, y_g, y_c], axis=2)
    br = jnp.einsum('bsnw,nwd->bsnd', ys, p['w_branch'])
    gts = jax.nn.sigmoid(gate.reshape(B, S, N_BRANCH, D_MODEL))
    out = jnp.einsum('bsnd,bsnd->bsd', gts, br) @ p['w_out']
    if ctx is None:
        state = (d_k.reshape(B, S, H_D, 2 * DQK_D), dv,
                 jnp.stack([Cf, Cb], axis=1), jnp.stack([nf, nb], axis=1),
                 jnp.stack([mf_fin, mb_fin], axis=1), jnp.stack([Sf, Sb], axis=1))
        return out, state
    return out, None

def _hier_moe(h, p):
    B, S, _ = h.shape
    gl = (h @ p['w_group_router']).astype(jnp.float32)
    g_sel = jax.nn.one_hot(jnp.argmax(gl, axis=-1), N_GROUPS, dtype=jnp.float32)
    g_p = jnp.sum(jax.nn.softmax(gl, axis=-1) * g_sel, axis=-1)
    el = (h @ p['w_expert_router']).astype(jnp.float32).reshape(B, S, N_GROUPS, EXPERTS_PER_GROUP)
    el_sel = jnp.einsum('bsge,bsg->bse', el, g_sel)
    top_v, top_i = lax.top_k(el_sel, TOP_K)
    top_w = jax.nn.softmax(top_v, axis=-1) * g_p[..., None]
    w_loc = jnp.einsum('bsk,bske->bse', top_w, jax.nn.one_hot(top_i, EXPERTS_PER_GROUP, dtype=jnp.float32))
    w_all = (g_sel[..., None] * w_loc[..., None, :]).astype(h.dtype)
    y = jnp.zeros_like(h)
    for gi in range(N_GROUPS):
        a = jnp.einsum('bsd,edf->bsef', h, p['w_e1'][gi])
        b = jnp.einsum('bsd,edf->bsef', h, p['w_e3'][gi])
        y = y + jnp.einsum('bsef,efd->bsd', jax.nn.silu(a) * b * w_all[:, :, gi, :, None], p['w_e2'][gi])
    return y

def _layer(x, cond, p, lam_init, ctx):
    mod = (jax.nn.silu(cond) @ p['w_mod'] + p['b_mod'])[:, None, :]
    sh1, sc1, g1, sh2, sc2, g2 = jnp.split(mod, N_MOD, axis=-1)
    h = _rms(x, p['norm1']) * (1 + sc1) + sh1
    out, state = _mixer(h, p, lam_init, ctx)
    x = x + g1 * out
    h = _rms(x, p['norm2']) * (1 + sc2) + sh2
    x = x + g2 * _hier_moe(h, p)
    return x, state

def setup_inputs(seed: int = 0) -> dict:
    key = jax.random.key(seed)
    ks = iter(jax.random.split(key, 48))
    nrm = lambda shape, s: jax.random.normal(next(ks), shape, jnp.float32) * s
    D = D_MODEL
    inp = {}
    inp['x_prompt'] = nrm((BATCH, SEQ, D), 1.0)
    inp['x_sample'] = nrm((DEC_BATCH, DEC_SEQ, D), 1.0)
    inp['c'] = nrm((DEC_BATCH, D), 1.0)
    inp['cache_diff_k'] = nrm((DEC_BATCH, DEPTH, PAST_LEN, H_D, 2 * DQK_D), 1.0)
    inp['cache_diff_v'] = nrm((DEC_BATCH, DEPTH, PAST_LEN, H_D, DV_D), 1.0)
    inp['state_mlstm_C'] = nrm((DEC_BATCH, DEPTH, 2, H_M, DK_M, DV_M), 0.5)
    inp['state_mlstm_n'] = nrm((DEC_BATCH, DEPTH, 2, H_M, DK_M), 0.5)
    inp['state_mlstm_m'] = nrm((DEC_BATCH, DEPTH, 2, H_M), 0.5)
    inp['state_gla_S'] = nrm((DEC_BATCH, DEPTH, 2, H_G, DK_G, DV_G), 0.5)
    inp['c_ctx'] = nrm((D,), 1.0)
    inp['w_mod'] = nrm((DEPTH, D, N_MOD * D), 0.5 * D ** -0.5)
    inp['b_mod'] = nrm((DEPTH, N_MOD * D), 0.02)
    inp['norm1'] = 1.0 + nrm((DEPTH, D), 0.02)
    inp['w_in'] = nrm((DEPTH, D, N_IN), D ** -0.5)
    inp['b_m_i'] = nrm((DEPTH, 2 * H_M), 0.1)
    inp['b_m_f'] = 3.0 + nrm((DEPTH, 2 * H_M), 0.5)
    inp['lam_q1'] = nrm((DEPTH, DQK_D), 0.1)
    inp['lam_k1'] = nrm((DEPTH, DQK_D), 0.1)
    inp['lam_q2'] = nrm((DEPTH, DQK_D), 0.1)
    inp['lam_k2'] = nrm((DEPTH, DQK_D), 0.1)
    inp['w_gla_up'] = nrm((DEPTH, 2, GATE_RANK, H_G * DK_G), GATE_RANK ** -0.5)
    inp['b_gla_gate'] = nrm((DEPTH, 2, H_G * DK_G), 0.1)
    inp['w_dw'] = nrm((DEPTH, CONV_W, BRANCH_W), CONV_W ** -0.5)
    inp['conv_ln_g'] = 1.0 + nrm((DEPTH, BRANCH_W), 0.02)
    inp['conv_ln_b'] = nrm((DEPTH, BRANCH_W), 0.02)
    inp['hnorm_m'] = 1.0 + nrm((DEPTH, BRANCH_W), 0.02)
    inp['hnorm_d'] = 1.0 + nrm((DEPTH, BRANCH_W), 0.02)
    inp['hnorm_g'] = 1.0 + nrm((DEPTH, BRANCH_W), 0.02)
    inp['w_branch'] = nrm((DEPTH, N_BRANCH, BRANCH_W, D), BRANCH_W ** -0.5)
    inp['w_out'] = nrm((DEPTH, D, D), D ** -0.5)
    inp['norm2'] = 1.0 + nrm((DEPTH, D), 0.02)
    inp['w_group_router'] = nrm((DEPTH, D, N_GROUPS), D ** -0.5)
    inp['w_expert_router'] = nrm((DEPTH, D, N_GROUPS * EXPERTS_PER_GROUP), D ** -0.5)
    inp['w_e1'] = nrm((DEPTH, N_GROUPS, EXPERTS_PER_GROUP, D, D_EXPERT), D ** -0.5)
    inp['w_e3'] = nrm((DEPTH, N_GROUPS, EXPERTS_PER_GROUP, D, D_EXPERT), D ** -0.5)
    inp['w_e2'] = nrm((DEPTH, N_GROUPS, EXPERTS_PER_GROUP, D_EXPERT, D), D_EXPERT ** -0.5)
    inp['final_norm'] = 1.0 + nrm((D,), 0.02)
    return inp

def reference(x_prompt, x_sample, c, cache_diff_k, cache_diff_v, state_mlstm_C, state_mlstm_n,
              state_mlstm_m, state_gla_S, c_ctx, w_mod, b_mod, norm1, w_in, b_m_i, b_m_f,
              lam_q1, lam_k1, lam_q2, lam_k2, w_gla_up, b_gla_gate, w_dw, conv_ln_g, conv_ln_b,
              hnorm_m, hnorm_d, hnorm_g, w_branch, w_out, norm2, w_group_router, w_expert_router,
              w_e1, w_e3, w_e2, final_norm):
    cond_ctx = jnp.broadcast_to(c_ctx, (x_prompt.shape[0], D_MODEL))
    yp, ys = x_prompt, x_sample
    ks, vs, Cs, ns, ms, Ss = [], [], [], [], [], []
    for l in range(DEPTH):
        p = {'w_mod': w_mod[l], 'b_mod': b_mod[l], 'norm1': norm1[l], 'w_in': w_in[l],
             'b_m_i': b_m_i[l], 'b_m_f': b_m_f[l], 'lam_q1': lam_q1[l], 'lam_k1': lam_k1[l],
             'lam_q2': lam_q2[l], 'lam_k2': lam_k2[l], 'w_gla_up': w_gla_up[l], 'b_gla_gate': b_gla_gate[l],
             'w_dw': w_dw[l], 'conv_ln_g': conv_ln_g[l], 'conv_ln_b': conv_ln_b[l],
             'hnorm_m': hnorm_m[l], 'hnorm_d': hnorm_d[l], 'hnorm_g': hnorm_g[l],
             'w_branch': w_branch[l], 'w_out': w_out[l], 'norm2': norm2[l],
             'w_group_router': w_group_router[l], 'w_expert_router': w_expert_router[l],
             'w_e1': w_e1[l], 'w_e3': w_e3[l], 'w_e2': w_e2[l]}
        lam_init = 0.8 - 0.6 * math.exp(-0.3 * l)
        yp, st = _layer(yp, cond_ctx, p, lam_init, None)
        ks.append(st[0]); vs.append(st[1]); Cs.append(st[2]); ns.append(st[3]); ms.append(st[4]); Ss.append(st[5])
        ctx = {'k': cache_diff_k[:, l], 'v': cache_diff_v[:, l], 'C': state_mlstm_C[:, l],
               'n': state_mlstm_n[:, l], 'm': state_mlstm_m[:, l], 'S': state_gla_S[:, l]}
        ys, _ = _layer(ys, c, p, lam_init, ctx)
    y_prompt = _rms(yp, final_norm)
    y_sample = _rms(ys, final_norm)
    return (y_prompt, y_sample, jnp.stack(ks, axis=1), jnp.stack(vs, axis=1), jnp.stack(Cs, axis=1),
            jnp.stack(ns, axis=1), jnp.stack(ms, axis=1), jnp.stack(Ss, axis=1))


_drawn_inputs = setup_inputs


def setup_inputs(seed=0):
    import zlib

    import numpy as np

    out = dict(_drawn_inputs(seed))
    spreads = {}
    factors = {'state_mlstm_n': 4.721,
     'state_mlstm_m': 6.102,
     'state_gla_S': 7.483,
     'lam_k1': 3.443,
     'lam_q2': 4.536,
     'lam_k2': 8.0,
     'conv_ln_g': 8.0,
     'conv_ln_b': 8.0,
     'hnorm_m': 8.0,
     'hnorm_d': 7.784,
     'hnorm_g': 8.0,
     'norm2': 3.544}
    for name, (base, spread) in spreads.items():
        noise = np.random.default_rng([zlib.crc32(name.encode()), seed]).standard_normal(out[name].shape)
        drawn = base * np.exp(spread * noise) if base else spread * noise
        out[name] = __import__('jax').numpy.asarray(drawn.astype(out[name].dtype))
    for name, factor in factors.items():
        out[name] = (out[name] * factor).astype(out[name].dtype)
    return out
```

```python
import math
from contextlib import ExitStack

import concourse.bass as bass
from concourse import mybir

F32 = mybir.dt.float32
ACT = mybir.ActivationFunctionType
ALU = mybir.AluOpType
AX = mybir.AxisListType

P = 128
D = 1024
DEPTH = 2
SEQ = 128
DEC = 256
T = SEQ + DEC
NT = T // P
KD = D // P
W = 512
H = 4
DK_M, DQK, DK_G, DV = 128, 64, 64, 128
CW = 31
PAD = CW // 2
UPAD = PAD + SEQ + PAD + DEC + PAD
NG, EPG, DE = 4, 4, 512
NE = NG * EPG
EPS = 1e-6
LEVELS = 7
M_SCALE = DK_M ** -0.5
D_SCALE = DQK ** -0.5
G_SCALE = DK_G ** -0.5
MASKED = -1e30

GR, CA, CB, GQK, DQ, DKK, MO, MQ, MK = range(9)
NCH = 9
NTOK = 3
NMOD = 12
RING = 3

PAR = {}
_c = 0
for _n, _w in (("norm1", KD), ("norm2", KD), ("bmod", 6 * KD), ("taps", 4 * CW), ("ln_g", 4), ("ln_b", 4),
               ("hn_m", 4), ("hn_d", 4), ("hn_g", 4), ("lam", 4), ("b_i", 1), ("b_f", 1), ("m0", 1),
               ("router", KD * 20), ("w_up", 512),
               ("S0", 2 * 2 * P), ("C0", 2 * H * (DV + 1)), ("k_cache", H * P), ("v_cache", H * P)):
    PAR[_n] = (_c, _c + _w)
    _c += _w
NPAR = _c
NEARLY = KD * (P + 32)

CST = {}
_c = 0
for _n, _w in (("ident", P), ("swap", P), ("cos", DEC), ("sin", DEC), ("tri_f", P), ("tri_b", P), ("ones", P),
               ("neg_f", P), ("neg_b", P), ("lev_f", 8 * P), ("lev_b", 8 * P), ("sixteenth", P), ("zero", 1), ("final", KD),
               ("lam_init", DEPTH), ("one_less", DEPTH), ("order", NG), ("cond", KD * 2)):
    CST[_n] = (_c, _c + _w)
    _c += _w
NCST = _c


def tok(t):
    return slice(t * P, (t + 1) * P)


CTX, LAT = slice(0, SEQ), slice(SEQ, T)


class Signal:

    def __init__(self, sem, per_layer, credit=0):
        self.sem, self.per_layer, self.credit = sem, per_layer, credit

    def at(self, layer, k):
        return layer * self.per_layer + (k + self.credit)


class Chain:

    def __init__(self, engine, sem, per_layer):
        self.engine, self.sem, self.per_layer, self.n = engine, sem, per_layer, 0
        self.layer = 0

    def step(self, instruction):
        instruction.then_inc(self.sem, 1)
        self.n += 1

    def settle(self, but=0):
        self.engine.wait_ge(self.sem, self.layer * self.per_layer + (self.n - but))


ACT_STEPS, DVE_STEPS = 51, 563


def hybrid_step(nc, par_d, early_d, cst_d, x_d, wmod_d, wch_d, wtok_d, wgate_d, wbr_d, wout_d, we13_d, we2_d,
                y_d, ko_d, vo_d, co_d, mo_d, so_d):
    nc.disable_value_cache = True
    with ExitStack() as ctx:
        def sb(name, shape):
            return ctx.enter_context(nc.sbuf_tensor(name, shape, F32))

        def sig(name, per_layer, credit=0):
            return Signal(ctx.enter_context(nc.semaphore(name)), per_layer, credit)

        psum = [ctx.enter_context(nc.psum_tensor(f"psum{i}", [P, 1024], F32)) for i in range(4)]

        def bank(b):
            return psum[b // 2][:, (b % 2) * 512:(b % 2) * 512 + 512]

        xT = sb("xT", [P, KD, T])
        hT = sb("hT", [P, KD, T])
        ring = [sb(f"ring{i}", [P, 4096]) for i in range(RING)]
        pc_flat = sb("pc", [P, NCH * 4 * T])
        pc = pc_flat[:, :].rearrange("p (s c t) -> p s c t", s=NCH, c=4)
        ring = [r[:, :] for r in ring]
        ring += [pc_flat[:, i * 4096:(i + 1) * 4096] for i in range(3)]
        merged = pc_flat[:, MQ * 4 * T:(MQ + 2) * 4 * T].rearrange("p (k t) -> p k t", k=KD)
        mva = sb("mva", [P, NT, H, DV + 1])
        dv = sb("dv", [P, NT, W])
        gv = sb("gv", [P, NT, W])
        par = sb("par", [P, NPAR])
        cst = sb("cst", [P, NCST])
        scr = sb("scr", [P, 2 * 4 * T])
        scrA, scrB = scr[:, 0:4 * T], scr[:, 4 * T:8 * T]
        upad = scr[:, 0:4 * UPAD].rearrange("p (c t) -> p c t", c=4)
        ytok = sb("ytok", [P, NT, W])
        mod = sb("mod", [P, 6 * KD, 2])
        amp = sb("amp", [P, 2, KD, 2])
        rstd = sb("rstd", [P, T])
        gaT = sb("gaT", [P, T])
        cols = sb("cols", [P, 10, 36])
        small = sb("small", [P, 64])
        eps = sb("eps", [P, 1])
        rt = sb("rt", [P, 160])
        rw = sb("rw", [P, NT, NE])
        wT = ytok[0:NE, 1, 0:T]
        wm = ytok[0:NE, 2, 0:T]

        def pp(name, a=None, b=None):
            lo, hi = PAR[name]
            return par[:, lo + (a or 0):(lo + b if b is not None else hi)]

        def cc(name, a=None, b=None):
            lo, hi = CST[name]
            return cst[:, lo + (a or 0):(lo + b if b is not None else hi)]

        ident, ones = cc("ident"), cc("ones")
        early = ytok[:, :, :].rearrange("p t n -> p (t n)")[:, 0:NEARLY]
        w_rows = early[:, 0:KD * P].rearrange("p (k n) -> p k n", k=KD)
        w_ga = early[:, KD * P:NEARLY].rearrange("p (k n) -> p k n", k=KD)
        w_router = pp("router").rearrange("p (k n) -> p k n", k=KD)
        w_up = pp("w_up")[0:33]
        S0 = pp("S0").rearrange("p (d a n) -> p d a n", d=2, a=2)
        C0 = pp("C0").rearrange("p (d h n) -> p d h n", d=2, h=H)
        k_cache = pp("k_cache").rearrange("p (h n) -> p h n", h=H)
        v_cache = pp("v_cache").rearrange("p (h n) -> p h n", h=H)
        taps = pp("taps").rearrange("p (c j) -> p c j", c=4)
        bmod = pp("bmod")
        cond = cc("cond").rearrange("p (k c) -> p k c", k=KD)
        lev = [cc("lev_f"), cc("lev_b")]
        tri = [cc("tri_f"), cc("tri_b")]
        neg = [cc("neg_f"), cc("neg_b")]

        rows = sb("rows", [64, 5, T])
        R_I, R_F, R_T, R_B, R_NG = range(5)
        R_U, R_EM, R_A = R_I, R_F, R_B

        m_exp = [scrA[:, i * 512:(i + 1) * 512] for i in range(2)]
        m_s = [scrB[:, i * 512:(i + 1) * 512] for i in range(2)]
        free = CB * 4 * T
        m_x = pc_flat[:, free:free + 4 * (DV + 1)].rearrange("p (a n) -> p a n", a=2)
        m_nd = pc_flat[:, free + 516:free + 516 + 3 * (DV + 1)].rearrange("p (a n) -> p a n", a=3)
        kstate = pc_flat[:, free + 904:free + 1032]
        st_out = pc_flat[:, free + 1032:free + 1032 + DV + 1]
        cmean = scrB[:, 0:T]
        mktok = scrB[:, 1024:1536].rearrange("p (h n) -> p h n", h=H)

        la = scrA.rearrange("p (t n) -> p t n", t=NT)
        gT = scrB.rearrange("p (u t) -> p u t", u=4)
        g_x = pc_flat[:, MQ * 1536:MQ * 1536 + 896].rearrange("p (l t) -> p l t", l=LEVELS)
        g_q = pc_flat[:, MQ * 1536 + 1024:MQ * 1536 + 2048].rearrange("p (l t) -> p l t", l=8)
        g_k = pc_flat[:, MQ * 1536 + 2048:MQ * 1536 + 3072].rearrange("p (l t) -> p l t", l=8)
        g_m = pc_flat[:, DKK * 1536:DKK * 1536 + 1024]
        g_att = [pc_flat[:, DKK * 1536 + 1024 + i * 128:DKK * 1536 + 1152 + i * 128] for i in range(2)]
        g_kd = scrA[:, 0:128]
        g_kt = scrA[:, 128:256]
        g_xx = scrA[:, 256:512]
        g_qx = scrA[:, 512:640]
        g_kx = scrA[:, 640:768]
        g_qs = scrA[:, 768:1024]
        g_so = scrA[:, 1024:1152]

        d_p = [scr[:, i * 768:i * 768 + 768].rearrange("p (c t) -> p c t", c=2) for i in range(2)]
        d_w = scr[:, 1536:1920]
        d_wt = scr[:, 1920:2304]

        wb = ytok[:, 0, 0:T]
        e_t = scrA.rearrange("p (a t) -> p a t", a=4)
        gu = scrB.rearrange("p (a t) -> p a t", a=4)

        loaded = sig("constants_loaded", 0)
        setup_s = sig("setup_step", 0)
        params_in = sig("params_in", 32)
        params_free = sig("params_free", 1, 1)
        slot_in = [sig(f"slot{i}_in", n * 16) for i, n in enumerate((21, 21, 20, 8, 8, 8))]
        FILLS_MIX = (13, 13, 12, 0, 0, 0)
        mod_done = sig("mod_done", NMOD)
        mod_used = sig("mod_used", NMOD, RING)
        merge_x = sig("merge_steps", 32 * 3)
        x_ready = sig("x_ready", 2, 1)
        squares_ready = sig("squares_ready", 2)
        sumsq_done = sig("sumsq_done", 2)
        rstd_ready = sig("rstd_ready", 2)
        xn_ready = sig("xn_ready", 16)
        h_ready = sig("h_ready", 2)
        small_done = sig("small_done", 2)
        ch_done = sig("ch_done", 36)
        ch_copied = sig("ch_copied", 36, 2)
        tok_done = sig("tok_done", 9)
        tok_copied = sig("tok_copied", 9, 2)
        cb_exp = sig("cb_exp", 1)
        rows_ready = sig("rows_ready", 1)
        rows_exp = sig("rows_exp", 1)
        cols_done = sig("cols_done", 1)
        cols_ready = sig("cols_ready", 1)
        kt_done = sig("kt_done", 1)
        kt_ready = sig("kt_ready", 1)
        bc_done = sig("bc_done", 8)
        qk_done = sig("qk_done", 8)
        mexp_ready = sig("mexp_ready", 8)
        s_ready = sig("s_ready", 8)
        pv_done = sig("pv_done", 8)
        inter_ready = sig("inter_ready", 8)
        m_out = sig("m_out", 8)
        kw_ready = sig("kw_ready", 8)
        st_done = sig("st_done", 8)
        st_copied = sig("st_copied", 8)
        outs = sig("dram_written", (2 + 8 + 2 + 8) * 16)
        fin_sq = sig("fin_sq", 3)
        fin_rs = sig("fin_rs", 3)
        fin_n = sig("fin_n", 3)
        fin_t = sig("fin_t", 3)
        fin_sigm = sig("fin_sig", 2)
        fin_done = sig("fin_done", 3)
        rot_done = sig("rot_done", 8)
        rot_used = sig("rot_used", 8)
        sc_done = sig("sc_done", 24)
        negmax = sig("negmax", 24)
        p_ready = sig("p_ready", 24)
        dw_ready = sig("dw_ready", 12)
        dwt_done = sig("dwt_done", 12)
        dwt_ready = sig("dwt_ready", 12)
        dpv_done = sig("dpv_done", 12)
        dpv_copied = sig("dpv_copied", 12)
        lamp_ready = sig("lamp_ready", 1)
        lams_done = sig("lams_done", 1)
        lame_ready = sig("lame_ready", 1)
        ga_ready = sig("ga_ready", 1)
        la_done = sig("la_done", 1)
        la_exp = sig("la_exp", 1)
        la_ready = sig("la_ready", 1)
        g_done = sig("g_done", 4)
        g_ready = sig("g_ready", 4)
        gd_ready = sig("gd_ready", 12)
        gx_ready = sig("gx_ready", 12)
        gqk_ready = sig("gqk_ready", 12)
        ga_done = sig("gla_scores_done", 24)
        gatt_ready = sig("gatt_ready", 24)
        gcd_ready = sig("gcd_ready", 4)
        gcx_ready = sig("gcx_ready", 4)
        gcq_ready = sig("gcq_ready", 4)
        gc_done = sig("gla_cross_done", 8)
        gc_copied = sig("gc_copied", 8)
        go_done = sig("gla_o_done", 8)
        gs_t = sig("gla_state_t", 4)
        gs_tc = sig("gla_state_tc", 4)
        gs_done = sig("gla_state_done", 4)
        gs_copied = sig("gla_state_copied", 8)
        go_copied = sig("gla_o_copied", 4)
        conv_acc = sig("conv_acc", 1)
        conv_sum = sig("conv_sum", 2)
        conv_mean = sig("conv_mean", 1)
        conv_sq = sig("conv_sq", 1)
        conv_rs = sig("conv_rs", 1)
        conv_n = sig("conv_n", 1)
        conv_v = sig("conv_v", 1)
        conv_done = sig("conv_done", 1)
        gate_done = sig("gate_done", 32)
        br_done = sig("br_done", 32)
        gate_exp = sig("gate_exp", 32, 2)
        merged_s = sig("merged", 32, 2)
        out_done = sig("out_done", 8)
        out_used = sig("out_used", 8, 2)
        rt_done = sig("router_done", 1)
        rt_ready = sig("router_ready", 1)
        rt_exp = sig("router_exp", 6)
        rt_step = sig("router_dve", 6)
        rtt_done = sig("router_t", 1)
        wT_ready = sig("wT_ready", 1)
        wm_ready = sig("wm_ready", NE + 1)
        wb_done = sig("wb_done", 16)
        wb_ready = sig("wb_ready", 16)
        ab_done = sig("ab_done", 64)
        a_exp = sig("a_exp", 64, 2)
        gu_ready = sig("gu_ready", 64, 4)
        y_done = sig("y_done", 128)
        y_used = sig("y_used", 128, 2)
        e_x = sig("expert_steps", 16 * 4 * 5)
        act_chain = ctx.enter_context(nc.semaphore("act_step"))
        dve_chain = ctx.enter_context(nc.semaphore("dve_step"))
        final_s = sig("final", 0)

        block = ctx.enter_context(nc.Block())

        def bflip(d, t):
            return 32 * d + t

        @block.sync
        def _(sp):
            sp.dma_start(cst[:, :], cst_d).then_inc(loaded.sem, 16)
            sp.dma_start(xT[:, :, :], x_d).then_inc(loaded.sem, 16)

            def fill(slot, src, l, k):
                sp.dma_start(ring[slot], src).then_inc(slot_in[slot].sem, 16)

            def rearr(a):
                return a.rearrange("a p n -> (a p) n")

            with sp.Fori(0, DEPTH) as l:
                sp.wait_ge(params_free.sem, params_free.at(l, 0))
                sp.dma_start(par[:, :], rearr(par_d[bass.ds(l, 1)])).then_inc(params_in.sem, 16)
                sp.dma_start(early, rearr(early_d[bass.ds(l, 1)])).then_inc(params_in.sem, 16)
                for j in range(RING):
                    fill(j, rearr(wmod_d[bass.ds(l * NMOD + j, 1)]), l, 0)
                with sp.Fori(1, NMOD // RING) as i:
                    for j in range(RING):
                        sp.wait_ge(mod_done.sem, l * NMOD + i * RING + (j - RING + 1))
                        fill(j, rearr(wmod_d[bass.ds(l * NMOD + i * RING + j, 1)]), l, 0)
                for j in range(RING):
                    sp.wait_ge(mod_done.sem, mod_done.at(l, NMOD - RING + j + 1))
                    fill(j, rearr(wch_d[bass.ds(l * NCH + j, 1)]), l, 0)
                with sp.Fori(1, NCH // RING) as i:
                    for j in range(RING):
                        sp.wait_ge(ch_done.sem, l * 36 + i * 12 + (4 * (j + 1) - 12))
                        fill(j, rearr(wch_d[bass.ds(l * NCH + i * RING + j, 1)]), l, 0)
                for j in range(NTOK):
                    sp.wait_ge(ch_done.sem, ch_done.at(l, 24 + 4 * (j + 1)))
                    fill(j, rearr(wtok_d[bass.ds(l * NTOK + j, 1)]), l, 0)
                def merge_fill(i, j):
                    if j < 2:
                        fill(j, rearr(wgate_d[bass.ds(l * 8 + i * 2 + j, 1)]), l, 0)
                    else:
                        fill(j, rearr(wbr_d[bass.ds(l * 4 + i, 1)]), l, 0)
                for j in range(RING):
                    sp.wait_ge(tok_done.sem, tok_done.at(l, 3 * (j + 1)))
                    merge_fill(0, j)
                sp.wait_ge(ch_copied.sem, ch_copied.at(l, 36))
                sp.dma_start(ko_d[bass.ds(l, 1)].rearrange("a p h n -> (a p) h n"), pc[:, DKK, :, CTX]).then_inc(outs.sem, 16)
                sp.wait_ge(tok_copied.sem, tok_copied.at(l, 9))
                sp.dma_start(rearr(vo_d[bass.ds(l, 1)]), dv[:, 0, :]).then_inc(outs.sem, 16)
                sp.wait_ge(rows_ready.sem, rows_ready.at(l, 1))
                for d in range(2):
                    sp.dma_start(mo_d[bass.ds(l * 2 + d, 1)].rearrange("a h n -> (a h) n"),
                                 small[32 * d:32 * d + 4, 60:61]).then_inc(outs.sem, 16)
                for n in range(8):
                    sp.wait_ge(st_copied.sem, st_copied.at(l, n + 1))
                    sp.dma_start(rearr(co_d[bass.ds(l * 8 + n, 1)]), st_out).then_inc(outs.sem, 16)
                for n in range(8):
                    sp.wait_ge(gs_copied.sem, gs_copied.at(l, n + 1))
                    sp.dma_start(rearr(so_d[bass.ds(l * 8 + n, 1)]),
                                 g_so[(n % 2) * 64:(n % 2) * 64 + 64, :]).then_inc(outs.sem, 16)
                with sp.Fori(1, 4) as i:
                    for j in range(2):
                        sp.wait_ge(gate_done.sem, l * 32 + i * 8 + (4 * (j + 1) - 8))
                        merge_fill(i, j)
                    sp.wait_ge(br_done.sem, l * 32 + i * 8)
                    merge_fill(i, 2)
                for j in range(2):
                    sp.wait_ge(gate_done.sem, gate_done.at(l, 28 + 4 * j))
                    fill(j, rearr(wout_d[bass.ds(l * 2 + j, 1)]), l, 0)
                def expert_fill(e, par_, j):
                    src = we13_d[bass.ds(l * 32 + e * 2 + j, 1)] if j < 2 else we2_d[bass.ds(l * 16 + e, 1)]
                    fill(3 * par_ + j, rearr(src), l, 0)
                sp.wait_ge(out_done.sem, out_done.at(l, 8))
                for p in range(2):
                    for j in range(3):
                        expert_fill(p, p, j)
                with sp.Fori(1, NE // 2) as i:
                    for p in range(2):
                        sp.wait_ge(ab_done.sem, l * 64 + i * 8 + (4 * p + 4 - 8))
                        expert_fill(i * 2 + p, p, 0)
                        expert_fill(i * 2 + p, p, 1)
                        sp.wait_ge(y_done.sem, l * 128 + i * 16 + (8 * p + 8 - 16))
                        expert_fill(i * 2 + p, p, 2)
            sp.wait_ge(final_s.sem, 4)
            sp.dma_start(y_d, hT[:, :, :]).then_inc(outs.sem, 16)
            sp.wait_ge(outs.sem, DEPTH * outs.per_layer + 16)

        @block.tensor
        def _(pe):
            pe.wait_ge(loaded.sem, 32)

            def sum_squares():
                for k in range(KD):
                    mm = pe.matmul(bank(0)[:, 0:T], ones, hT[:, k, :], start=k == 0, stop=k == KD - 1)
                mm.then_inc(sumsq_done.sem, 1)

            def finish_transposes(l, b):
                pe.wait_ge(fin_n.sem, fin_n.at(l, b + 1))
                for h in range(H):
                    for t in range(NT):
                        mm = pe.transpose(bank(h)[:, tok(t)], ytok[:, t, h * P:(h + 1) * P], ident)
                mm.then_inc(fin_t.sem, 1)

            with pe.Fori(0, DEPTH) as l:
                pe.wait_ge(setup_s.sem, 7)
                def mod_block(i, j):
                    pe.wait_ge(mod_used.sem, l * NMOD + i * RING + (j + 1))
                    pe.wait_ge(slot_in[j].sem, (l * slot_in[j].per_layer + i * 16) + 16)
                    wv = ring[j].rearrange("p (k n) -> p k n", k=KD)
                    for n in range(4):
                        for k in range(KD):
                            mm = pe.matmul(bank(5 + j)[:, n * 2:n * 2 + 2], wv[:, k, n * P:(n + 1) * P], cond[:, k, :],
                                           start=k == 0, stop=k == KD - 1, skip_group_check=True)
                    mm.then_inc(mod_done.sem, 1)
                with pe.Fori(0, NMOD // RING) as i:
                    for j in range(RING):
                        mod_block(i, j)
                pe.wait_ge(squares_ready.sem, squares_ready.at(l, 1))
                sum_squares()

                pe.wait_ge(h_ready.sem, h_ready.at(l, 1))
                for k in range(KD):
                    mm = pe.matmul(bank(4)[:, 0:T], w_rows[:, k, :], hT[:, k, :], start=k == 0, stop=k == KD - 1)
                mm.then_inc(small_done.sem, 1)
                for k in range(KD):
                    mm = pe.matmul(bank(5)[0:32, 0:T], w_ga[:, k, :], hT[:, k, :], start=k == 0, stop=k == KD - 1)
                mm.then_inc(small_done.sem, 1)

                with pe.Fori(0, NCH // RING) as i:
                    for j in range(RING):
                        pe.wait_ge(slot_in[j].sem, l * slot_in[j].per_layer + i * 16 + (4 * 16 + 16))
                        wv = ring[j].rearrange("p (k n) -> p k n", k=KD)
                        for n in range(4):
                            g = j * 4 + n
                            pe.wait_ge(ch_copied.sem, l * 36 + i * 12 + (g + 1))
                            for k in range(KD):
                                mm = pe.matmul(bank(g % 2)[:, 0:T], wv[:, k, n * P:(n + 1) * P], hT[:, k, :],
                                               start=k == 0, stop=k == KD - 1)
                            mm.then_inc(ch_done.sem, 1)
                for j in range(NTOK):
                    pe.wait_ge(slot_in[j].sem, slot_in[j].at(l, 7 * 16 + 16))
                    wv = ring[j].rearrange("p (k n) -> p k n", k=KD)
                    for t in range(NT):
                        g = j * 3 + t
                        pe.wait_ge(tok_copied.sem, tok_copied.at(l, g - 1))
                        for k in range(KD):
                            mm = pe.matmul(bank(2 + g % 2), hT[:, k, tok(t)], wv[:, k, :],
                                           start=k == 0, stop=k == KD - 1)
                        mm.then_inc(tok_done.sem, 1)

                pe.wait_ge(lamp_ready.sem, lamp_ready.at(l, 1))
                pe.matmul(bank(7)[:, 256:258], ones[0:64, :], small[0:64, 40:42], start=True, stop=True)\
                  .then_inc(lams_done.sem, 1)

                pe.wait_ge(rows_exp.sem, rows_exp.at(l, 1))
                pe.wait_ge(ch_copied.sem, ch_copied.at(l, 36))
                for h in range(H):
                    mm = pe.transpose(bank(5)[:, h * P:(h + 1) * P], pc[:, MK, h, CTX], ident)
                mm.then_inc(kt_done.sem, 1)
                for q, r in enumerate((R_U, R_A, R_EM)):
                    for t in range(NT):
                        pe.transpose(bank(4)[:, (q * 3 + t) * 36:(q * 3 + t) * 36 + 36],
                                     rows[0:36, r, tok(t)], ident[0:36, 0:36])
                pe.transpose(bank(4)[:, 324:360], rows[0:36, R_T, CTX], ident[0:36, 0:36])\
                  .then_inc(cols_done.sem, 1)
                pe.wait_ge(cols_ready.sem, cols_ready.at(l, 1))
                pe.wait_ge(kt_ready.sem, kt_ready.at(l, 1))
                pe.wait_ge(tok_copied.sem, tok_copied.at(l, 9))

                def m_front(i):
                    d, h = divmod(i, H)
                    E, Q = bank(i % 2), bank(2 + i % 2)
                    q, k = pc[:, MQ, h, :], pc[:, MK, h, :]
                    r = bflip(d, h)
                    sel = ident[0:36, r:r + 1].to_broadcast([36, P])
                    if i >= 2:
                        pe.wait_ge(s_ready.sem, s_ready.at(l, i - 1))
                    off_s, off_t = (1, 2) if d == 0 else (2, 1)
                    ng = rows[0:36, R_NG, :]
                    pe.matmul(E[:, 0:T], sel, ng, start=True, stop=False)
                    pe.matmul(E[:, 0:T], ident, neg[d].rearrange("p (a t) -> p a t", a=1).to_broadcast([P, NT, P]),
                              start=False, stop=True)
                    pe.matmul(E[:, T:512], sel, ng[:, tok(off_t)], start=True, stop=True, skip_group_check=True)\
                      .then_inc(bc_done.sem, 1)
                    for n, (s, t) in enumerate(((0, 0), (1, 1), (2, 2), (off_s, off_t))):
                        mm = pe.matmul(Q[:, n * P:(n + 1) * P], k[:, tok(s)], q[:, tok(t)], start=True, stop=True,
                                       skip_group_check=True)
                    mm.then_inc(qk_done.sem, 1)

                def m_back(i):
                    d, h = divmod(i, H)
                    V, I = bank(4 + i % 2), bank(6 + i % 2)
                    S = m_s[i % 2]
                    N = DV + 1
                    pe.wait_ge(s_ready.sem, s_ready.at(l, i + 1))
                    if i >= 2:
                        pe.wait_ge(m_out.sem, m_out.at(l, i - 1))
                    off_s, off_t = (1, 2) if d == 0 else (2, 1)
                    for t in range(NT):
                        two = t == off_t
                        pe.matmul(V[:, t * N:(t + 1) * N], S[:, tok(t)], mva[:, t, h, :], start=True, stop=not two,
                                  skip_group_check=True)
                        if two:
                            pe.matmul(V[:, t * N:(t + 1) * N], S[:, T:512], mva[:, off_s, h, :],
                                      start=False, stop=True, skip_group_check=True)
                    for t in (1, 2):
                        mm = pe.matmul(I[:, (t - 1) * N:t * N], pc[:, MQ, h, tok(t)], C0[:, d, h, :],
                                       start=True, stop=True, skip_group_check=True)
                    mm.then_inc(pv_done.sem, 1)

                for i in range(8):
                    m_front(i)
                    if i >= 1:
                        m_back(i - 1)
                m_back(7)
                for i in range(8):
                    d, h = divmod(i, H)
                    pe.wait_ge(kw_ready.sem, kw_ready.at(l, i + 1))
                    if i >= 1:
                        pe.wait_ge(st_copied.sem, st_copied.at(l, i))
                    pe.matmul(bank(0)[:, 0:DV + 1], kstate, mva[:, 0, h, :], start=True, stop=True)\
                      .then_inc(st_done.sem, 1)
                finish_transposes(l, 0)

                pe.wait_ge(fin_done.sem, fin_done.at(l, 1))
                for n in range(8):
                    slot, h = (DQ, DKK)[n // 4], n % 4
                    if n >= 2:
                        pe.wait_ge(rot_used.sem, rot_used.at(l, n - 1))
                    pe.matmul(bank(n % 2)[:, 0:DEC], cc("swap"), pc[:, slot, h, LAT], start=True, stop=True)\
                      .then_inc(rot_done.sem, 1)
                pe.wait_ge(rot_used.sem, rot_used.at(l, 8))

                def d_scores(u):
                    h, t, c = u // 6, (u // 2) % 3, u % 2
                    if u >= 2:
                        pe.wait_ge(p_ready.sem, p_ready.at(l, u - 1))
                    B = bank(u % 2)
                    half = slice(64 * c, 64 * c + 64)
                    q = pc[half, DQ, h, tok(t)]
                    if t == 0:
                        mm = pe.matmul(B[:, 0:P], q, pc[half, DKK, h, CTX], start=True, stop=True)
                    else:
                        pe.matmul(B[:, 0:DEC], q, pc[half, DKK, h, LAT], start=True, stop=True)
                        mm = pe.matmul(B[:, DEC:T], q, k_cache[half, h, :], start=True, stop=True,
                                       skip_group_check=True)
                    mm.then_inc(sc_done.sem, 1)

                def d_out(v):
                    h, t = divmod(v, 3)
                    nk = 1 if t == 0 else 3
                    pe.wait_ge(dw_ready.sem, dw_ready.at(l, v + 1))
                    for s in range(nk):
                        mm = pe.transpose(bank(2)[:, tok(s)], d_w[:, tok(s)], ident)
                    mm.then_inc(dwt_done.sem, 1)
                    pe.wait_ge(dwt_ready.sem, dwt_ready.at(l, v + 1))
                    if v >= 2:
                        pe.wait_ge(dpv_copied.sem, dpv_copied.at(l, v - 1))
                    for s in range(nk):
                        vals = dv[:, 0, h * P:(h + 1) * P] if t == 0 else (
                            dv[:, s + 1, h * P:(h + 1) * P] if s < 2 else v_cache[:, h, :])
                        mm = pe.matmul(bank(4 + v % 2)[:, 0:P], d_wt[:, tok(s)], vals, start=s == 0, stop=s == nk - 1)
                    mm.then_inc(dpv_done.sem, 1)

                for v in range(12):
                    d_scores(2 * v)
                    d_scores(2 * v + 1)
                    if v >= 1:
                        d_out(v - 1)
                d_out(11)
                finish_transposes(l, 1)

                pe.wait_ge(ga_ready.sem, ga_ready.at(l, 1))
                for t in range(NT):
                    mm = pe.matmul(bank(4 + t), gaT[0:33, tok(t)], w_up, start=True, stop=True)
                mm.then_inc(la_done.sem, 1)
                pe.wait_ge(la_ready.sem, la_ready.at(l, 1))
                pe.wait_ge(fin_done.sem, fin_done.at(l, 2))
                for u in range(4):
                    pair, d = divmod(u, 2)
                    if u >= 2:
                        pe.wait_ge(g_ready.sem, g_ready.at(l, u - 1))
                    B = bank(u % 2)
                    lc = slice(d * 256 + pair * P, d * 256 + pair * P + P)
                    near, far = (1, 2) if d == 0 else (2, 1)
                    pe.matmul(B[:, CTX], la[:, 0, lc], tri[d], start=True, stop=True)
                    pe.matmul(B[:, tok(near)], la[:, near, lc], tri[d], start=True, stop=True, skip_group_check=True)
                    pe.matmul(B[:, tok(far)], la[:, near, lc], cc("sixteenth"), start=True, stop=False, skip_group_check=True)
                    pe.matmul(B[:, tok(far)], la[:, far, lc], tri[d], start=False, stop=True, skip_group_check=True)\
                      .then_inc(g_done.sem, 1)

                for pair in range(2):
                    for d in range(2):
                        u = pair * 2 + d
                        for t in range(NT):
                            n = u * 3 + t
                            pe.wait_ge(gqk_ready.sem, gqk_ready.at(l, n + 1))
                            for hh in range(2):
                                A = psum[hh]
                                rows_ = slice(64 * hh, 64 * hh + 64)
                                for lv in range(8):
                                    mm = pe.matmul(A[:, lv * P:(lv + 1) * P], g_k[rows_, lv, :], g_q[rows_, lv, :],
                                                   start=True, stop=True, skip_group_check=True)
                                mm.then_inc(ga_done.sem, 1)
                            if pair == 1 and d == 0 and t == 0:
                                pe.wait_ge(go_copied.sem, go_copied.at(l, 2))
                            for hh in range(2):
                                head = pair * 2 + hh
                                pe.wait_ge(gatt_ready.sem, gatt_ready.at(l, 2 * n + hh + 1))
                                mm = pe.matmul(bank(4 + hh)[:, tok(t)], g_att[hh], gv[:, t, head * P:(head + 1) * P],
                                               start=(d == 0 and t == 0), stop=False, skip_group_check=True)
                        pe.wait_ge(gcq_ready.sem, gcq_ready.at(l, u + 1))
                        tq, tk = (2, 1) if d == 0 else (1, 2)
                        for hh in range(2):
                            head = pair * 2 + hh
                            rows_ = slice(64 * hh, 64 * hh + 64)
                            if u * 2 + hh >= 1:
                                pe.wait_ge(gc_copied.sem, gc_copied.at(l, u * 2 + hh))
                            pe.matmul(bank(6)[:, 0:P], g_kx[rows_, :], g_qx[rows_, :], start=True, stop=True)\
                              .then_inc(gc_done.sem, 1)
                            for t in (1, 2):
                                pe.matmul(bank(4 + hh)[:, tok(t)], g_qs[rows_, tok(t - 1)], S0[rows_, d, pair, :],
                                          start=False, stop=False, skip_group_check=True)
                            pe.wait_ge(gc_copied.sem, gc_copied.at(l, u * 2 + hh + 1))
                            pe.matmul(bank(4 + hh)[:, tok(tq)], g_att[hh], gv[:, tk, head * P:(head + 1) * P],
                                      start=False, stop=d == 1, skip_group_check=True).then_inc(go_done.sem, 1)
                        pe.transpose(bank(7)[:, 0:P], g_kd, ident).then_inc(gs_t.sem, 1)
                        pe.wait_ge(gs_tc.sem, gs_tc.at(l, u + 1))
                        pe.matmul(bank(7)[:, 0:256], g_kt, gv[:, 0, pair * 256:pair * 256 + 256],
                                  start=True, stop=True).then_inc(gs_done.sem, 1)
                finish_transposes(l, 2)

                pe.wait_ge(conv_acc.sem, conv_acc.at(l, 1))
                for c in range(4):
                    mm = pe.matmul(bank(6)[:, 0:T], ones, pc[:, CA, c, :], start=c == 0, stop=c == 3)
                mm.then_inc(conv_sum.sem, 1)
                pe.wait_ge(conv_sq.sem, conv_sq.at(l, 1))
                for c in range(4):
                    mm = pe.matmul(bank(7)[:, 0:T], ones, e_t[:, c, :], start=c == 0, stop=c == 3)
                mm.then_inc(conv_sum.sem, 1)

                with pe.Fori(0, 4) as i:
                    pe.wait_ge(fin_done.sem, fin_done.at(l, 3))
                    pe.wait_ge(conv_done.sem, conv_done.at(l, 1))
                    for n in range(8):
                        j = n // 4
                        if n % 4 == 0:
                            pe.wait_ge(slot_in[j].sem, l * slot_in[j].per_layer + i * 16 + (8 * 16 + 16))
                        wv = ring[j].rearrange("p (k n) -> p k n", k=KD)
                        pe.wait_ge(merged_s.sem, l * 32 + i * 8 + (n + 1))
                        for k in range(KD):
                            mm = pe.matmul(bank(n % 2)[:, 0:T], wv[:, k, (n % 4) * P:(n % 4 + 1) * P], hT[:, k, :],
                                           start=k == 0, stop=k == KD - 1)
                        mm.then_inc(gate_done.sem, 1)
                        if n == 0:
                            pe.wait_ge(slot_in[2].sem, l * slot_in[2].per_layer + i * 16 + (8 * 16 + 16))
                        wb_v = ring[2].rearrange("p (c n) -> p c n", c=4)
                        for c in range(4):
                            mm = pe.matmul(bank(2 + n % 2)[:, 0:T], wb_v[:, c, n * P:(n + 1) * P],
                                           pc_flat[:, bass.ds(i * (2 * 4 * T) + c * T, T)],
                                           start=c == 0, stop=c == 3)
                        mm.then_inc(br_done.sem, 1)
                pe.wait_ge(merged_s.sem, merged_s.at(l, 32))
                for n in range(8):
                    j = n // 4
                    if n % 4 == 0:
                        pe.wait_ge(slot_in[j].sem, slot_in[j].at(l, 12 * 16 + 16))
                    wv = ring[j].rearrange("p (k n) -> p k n", k=KD)
                    pe.wait_ge(out_used.sem, out_used.at(l, n - 1))
                    for k in range(KD):
                        mm = pe.matmul(bank(4 + n % 2)[:, 0:T], wv[:, k, (n % 4) * P:(n % 4 + 1) * P],
                                       merged[:, k, :], start=k == 0, stop=k == KD - 1)
                    mm.then_inc(out_done.sem, 1)

                pe.wait_ge(squares_ready.sem, squares_ready.at(l, 2))
                sum_squares()
                pe.wait_ge(h_ready.sem, h_ready.at(l, 2))
                for t in range(NT):
                    for k in range(KD):
                        mm = pe.matmul(bank(6)[:, t * 20:t * 20 + 20], hT[:, k, tok(t)], w_router[:, k, :],
                                       start=k == 0, stop=k == KD - 1, skip_group_check=True)
                mm.then_inc(rt_done.sem, 1)
                pe.wait_ge(rt_ready.sem, rt_ready.at(l, 1))
                for t in range(NT):
                    mm = pe.transpose(bank(7)[0:NE, tok(t)], rw[:, t, :], ident)
                mm.then_inc(rtt_done.sem, 1)

                with pe.Fori(0, NE // 2) as i:
                    for p in range(2):
                        w1 = ring[3 * p]
                        w3 = ring[3 * p + 1]
                        w2 = ring[3 * p + 2]
                        w1 = w1.rearrange("p (k n) -> p k n", k=KD)
                        w3 = w3.rearrange("p (k n) -> p k n", k=KD)
                        w2 = w2.rearrange("p (c n) -> p c n", c=4)
                        pe.wait_ge(wm_ready.sem, l * (NE + 1) + i * 2 + (p + 1))
                        pe.matmul(bank(6)[:, 0:T], ones[0:NE, :], wm, start=True, stop=True)\
                          .then_inc(wb_done.sem, 1)
                        for j in range(2):
                            s = slot_in[3 * p + j]
                            pe.wait_ge(s.sem, l * s.per_layer + i * 16 + (FILLS_MIX[3 * p + j] * 16 + 16))
                        for f in range(4):
                            pe.wait_ge(gu_ready.sem, l * 64 + i * 8 + (4 * p + f + 3))
                            for k in range(KD):
                                pe.matmul(bank(f % 2)[:, 0:T], w1[:, k, f * P:(f + 1) * P], hT[:, k, :],
                                          start=k == 0, stop=k == KD - 1)
                            for k in range(KD):
                                mm = pe.matmul(bank(2 + f % 2)[:, 0:T], w3[:, k, f * P:(f + 1) * P], hT[:, k, :],
                                               start=k == 0, stop=k == KD - 1)
                            mm.then_inc(ab_done.sem, 1)
                        s = slot_in[3 * p + 2]
                        pe.wait_ge(s.sem, l * s.per_layer + i * 16 + (FILLS_MIX[3 * p + 2] * 16 + 16))
                        pe.wait_ge(gu_ready.sem, l * 64 + i * 8 + (4 * p + 4 + 4))
                        for n in range(KD):
                            pe.wait_ge(y_used.sem, l * 128 + i * 16 + (8 * p + n + 1))
                            for f in range(4):
                                mm = pe.matmul(bank(4 + n % 2)[:, 0:T], w2[:, f, n * P:(n + 1) * P], gu[:, f, :],
                                               start=f == 0, stop=f == 3)
                            mm.then_inc(y_done.sem, 1)
            pe.wait_ge(squares_ready.sem, 2 * DEPTH + 1)
            sum_squares()

        @block.scalar
        def _(ac):
            def d_copy(v):
                h, t = divmod(v, 3)
                ac.wait_ge(dpv_done.sem, dpv_done.at(l, v + 1))
                ac.activation(ytok[:, t, h * P:(h + 1) * P], bank(4 + v % 2)[:, 0:P], ACT.Copy)\
                  .then_inc(dpv_copied.sem, 1)

            chain = Chain(ac, act_chain, ACT_STEPS)
            ac.sem_inc(ch_copied.sem, 2)
            ac.sem_inc(tok_copied.sem, 2)
            ac.sem_inc(gate_exp.sem, 2)
            ac.sem_inc(a_exp.sem, 2)
            ac.wait_ge(loaded.sem, 32)
            ac.activation(small[:, 0:16], cc("cond"), ACT.Exp, scale=-1.0).then_inc(setup_s.sem, 1)

            def squares():
                for k in range(KD):
                    o = ac.activation(hT[:, k, :], xT[:, k, :], ACT.Square)
                o.then_inc(squares_ready.sem, 1)

            def inverse_rms(l, n):
                ac.wait_ge(sumsq_done.sem, n)
                chain.step(ac.activation(rstd[:, :], bank(0)[:, 0:T], ACT.Ln, scale=1.0 / D, bias=eps[:, 0:1]))
                chain.settle()
                ac.activation(rstd[:, :], rstd[:, :], ACT.Exp, scale=-0.5).then_inc(rstd_ready.sem, 1)

            def norm(l, which):
                ac.wait_ge(x_ready.sem, l * 2 + (which + 1))
                squares()
                inverse_rms(l, l * 2 + (which + 1))
                for k in range(KD):
                    ac.wait_ge(xn_ready.sem, l * 16 + (8 * which + k + 1))
                    for c, cols_ in enumerate((CTX, LAT)):
                        o = ac.activation(hT[:, k, cols_], hT[:, k, cols_], ACT.Identity,
                                          scale=amp[:, which, k, c:c + 1],
                                          bias=mod[:, 24 * which + k, c:c + 1])
                o.then_inc(h_ready.sem, 1)

            def finish(l, b):
                ac.wait_ge(fin_sq.sem, fin_sq.at(l, b + 1))
                chain.step(ac.activation(small[:, 12:24], small[:, 0:12], ACT.Ln, scale=1.0 / DV, bias=eps[:, 0:1]))
                chain.settle()
                ac.activation(small[:, 12:24], small[:, 12:24], ACT.Exp, scale=-0.5).then_inc(fin_rs.sem, 1)

            def ch_copy(l, i):
                for g in range(12):
                    ac.wait_ge(ch_done.sem, l * 36 + i * 12 + (g + 1))
                    ac.activation(pc_flat[:, bass.ds(i * (12 * T) + g * T, T)], bank(g % 2)[:, 0:T], ACT.Copy)\
                      .then_inc(ch_copied.sem, 1)

            ac.wait_ge(setup_s.sem, 7)
            with ac.Fori(0, DEPTH) as l:
                chain.layer, chain.n = l, 0
                norm(l, 0)
                ac.wait_ge(small_done.sem, small_done.at(l, 2))
                chain.step(ac.activation(rows[:, R_I, :], bank(4)[0:64, 0:T], ACT.Identity, bias=pp("b_i")[0:64]))
                chain.step(ac.activation(rows[:, R_F, :], bank(4)[64:128, 0:T], ACT.Identity,
                                         bias=pp("b_f")[64:128]))
                chain.step(ac.activation(gaT[0:32, :], bank(5)[0:32, 0:T], ACT.Copy))
                chain.settle()
                chain.step(ac.activation(rows[:, R_T, :], rows[:, R_F, :], ACT.Abs))
                chain.settle()
                chain.step(ac.activation(rows[:, R_T, :], rows[:, R_T, :], ACT.Exp, scale=-1.0))
                chain.settle()
                ac.activation(rows[:, R_T, :], rows[:, R_T, :], ACT.Ln, bias=ones[0:64, 0:1]).then_inc(ga_ready.sem, 1)
                ch_copy(l, 0)
                ac.wait_ge(ch_copied.sem, ch_copied.at(l, 12))
                ac.activation(pc[:, CB, :, :], pc[:, CB, :, :], ACT.Exp, scale=-1.0).then_inc(cb_exp.sem, 1)
                with ac.Fori(1, NCH // RING) as i:
                    ch_copy(l, i)
                for j in range(NTOK):
                    for t in range(NT):
                        g = j * 3 + t
                        ac.wait_ge(tok_done.sem, tok_done.at(l, g + 1))
                        B = bank(2 + g % 2)
                        if j == 0:
                            o = ac.activation(mva[:, t, :, 0:DV], B.rearrange("p (h n) -> p h n", h=H), ACT.Copy)
                        else:
                            o = ac.activation((dv, gv)[j - 1][:, t, :], B, ACT.Copy)
                        o.then_inc(tok_copied.sem, 1)
                ac.wait_ge(lams_done.sem, lams_done.at(l, 1))
                ac.activation(small[:, 42:44], bank(7)[:, 256:258], ACT.Exp).then_inc(lame_ready.sem, 1)
                ac.wait_ge(ch_copied.sem, ch_copied.at(l, 36))
                chain.step(ac.activation(pc[:, MO, :, :], pc[:, MO, :, :], ACT.Exp, scale=-1.0))
                ac.wait_ge(rows_ready.sem, rows_ready.at(l, 1))
                chain.step(ac.activation(rows[0:36, R_A, :], rows[0:36, R_NG, :], ACT.Exp, bias=pp("m0")[0:36]))
                chain.step(ac.activation(rows[0:36, R_EM, :], rows[0:36, R_EM, :], ACT.Exp, scale=-1.0))
                ac.activation(rows[0:36, R_T, CTX], rows[0:36, R_U, CTX], ACT.Exp, bias=small[0:36, 61:62])\
                  .then_inc(rows_exp.sem, 1)
                ac.wait_ge(cols_ready.sem, cols_ready.at(l, 1))
                for i in range(9):
                    if i < 8:
                        d, h = divmod(i, H)
                        off_s = 1 if d == 0 else 2
                        ac.wait_ge(bc_done.sem, bc_done.at(l, i + 1))
                        if i >= 2:
                            ac.wait_ge(s_ready.sem, s_ready.at(l, i - 1))
                        for n, s in enumerate((0, 1, 2, off_s)):
                            r = bflip(d, h)
                            o = ac.activation(m_exp[i % 2][:, n * P:(n + 1) * P], bank(i % 2)[:, n * P:(n + 1) * P],
                                              ACT.Exp, bias=cols[:, s, r:r + 1])
                        o.then_inc(mexp_ready.sem, 1)
                    if i >= 1:
                        d, h = divmod(i - 1, H)
                        r, N = bflip(d, h), DV + 1
                        ac.wait_ge(pv_done.sem, pv_done.at(l, i))
                        if i >= 3:
                            ac.wait_ge(m_out.sem, m_out.at(l, i - 2))
                        for t in (1, 2):
                            o = ac.activation(m_x[:, (i - 1) % 2, (t - 1) * N:t * N],
                                              bank(6 + (i - 1) % 2)[:, (t - 1) * N:t * N],
                                              ACT.Copy, scale=cols[:, 3 + t, r:r + 1])
                        o.then_inc(inter_ready.sem, 1)
                for i in range(8):
                    ac.wait_ge(st_done.sem, st_done.at(l, i + 1))
                    ac.wait_ge(outs.sem, l * outs.per_layer + 16 * (4 + i))
                    ac.activation(st_out, bank(0)[:, 0:DV + 1], ACT.Copy).then_inc(st_copied.sem, 1)
                finish(l, 0)

                for u in range(24):
                    h, t, c = u // 6, (u // 2) % 3, u % 2
                    nk = P if t == 0 else T
                    ac.wait_ge(negmax.sem, negmax.at(l, u + 1))
                    if u >= 4:
                        ac.wait_ge(dw_ready.sem, dw_ready.at(l, u // 2 - 1))
                    ac.activation(d_p[(u // 2) % 2][:, c, 0:nk], bank(u % 2)[:, 0:nk], ACT.Exp, scale=D_SCALE,
                                  bias=small[:, 24 + u % 4:25 + u % 4],
                                  accum_out=small[:, 28 + u % 4:29 + u % 4]).then_inc(p_ready.sem, 1)
                    if u % 2 and u >= 3:
                        v = u // 2 - 1
                        d_copy(v)
                d_copy(11)
                finish(l, 1)

                ac.wait_ge(la_done.sem, la_done.at(l, 1))
                ac.wait_ge(fin_n.sem, fin_n.at(l, 2))
                for t in range(NT):
                    chain.step(ac.activation(scrB[:, t * 512:(t + 1) * 512], bank(4 + t), ACT.Abs))
                chain.settle()
                chain.step(ac.activation(scrB, scrB, ACT.Exp, scale=-1.0))
                chain.settle()
                ac.activation(scrB, scrB, ACT.Ln, bias=ones[:, 0:1]).then_inc(la_exp.sem, 1)
                for u in range(4):
                    ac.wait_ge(g_done.sem, g_done.at(l, u + 1))
                    if u == 0:
                        ac.wait_ge(la_ready.sem, la_ready.at(l, 1))
                    ac.activation(gT[:, u, :], bank(u % 2)[:, 0:T], ACT.Copy).then_inc(g_ready.sem, 1)
                for u in range(4):
                    for t in range(NT):
                        n = u * 3 + t
                        ac.wait_ge(gd_ready.sem, gd_ready.at(l, n + 1))
                        chain.step(ac.activation(g_x, g_x, ACT.Abs))
                        chain.settle()
                        ac.activation(g_x, g_x, ACT.Exp, scale=-1.0).then_inc(gx_ready.sem, 1)
                    ac.wait_ge(gcd_ready.sem, gcd_ready.at(l, u + 1))
                    chain.step(ac.activation(g_xx, g_xx, ACT.Abs))
                    chain.step(ac.activation(g_kd, g_kd, ACT.Abs))
                    chain.settle()
                    chain.step(ac.activation(g_xx, g_xx, ACT.Exp, scale=-1.0))
                    chain.step(ac.activation(g_kd, g_kd, ACT.Exp, scale=-1.0))
                    ac.activation(g_qs, gT[:, u, LAT], ACT.Exp).then_inc(gcx_ready.sem, 1)
                    for hh in range(2):
                        ac.wait_ge(gc_done.sem, gc_done.at(l, u * 2 + hh + 1))
                        ac.activation(g_att[hh], bank(6)[:, 0:P], ACT.Copy).then_inc(gc_copied.sem, 1)
                    ac.wait_ge(gs_t.sem, gs_t.at(l, u + 1))
                    ac.activation(g_kt, bank(7)[:, 0:P], ACT.Copy).then_inc(gs_tc.sem, 1)
                    ac.wait_ge(gs_done.sem, gs_done.at(l, u + 1))
                    ac.wait_ge(outs.sem, l * outs.per_layer + 16 * (12 + 2 * u))
                    for hh in range(2):
                        ac.activation(g_so[64 * hh:64 * hh + 64, :], bank(7)[64 * hh:64 * hh + 64, hh * P:(hh + 1) * P],
                                      ACT.Copy).then_inc(gs_copied.sem, 1)
                    if u % 2:
                        for hh in range(2):
                            head = (u // 2) * 2 + hh
                            ac.wait_ge(go_done.sem, go_done.at(l, u * 2 + hh + 1))
                            ac.activation(ytok[:, :, head * P:(head + 1) * P],
                                          bank(4 + hh)[:, 0:T].rearrange("p (t n) -> p t n", t=NT), ACT.Copy)\
                              .then_inc(go_copied.sem, 1)
                chain.step(ac.activation(pc[:, GQK, :, :], pc[:, GR, :, :], ACT.Exp, scale=-1.0))
                finish(l, 2)

                ac.wait_ge(conv_mean.sem, conv_mean.at(l, 1))
                ac.wait_ge(outs.sem, l * outs.per_layer + outs.per_layer)
                ac.activation(e_t[:, :, :], pc[:, CA, :, :], ACT.Square).then_inc(conv_sq.sem, 1)
                ac.wait_ge(conv_sum.sem, conv_sum.at(l, 2))
                chain.step(ac.activation(rstd[:, :], bank(7)[:, 0:T], ACT.Ln, scale=1.0 / W, bias=eps[:, 0:1]))
                chain.settle()
                ac.activation(rstd[:, :], rstd[:, :], ACT.Exp, scale=-0.5).then_inc(conv_rs.sem, 1)
                ac.wait_ge(conv_n.sem, conv_n.at(l, 1))
                for c in range(4):
                    chain.step(ac.activation(pc[:, CB, c, :], pc[:, CB, c, :], ACT.Identity,
                                             scale=pp("ln_g")[:, c:c + 1], bias=pp("ln_b")[:, c:c + 1]))
                chain.settle()
                ac.activation(pc[:, CA, :, :], pc[:, CB, :, :], ACT.Exp, scale=-1.0).then_inc(conv_v.sem, 1)

                with ac.Fori(0, 4) as i:
                    for n in range(8):
                        ac.wait_ge(gate_done.sem, l * 32 + i * 8 + (n + 1))
                        ac.wait_ge(merged_s.sem, l * 32 + i * 8 + (n + 1))
                        ac.activation(e_t[:, n % 2, :], bank(n % 2)[:, 0:T], ACT.Exp, scale=-1.0)\
                          .then_inc(gate_exp.sem, 1)
                norm(l, 1)
                for t in range(NT):
                    ac.wait_ge(rt_step.sem, rt_step.at(l, 2 * t + 1))
                    ac.activation(rt[:, 100:104], rt[:, 100:104], ACT.Exp,
                                  accum_out=rt[:, 104:105]).then_inc(rt_exp.sem, 1)
                    ac.wait_ge(rt_step.sem, rt_step.at(l, 2 * t + 2))
                    ac.activation(rt[:, 105:106], rt[:, 105:106], ACT.Exp).then_inc(rt_exp.sem, 1)
                with ac.Fori(0, NE // 2) as i:
                    for p in range(2):
                        ac.wait_ge(wb_done.sem, l * 16 + i * 2 + (p + 1))
                        ac.wait_ge(gu_ready.sem, l * 64 + i * 8 + (4 * p + 4))
                        ac.activation(wb, bank(6)[:, 0:T], ACT.Copy).then_inc(wb_ready.sem, 1)
                        for f in range(4):
                            ac.wait_ge(ab_done.sem, l * 64 + i * 8 + (4 * p + f + 1))
                            ac.wait_ge(gu_ready.sem, l * 64 + i * 8 + (4 * p + f + 3))
                            ac.activation(e_t[:, f % 2, :], bank(f % 2)[:, 0:T], ACT.Exp, scale=-1.0)\
                              .then_inc(a_exp.sem, 1)
            assert chain.n == ACT_STEPS, chain.n
            ac.wait_ge(x_ready.sem, 2 * DEPTH + 1)
            squares()
            ac.wait_ge(sumsq_done.sem, 2 * DEPTH + 1)
            ac.activation(rstd[:, :], bank(0)[:, 0:T], ACT.Ln, scale=1.0 / D, bias=eps[:, 0:1]).then_inc(final_s.sem, 1)
            ac.wait_ge(final_s.sem, 1)
            ac.activation(rstd[:, :], rstd[:, :], ACT.Exp, scale=-0.5).then_inc(final_s.sem, 1)

        @block.vector
        def _(ve):
            chain = Chain(ve, dve_chain, DVE_STEPS)
            for s, n in ((params_free, 1), (mod_used, RING), (merged_s, 2), (out_used, 2), (gu_ready, 4), (y_used, 2)):
                ve.sem_inc(s.sem, n)
            ve.memset(mva[:, :, :, DV:DV + 1], 1.0)
            ve.memset(gaT[32:33, :], 1.0)
            ve.memset(eps[:, :], EPS)
            ve.wait_ge(loaded.sem, 32)
            ve.sem_inc(x_ready.sem, 1)
            ve.wait_ge(setup_s.sem, 1)
            ve.tensor_scalar(small[:, 0:16], small[:, 0:16], 1.0, None, ALU.add).then_inc(setup_s.sem, 1)
            ve.wait_ge(setup_s.sem, 2)
            ve.reciprocal(small[:, 0:16], small[:, 0:16]).then_inc(setup_s.sem, 1)
            ve.wait_ge(setup_s.sem, 3)
            ve.tensor_tensor(cc("cond"), cc("cond"), small[:, 0:16], ALU.mult).then_inc(setup_s.sem, 1)
            ve.wait_ge(setup_s.sem, 4)
            ve.memset(rows[:, :, :], 0.0).then_inc(setup_s.sem, 1)
            ve.memset(merged[:, :, :], 0.0).then_inc(setup_s.sem, 1)
            ve.memset(small[:, 60:62], 0.0).then_inc(setup_s.sem, 1)
            ve.wait_ge(setup_s.sem, 7)

            def step(o):
                chain.step(o)

            def scaled(l, which):
                for k in range(KD):
                    if k == 0:
                        ve.wait_ge(rstd_ready.sem, l * 2 + (which + 1))
                    ve.tensor_tensor(hT[:, k, :], xT[:, k, :], rstd[:, :], ALU.mult).then_inc(xn_ready.sem, 1)

            def finish_sums(l, b):
                step(ve.tensor_tensor(scrB, ytok[:, :, :].rearrange("p t n -> p (t n)"),
                                      ytok[:, :, :].rearrange("p t n -> p (t n)"), ALU.mult))
                chain.settle()
                o = ve.tensor_reduce(small[:, 0:12], scrB.rearrange("p (a n) -> p a n", n=P), AX.X, ALU.add)
                o.then_inc(fin_sq.sem, 1)
                ve.wait_ge(fin_rs.sem, fin_rs.at(l, b + 1))
                yv = ytok[:, :, :].rearrange("p t (h n) -> p (t h) n", h=H)
                ve.tensor_tensor(yv, yv, small[:, 12:24].rearrange("p (a b) -> p a b", b=1)
                                 .to_broadcast([P, 12, P]), ALU.mult).then_inc(fin_n.sem, 1)

            with ve.Fori(0, DEPTH) as l:
                chain.layer, chain.n = l, 0
                with ve.Fori(0, NMOD // RING) as i:
                    ve.wait_ge(params_in.sem, params_in.at(l, 32))
                    for j in range(RING):
                        ve.wait_ge(mod_done.sem, l * NMOD + i * RING + (j + 1))
                        bias = par[:, bass.ds(i * 12 + (PAR["bmod"][0] + 4 * j), 4)]
                        ve.tensor_tensor(mod[:, bass.ds(i * 12 + 4 * j, 4), :],
                                         bank(5 + j)[:, 0:8].rearrange("p (a b) -> p a b", b=2),
                                         bias.rearrange("p (a b) -> p a b", b=1).to_broadcast([P, 4, 2]), ALU.add)\
                          .then_inc(mod_used.sem, 1)
                ve.wait_ge(mod_used.sem, mod_used.at(l, NMOD))
                for w, nm in enumerate(("norm1", "norm2")):
                    g = pp(nm).rearrange("p (a b) -> p a b", b=1).to_broadcast([P, KD, 2])
                    step(ve.scalar_tensor_tensor(amp[:, w, :, :], mod[:, 24 * w + 8:24 * w + 16, :], 1.0, g,
                                                 ALU.add, ALU.mult))
                ve.tensor_tensor(small[0:64, 40:42], pp("lam")[0:64, 0:4:2], pp("lam")[0:64, 1:4:2], ALU.mult)\
                  .then_inc(lamp_ready.sem, 1)
                scaled(l, 0)

                ve.wait_ge(ga_ready.sem, ga_ready.at(l, 1))
                step(ve.scalar_tensor_tensor(rows[:, R_F, :], rows[:, R_F, :], 0.0, rows[:, R_T, :],
                                             ALU.min, ALU.subtract))
                chain.settle()

                def scans(fn):
                    for d in range(2):
                        rs = slice(32 * d, 32 * d + 4)
                        for grp, (a, b) in enumerate(((0, SEQ), (SEQ, T))):
                            back = slice(b - 1, a - 1 if a else None, -1)
                            fn(rs, grp, slice(a, b) if d == 0 else back)
                scans(lambda rs, grp, s: step(ve.tensor_tensor_scan(
                    rows[rs, R_B, s], ones[rs, 0:1].to_broadcast([4, (P, DEC)[grp]]), rows[rs, R_F, s], 0.0, ALU.mult, ALU.add)))
                chain.settle()
                step(ve.tensor_tensor(rows[0:36, R_U, :], rows[0:36, R_I, :], rows[0:36, R_B, :], ALU.subtract))
                chain.settle()
                scans(lambda rs, grp, s: step(ve.tensor_tensor_scan(
                    rows[rs, R_T, s], cc("zero")[rs, 0:1].to_broadcast([4, (P, DEC)[grp]]), rows[rs, R_U, s],
                    0.0 if grp == 0 else pp("m0")[rs, :], ALU.add, ALU.max)))
                chain.settle()
                step(ve.tensor_scalar(rows[0:36, R_NG, :], rows[0:36, R_T, :], -1.0, None, ALU.mult))
                step(ve.tensor_tensor(rows[0:36, R_EM, :], rows[0:36, R_T, :], rows[0:36, R_B, :], ALU.add))
                chain.settle()
                for d in range(2):
                    rs, last = slice(32 * d, 32 * d + 4), SEQ - 1 if d == 0 else 0
                    step(ve.tensor_copy(small[rs, 60:61], rows[rs, R_EM, last:last + 1]))
                    o = ve.tensor_copy(small[rs, 61:62], rows[rs, R_NG, last:last + 1])
                    if d == 0:
                        step(o)
                o.then_inc(rows_ready.sem, 1)

                ve.wait_ge(cb_exp.sem, cb_exp.at(l, 1))
                step(ve.tensor_scalar(pc[:, CB, :, :], pc[:, CB, :, :], 1.0, None, ALU.add))
                chain.settle()
                step(ve.reciprocal(pc[:, CB, :, :], pc[:, CB, :, :]))
                chain.settle()
                step(ve.tensor_tensor(upad[:, :, PAD:PAD + SEQ], pc[:, CA, :, CTX], pc[:, CB, :, CTX], ALU.mult))
                step(ve.tensor_tensor(upad[:, :, 2 * PAD + SEQ:2 * PAD + T], pc[:, CA, :, LAT], pc[:, CB, :, LAT],
                                      ALU.mult))
                for z in (0, PAD + SEQ, 2 * PAD + T):
                    step(ve.memset(upad[:, :, z:z + PAD], 0.0))
                chain.settle()
                for j in range(CW):
                    for c in range(4):
                        for first, g in ((0, CTX), (PAD, LAT)):
                            src = upad[:, c, g.start + first + j:g.stop + first + j]
                            dst = pc[:, CA, c, g]
                            if j == 0:
                                step(ve.tensor_scalar(dst, src, taps[:, c, 0:1], None, ALU.mult))
                                continue
                            chain.settle(but=7)
                            o = ve.scalar_tensor_tensor(dst, src, taps[:, c, j:j + 1], dst, ALU.mult, ALU.add)
                            if j == CW - 1 and c == 3 and g is LAT:
                                o.then_inc(conv_acc.sem, 1)
                            else:
                                step(o)

                ve.wait_ge(lame_ready.sem, lame_ready.at(l, 1))
                chain.settle()
                step(ve.tensor_tensor(small[:, 44:45], small[:, 42:43], small[:, 43:44], ALU.subtract))
                chain.settle()
                step(ve.tensor_tensor(small[:, 44:45], small[:, 44:45],
                                      cst[:, bass.ds(l + CST["lam_init"][0], 1)], ALU.add))

                ve.wait_ge(cols_done.sem, cols_done.at(l, 1))
                ve.tensor_copy(cols[:, :, :], bank(4)[:, 0:360].rearrange("p (a b) -> p a b", a=10))\
                  .then_inc(cols_ready.sem, 1)
                ve.wait_ge(kt_done.sem, kt_done.at(l, 1))
                ve.tensor_copy(mktok, bank(5).rearrange("p (h n) -> p h n", h=H)).then_inc(kt_ready.sem, 1)
                for i in range(9):
                    if i < 8:
                        ve.wait_ge(mexp_ready.sem, mexp_ready.at(l, i + 1))
                        ve.wait_ge(qk_done.sem, qk_done.at(l, i + 1))
                        if i >= 2:
                            ve.wait_ge(pv_done.sem, pv_done.at(l, i - 1))
                        ve.scalar_tensor_tensor(m_s[i % 2], bank(2 + i % 2), M_SCALE, m_exp[i % 2],
                                                ALU.mult, ALU.mult).then_inc(s_ready.sem, 1)
                    if i >= 1:
                        n, N = i - 1, DV + 1
                        d, h = divmod(n, H)
                        r = bflip(d, h)
                        ve.wait_ge(inter_ready.sem, inter_ready.at(l, n + 1))
                        V = bank(4 + n % 2)
                        if n >= 1:
                            ve.wait_ge(m_out.sem, m_out.at(l, n))
                        step(ve.tensor_copy(m_nd[:, 0, :], V[:, 0:N]))
                        step(ve.tensor_tensor(m_nd[:, 1:3, :], V[:, N:3 * N].rearrange("p (t n) -> p t n", t=2),
                                              m_x[:, n % 2, :].rearrange("p (t n) -> p t n", t=2), ALU.add))
                        chain.settle()
                        den = m_nd[:, :, DV:N].rearrange("p t n -> p (t n)")
                        step(ve.scalar_tensor_tensor(small[:, 45:48], den, -1.0, den, ALU.mult, ALU.max))
                        chain.settle()
                        step(ve.tensor_tensor(small[:, 45:48], small[:, 45:48],
                                              cols[:, 6:9, r:r + 1].rearrange("p t n -> p (t n)"), ALU.max))
                        chain.settle()
                        step(ve.reciprocal(small[:, 45:48], small[:, 45:48]))
                        chain.settle()
                        for t in range(NT):
                            y = ytok[:, t, h * P:(h + 1) * P]
                            if d == 0:
                                o = ve.tensor_scalar(y, m_nd[:, t, 0:DV], small[:, 45 + t:46 + t], None, ALU.mult)
                            else:
                                o = ve.scalar_tensor_tensor(y, m_nd[:, t, 0:DV], small[:, 45 + t:46 + t], y,
                                                            ALU.mult, ALU.add)
                            if t < NT - 1:
                                step(o)
                        o.then_inc(m_out.sem, 1)
                        chain.settle()
                for i in range(8):
                    d, h = divmod(i, H)
                    r = bflip(d, h)
                    if i >= 1:
                        ve.wait_ge(st_done.sem, st_done.at(l, i))
                    ve.tensor_scalar(kstate, mktok[:, h, :], cols[:, 9, r:r + 1], M_SCALE,
                                     ALU.mult, ALU.mult).then_inc(kw_ready.sem, 1)
                step(ve.tensor_scalar(pc[:, MO, :, :], pc[:, MO, :, :], 1.0, None, ALU.add))
                chain.settle()
                step(ve.reciprocal(pc[:, MO, :, :], pc[:, MO, :, :]))
                ve.wait_ge(m_out.sem, m_out.at(l, 8))
                ve.wait_ge(kw_ready.sem, kw_ready.at(l, 8))
                finish_sums(l, 0)
                ve.wait_ge(fin_t.sem, fin_t.at(l, 1))
                chain.settle()
                for h in range(H):
                    o = ve.scalar_tensor_tensor(pc[:, MO, h, :], bank(h)[:, 0:T], pp("hn_m")[:, h:h + 1],
                                                pc[:, MO, h, :], ALU.mult, ALU.mult)
                o.then_inc(fin_done.sem, 1)

                for n in range(8):
                    slot, h = (DQ, DKK)[n // 4], n % 4
                    v = pc[:, slot, h, LAT]
                    ve.wait_ge(rot_done.sem, rot_done.at(l, n + 1))
                    step(ve.tensor_tensor(scr[:, 0:DEC], bank(n % 2)[:, 0:DEC], cc("sin"), ALU.mult))
                    step(ve.tensor_tensor(v, v, cc("cos"), ALU.mult))
                    chain.settle()
                    ve.tensor_tensor(v, v, scr[:, 0:DEC], ALU.add).then_inc(rot_used.sem, 1)
                    ve.wait_ge(rot_used.sem, rot_used.at(l, n + 1))

                def d_weights(v):
                    h, t = divmod(v, 3)
                    nk = P if t == 0 else T
                    q = (v % 2) * 2
                    dp = d_p[v % 2]
                    ve.wait_ge(p_ready.sem, p_ready.at(l, 2 * v + 2))
                    step(ve.reciprocal(small[:, 32:34], small[:, 28 + q:30 + q]))
                    chain.settle()
                    step(ve.tensor_tensor(small[:, 34:35], small[:, 33:34], small[:, 44:45], ALU.mult))
                    chain.settle()
                    step(ve.tensor_scalar(dp[:, 1, 0:nk], dp[:, 1, 0:nk], small[:, 34:35], None, ALU.mult))
                    if v >= 1:
                        ve.wait_ge(dwt_done.sem, dwt_done.at(l, v))
                    chain.settle()
                    ve.scalar_tensor_tensor(d_w[:, 0:nk], dp[:, 0, 0:nk], small[:, 32:33], dp[:, 1, 0:nk],
                                            ALU.mult, ALU.subtract).then_inc(dw_ready.sem, 1)
                    ve.wait_ge(dwt_done.sem, dwt_done.at(l, v + 1))
                    if v >= 1:
                        ve.wait_ge(dpv_done.sem, dpv_done.at(l, v))
                    ve.tensor_copy(d_wt[:, 0:nk], bank(2)[:, 0:nk]).then_inc(dwt_ready.sem, 1)

                for u in range(24):
                    h, t, c = u // 6, (u // 2) % 3, u % 2
                    nk = P if t == 0 else T
                    ve.wait_ge(sc_done.sem, sc_done.at(l, u + 1))
                    if u >= 4:
                        ve.wait_ge(p_ready.sem, p_ready.at(l, u - 3))
                    step(ve.tensor_reduce(small[:, 35:36], bank(u % 2)[:, 0:nk], AX.X, ALU.max))
                    chain.settle()
                    ve.tensor_scalar(small[:, 24 + u % 4:25 + u % 4], small[:, 35:36], -D_SCALE, None, ALU.mult)\
                      .then_inc(negmax.sem, 1)
                    ve.wait_ge(negmax.sem, negmax.at(l, u + 1))
                    if u % 2 and u >= 3:
                        d_weights(u // 2 - 1)
                d_weights(11)
                ve.wait_ge(dpv_copied.sem, dpv_copied.at(l, 12))
                finish_sums(l, 1)
                step(ve.tensor_scalar(small[:, 36:40], pp("hn_d"), cst[:, bass.ds(l + CST["one_less"][0], 1)], None,
                                      ALU.mult))
                ve.wait_ge(fin_t.sem, fin_t.at(l, 2))
                chain.settle()
                for h in range(H):
                    o = ve.tensor_scalar(pc[:, DQ, h, :], bank(h)[:, 0:T], small[:, 36 + h:37 + h], None, ALU.mult)
                o.then_inc(fin_done.sem, 1)

                ve.wait_ge(la_exp.sem, la_exp.at(l, 1))
                for t in range(NT):
                    o = ve.scalar_tensor_tensor(la[:, t, :], bank(4 + t), 0.0, scrB[:, t * 512:(t + 1) * 512],
                                                ALU.min, ALU.subtract)
                o.then_inc(la_ready.sem, 1)
                step(ve.tensor_scalar(pc[:, GQK, 0:2, :], pc[:, GQK, 0:2, :], G_SCALE, None, ALU.mult))
                ve.wait_ge(g_ready.sem, g_ready.at(l, 4))
                ve.wait_ge(outs.sem, l * outs.per_layer + 16 * 12)
                for u in range(4):
                    pair, d = divmod(u, 2)
                    q, k = pc[:, GQK, pair, :], pc[:, GQK, 2 + pair, :]
                    for t in range(NT):
                        n = u * 3 + t
                        for lv in range(LEVELS):
                            w = 1 << lv
                            gv_ = gT[:, u, tok(t)].rearrange("p (b w) -> p b w", w=2 * w)
                            mid = w - 1 if d == 0 else w
                            o = ve.tensor_tensor(g_x[:, lv, :].rearrange("p (b w) -> p b w", w=2 * w), gv_,
                                                 gv_[:, :, mid:mid + 1].to_broadcast([P, P // (2 * w), 2 * w]),
                                                 ALU.subtract)
                        o.then_inc(gd_ready.sem, 1)
                        ve.wait_ge(gx_ready.sem, gx_ready.at(l, n + 1))
                        if n >= 1:
                            ve.wait_ge(ga_done.sem, ga_done.at(l, 2 * n))
                        chain.settle()
                        for dst, src in ((g_q, q), (g_k, k)):
                            s3 = src[:, tok(t)].rearrange("p (a b) -> p a b", a=1).to_broadcast([P, LEVELS, P])
                            step(ve.tensor_tensor(dst[:, 0:LEVELS, :], s3, g_x, ALU.mult))
                            o = ve.tensor_copy(dst[:, LEVELS, :], src[:, tok(t)])
                            if dst is g_q:
                                step(o)
                        o.then_inc(gqk_ready.sem, 1)
                        for hh in range(2):
                            ve.wait_ge(ga_done.sem, ga_done.at(l, 2 * n + hh + 1))
                            chain.settle()
                            if n >= 1:
                                ve.wait_ge(gatt_ready.sem, gatt_ready.at(l, 2 * n + hh))
                            step(ve.tensor_tensor(g_m, psum[hh][:, :], lev[d], ALU.mult))
                            chain.settle()
                            ve.tensor_reduce(g_att[hh], g_m.rearrange("p (l t) -> p t l", l=8), AX.X, ALU.add)\
                              .then_inc(gatt_ready.sem, 1)
                            ve.wait_ge(gatt_ready.sem, gatt_ready.at(l, 2 * n + hh + 1))
                    ref = 2 * P - 1 if d == 0 else 2 * P
                    last = SEQ - 1 if d == 0 else 0
                    tq, tk = (2, 1) if d == 0 else (1, 2)
                    if u >= 1:
                        ve.wait_ge(go_done.sem, go_done.at(l, 2 * u))
                        ve.wait_ge(gs_copied.sem, gs_copied.at(l, 2 * u))
                    gr = gT[:, u, :]
                    step(ve.tensor_tensor(g_xx, gr[:, LAT], gr[:, ref:ref + 1].to_broadcast([P, DEC]), ALU.subtract))
                    ve.tensor_tensor(g_kd, gr[:, CTX], gr[:, last:last + 1].to_broadcast([P, P]), ALU.subtract)\
                      .then_inc(gcd_ready.sem, 1)
                    ve.wait_ge(gcx_ready.sem, gcx_ready.at(l, u + 1))
                    step(ve.tensor_tensor(g_qx, q[:, tok(tq)], g_xx[:, tok(tq - 1)], ALU.mult))
                    step(ve.tensor_tensor(g_kx, k[:, tok(tk)], g_xx[:, tok(tk - 1)], ALU.mult))
                    step(ve.tensor_tensor(g_kd, k[:, CTX], g_kd, ALU.mult))
                    ve.tensor_tensor(g_qs, q[:, LAT], g_qs, ALU.mult).then_inc(gcq_ready.sem, 1)
                    ve.wait_ge(go_done.sem, go_done.at(l, 2 * u + 2))
                ve.wait_ge(go_copied.sem, go_copied.at(l, 4))
                finish_sums(l, 2)
                step(ve.tensor_scalar(pc[:, GQK, :, :], pc[:, GQK, :, :], 1.0, None, ALU.add))
                chain.settle()
                step(ve.reciprocal(pc[:, GQK, :, :], pc[:, GQK, :, :]))
                chain.settle()
                step(ve.tensor_tensor(pc[:, GR, :, :], pc[:, GR, :, :], pc[:, GQK, :, :], ALU.mult))
                ve.wait_ge(fin_t.sem, fin_t.at(l, 3))
                chain.settle()
                for h in range(H):
                    o = ve.scalar_tensor_tensor(pc[:, GR, h, :], bank(h)[:, 0:T], pp("hn_g")[:, h:h + 1],
                                                pc[:, GR, h, :], ALU.mult, ALU.mult)
                o.then_inc(fin_done.sem, 1)

                ve.wait_ge(conv_sum.sem, conv_sum.at(l, 1))
                step(ve.tensor_scalar(cmean, bank(6)[:, 0:T], 1.0 / W, None, ALU.mult))
                chain.settle()
                ve.tensor_tensor(pc[:, CA, :, :], pc[:, CA, :, :],
                                 cmean.rearrange("p (a b) -> p a b", a=1).to_broadcast([P, 4, T]),
                                 ALU.subtract).then_inc(conv_mean.sem, 1)
                ve.wait_ge(conv_mean.sem, conv_mean.at(l, 1))
                ve.wait_ge(conv_rs.sem, conv_rs.at(l, 1))
                ve.tensor_tensor(pc[:, CB, :, :], pc[:, CA, :, :],
                                 rstd[:, :].rearrange("p (a b) -> p a b", a=1).to_broadcast([P, 4, T]),
                                 ALU.mult).then_inc(conv_n.sem, 1)
                ve.wait_ge(conv_v.sem, conv_v.at(l, 1))
                step(ve.tensor_scalar(pc[:, CA, :, :], pc[:, CA, :, :], 1.0, None, ALU.add))
                chain.settle()
                step(ve.reciprocal(pc[:, CA, :, :], pc[:, CA, :, :]))
                chain.settle()
                ve.tensor_tensor(pc[:, CB, :, :], pc[:, CB, :, :], pc[:, CA, :, :], ALU.mult).then_inc(conv_done.sem, 1)

                step(ve.memset(merged[:, :, :], 0.0))
                with ve.Fori(0, 4) as i:
                    for n in range(8):
                        e = e_t[:, n % 2, :]
                        gg = e_t[:, 2 + n % 2, :]
                        base = l * (32 * 3) + i * 24 + 3 * n
                        ve.wait_ge(gate_exp.sem, l * 32 + i * 8 + (n + 3))
                        ve.tensor_scalar(gg, e, 1.0, None, ALU.add).then_inc(merge_x.sem, 1)
                        ve.wait_ge(merge_x.sem, base + 1)
                        ve.reciprocal(gg, gg).then_inc(merge_x.sem, 1)
                        ve.wait_ge(merge_x.sem, base + 2)
                        ve.wait_ge(br_done.sem, l * 32 + i * 8 + (n + 1))
                        ve.tensor_tensor(gg, gg, bank(2 + n % 2)[:, 0:T], ALU.mult).then_inc(merge_x.sem, 1)
                        ve.wait_ge(merge_x.sem, base + 3)
                        ve.wait_ge(merged_s.sem, l * 32 + i * 8 + (n + 2))
                        ve.tensor_tensor(merged[:, n, :], merged[:, n, :], gg, ALU.add).then_inc(merged_s.sem, 1)
                for n in range(8):
                    ve.wait_ge(out_done.sem, out_done.at(l, n + 1))
                    for c, s in enumerate((CTX, LAT)):
                        o = ve.scalar_tensor_tensor(xT[:, n, s], bank(4 + n % 2)[:, s], mod[:, 16 + n, c:c + 1],
                                                    xT[:, n, s], ALU.mult, ALU.add)
                        if c == 0:
                            step(o)
                    o.then_inc(out_used.sem, 1)
                ve.wait_ge(out_used.sem, out_used.at(l, 8))
                ve.sem_inc(x_ready.sem, 1)
                scaled(l, 1)

                ve.wait_ge(rt_done.sem, rt_done.at(l, 1))
                step(ve.tensor_copy(rt[:, 0:60], bank(6)[:, 0:60]))
                chain.settle()

                def first_best(score, best, sel, tmp):
                    step(ve.tensor_reduce(best, score, AX.X, ALU.max))
                    chain.settle()
                    step(ve.scalar_tensor_tensor(sel, score, best, cc("order"), ALU.is_equal, ALU.mult))
                    chain.settle()
                    step(ve.tensor_reduce(tmp, sel, AX.X, ALU.max))
                    chain.settle()
                    step(ve.tensor_scalar(sel, sel, tmp, None, ALU.is_equal))
                    chain.settle()

                for t in range(NT):
                    gl, el = rt[:, t * 20:t * 20 + 4], rt[:, t * 20 + 4:t * 20 + 20]
                    best, gsel, tmp = rt[:, 60:61], rt[:, 61:65], rt[:, 65:66]
                    first_best(gl, best, gsel, tmp)
                    ve.tensor_scalar(rt[:, 100:104], gl, best, None, ALU.subtract).then_inc(rt_step.sem, 1)
                    g3 = gsel.rearrange("p (a b) -> p a b", b=1).to_broadcast([P, NG, EPG])
                    step(ve.tensor_tensor(rt[:, 70:86].rearrange("p (a b) -> p a b", a=NG),
                                          el.rearrange("p (a b) -> p a b", a=NG), g3, ALU.mult))
                    chain.settle()
                    es = rt[:, 86:90]
                    step(ve.tensor_reduce(es, rt[:, 70:86].rearrange("p (a b) -> p b a", a=NG), AX.X, ALU.add))
                    chain.settle()
                    v1, s1, v2, s2 = rt[:, 90:91], rt[:, 106:110], rt[:, 91:92], rt[:, 110:114]
                    first_best(es, v1, s1, tmp)
                    step(ve.scalar_tensor_tensor(es, s1, -3e38, es, ALU.mult, ALU.add))
                    chain.settle()
                    first_best(es, v2, s2, tmp)
                    ve.wait_ge(rt_exp.sem, rt_exp.at(l, 2 * t + 1))
                    ve.tensor_tensor(rt[:, 105:106], v2, v1, ALU.subtract).then_inc(rt_step.sem, 1)
                    ve.wait_ge(rt_exp.sem, rt_exp.at(l, 2 * t + 2))
                    step(ve.scalar_tensor_tensor(rt[:, 92:93], rt[:, 105:106], 1.0, rt[:, 104:105],
                                                 ALU.add, ALU.mult))
                    chain.settle()
                    step(ve.reciprocal(rt[:, 92:93], rt[:, 92:93]))
                    chain.settle()
                    step(ve.scalar_tensor_tensor(s1, s2, rt[:, 105:106], s1, ALU.mult, ALU.add))
                    chain.settle()
                    step(ve.tensor_scalar(s1, s1, rt[:, 92:93], None, ALU.mult))
                    chain.settle()
                    o = ve.tensor_tensor(rw[:, t, :].rearrange("p (a b) -> p a b", a=NG), g3,
                                         s1.rearrange("p (a b) -> p a b", a=1).to_broadcast([P, NG, EPG]), ALU.mult)
                    if t < NT - 1:
                        step(o)
                        chain.settle()
                o.then_inc(rt_ready.sem, 1)
                ve.wait_ge(rtt_done.sem, rtt_done.at(l, 1))
                ve.tensor_copy(wT, bank(7)[0:NE, 0:T]).then_inc(wT_ready.sem, 1)
                ve.wait_ge(wT_ready.sem, wT_ready.at(l, 1))

                ve.tensor_scalar(wm, wT, ident[0:NE, 0:1], None, ALU.mult).then_inc(wm_ready.sem, 1)
                with ve.Fori(0, NE // 2) as i:
                    for p in range(2):
                        for f in range(4):
                            e, s = e_t[:, f % 2, :], e_t[:, 2 + f % 2, :]
                            base = l * 256 + i * 32 + (16 * p + 4 * f)
                            ve.wait_ge(a_exp.sem, l * 64 + i * 8 + (4 * p + f + 3))
                            ve.tensor_scalar(s, e, 1.0, None, ALU.add).then_inc(e_x.sem, 1)
                            ve.wait_ge(e_x.sem, base + 1)
                            ve.reciprocal(s, s).then_inc(e_x.sem, 1)
                            ve.wait_ge(e_x.sem, base + 2)
                            ve.tensor_tensor(s, s, bank(f % 2)[:, 0:T], ALU.mult).then_inc(e_x.sem, 1)
                            ve.wait_ge(e_x.sem, base + 3)
                            ve.tensor_tensor(s, s, bank(2 + f % 2)[:, 0:T], ALU.mult).then_inc(e_x.sem, 1)
                            ve.wait_ge(e_x.sem, base + 4)
                            if f == 0:
                                ve.wait_ge(wb_ready.sem, l * 16 + i * 2 + (p + 1))
                                ve.wait_ge(y_used.sem, l * 128 + i * 16 + (8 * p + 2))
                            ve.tensor_tensor(gu[:, f, :], s, wb, ALU.mult).then_inc(gu_ready.sem, 1)
                        ve.tensor_scalar(wm, wT, cst[0:NE, bass.ds(i * 2 + (p + 1 + CST["ident"][0]), 1)], None,
                                         ALU.mult).then_inc(wm_ready.sem, 1)
                        for n in range(KD):
                            ve.wait_ge(y_done.sem, l * 128 + i * 16 + (8 * p + n + 1))
                            for c, s in enumerate((CTX, LAT)):
                                o = ve.scalar_tensor_tensor(xT[:, n, s], bank(4 + n % 2)[:, s],
                                                            mod[:, 40 + n, c:c + 1], xT[:, n, s], ALU.mult, ALU.add)
                            o.then_inc(y_used.sem, 1)
                ve.wait_ge(y_used.sem, l * 128 + (128 + 2))
                ve.sem_inc(x_ready.sem, 1)
                ve.sem_inc(params_free.sem, 1)
            assert chain.n == DVE_STEPS, chain.n
            ve.wait_ge(final_s.sem, 2)
            for k in range(KD):
                o = ve.tensor_tensor(hT[:, k, :], xT[:, k, :], rstd[:, :], ALU.mult)
            o.then_inc(final_s.sem, 1)
            ve.wait_ge(final_s.sem, 3)
            for k in range(KD):
                o = ve.tensor_scalar(hT[:, k, :], hT[:, k, :], cc("final")[:, k:k + 1], None, ALU.mult)
            o.then_inc(final_s.sem, 1)


_STARTS = {GR: 4656, CA: 5168, CB: 5680, GQK: 3600, DQ: 2064, DKK: 2576, MO: 1536, MQ: 0, MK: 512}
_TOKEN_STARTS = (1024, 3088, 4112)
_MERGE_ORDER = (2, 3, 1, 0)


def _by_partition(w, n):
    import numpy as np
    k, cols = w.shape
    return np.ascontiguousarray(w.reshape(k // P, P, cols // n, n).transpose(2, 1, 0, 3)).reshape(cols // n, P, -1)


def _constants(inputs):
    import numpy as np
    c = np.zeros((P, NCST), np.float32)

    def put(name, v):
        c[:, CST[name][0]:CST[name][1]] = np.asarray(v, np.float32).reshape(P, -1)

    s, t = np.arange(P)[:, None], np.arange(P)[None, :]
    put("ident", s == t)
    put("swap", (s // 64 == t // 64) & (s % 32 == t % 32) & (s != t))
    n_freq = DQK // 4
    inv = 10000.0 ** (-np.arange(n_freq, dtype=np.float32) / n_freq)
    r, col = np.divmod(np.arange(DEC), 64)
    ang = np.concatenate([r[:, None] * inv, col[:, None] * inv], axis=1).astype(np.float32)
    part = np.arange(P)
    put("cos", np.cos(ang).T[part % 32])
    put("sin", np.sin(ang).T[part % 32] * np.where(part % 64 < 32, -1.0, 1.0)[:, None])
    put("tri_f", (s <= t) / 16.0)
    put("tri_b", (s >= t) / 16.0)
    put("sixteenth", np.full((P, P), 1 / 16.0))
    put("ones", np.ones((P, P)))
    put("neg_f", np.where(s <= t, 0.0, MASKED))
    put("neg_b", np.where(s >= t, 0.0, MASKED))
    for name, a, b in (("lev_f", s, t), ("lev_b", t, s)):
        m = np.zeros((P, 8, P))
        for lv in range(LEVELS):
            w = 1 << lv
            m[:, lv] = (s // (2 * w) == t // (2 * w)) & (a % (2 * w) < w) & (b % (2 * w) >= w)
        m[:, LEVELS] = s == t
        put(name, m)
    put("order", np.tile(np.arange(NG, 0, -1), (P, 1)))
    lam = [0.8 - 0.6 * math.exp(-0.3 * l) for l in range(DEPTH)]
    put("lam_init", np.tile(lam, (P, 1)))
    put("one_less", np.tile([1.0 - v for v in lam], (P, 1)))
    put("final", inputs["final_norm"].reshape(KD, P).T)
    put("cond", np.stack([inputs["c_ctx"].reshape(KD, P).T, inputs["c"][0].reshape(KD, P).T], axis=2))
    return c


def _parameters(inputs, l):
    import numpy as np
    a = np.zeros((P, NPAR), np.float32)

    def view(name):
        return a[:, PAR[name][0]:PAR[name][1]]

    def chunks(v):
        return v.reshape(-1, P).T

    for name, key in (("norm1", "norm1"), ("norm2", "norm2"), ("bmod", "b_mod"), ("ln_g", "conv_ln_g"),
                      ("ln_b", "conv_ln_b"), ("hn_m", "hnorm_m"), ("hn_d", "hnorm_d"), ("hn_g", "hnorm_g")):
        view(name)[:] = chunks(inputs[key][l])
    view("taps")[:] = inputs["w_dw"][l].reshape(CW, 4, P).transpose(2, 1, 0).reshape(P, -1)
    for i, key in enumerate(("lam_q1", "lam_k1", "lam_q2", "lam_k2")):
        view("lam")[0:64, i] = inputs[key][l]
    w = inputs["w_in"][l]
    rows, bi, bf = np.zeros((D, P), np.float32), inputs["b_m_i"][l], inputs["b_m_f"][l]
    for d in range(2):
        rows[:, 32 * d:32 * d + 4] = w[:, 2048 + 4 * d:2052 + 4 * d]
        rows[:, 64 + 32 * d:68 + 32 * d] = w[:, 2056 + 4 * d:2060 + 4 * d]
        view("b_i")[32 * d:32 * d + 4, 0] = bi[4 * d:4 * d + 4]
        view("b_f")[64 + 32 * d:68 + 32 * d, 0] = bf[4 * d:4 * d + 4]
        view("m0")[32 * d:32 * d + 4, 0] = inputs["state_mlstm_m"][0, l, d]
    early = np.concatenate([_by_partition(rows, P)[0], _by_partition(w[:, 4624:4656], 32)[0]], axis=1)
    view("router")[:] = _by_partition(np.concatenate([inputs["w_group_router"][l], inputs["w_expert_router"][l]], 1), 20)[0]
    for d in range(2):
        view("w_up")[16 * d:16 * d + 16, 256 * d:256 * d + 256] = inputs["w_gla_up"][l, d]
        view("w_up")[32, 256 * d:256 * d + 256] = inputs["b_gla_gate"][l, d]
    view("S0")[:] = inputs["state_gla_S"][0, l].reshape(2, 2, 2, 64, P).transpose(2, 3, 0, 1, 4).reshape(P, -1)
    cn = np.concatenate([inputs["state_mlstm_C"][0, l], inputs["state_mlstm_n"][0, l][..., None]], axis=3)
    view("C0")[:] = cn.transpose(2, 0, 1, 3).reshape(P, -1)
    view("k_cache")[:] = inputs["cache_diff_k"][0, l].transpose(2, 1, 0).reshape(P, -1)
    view("v_cache")[:] = inputs["cache_diff_v"][0, l].reshape(P, -1)
    return a, early


def kernel(**inputs):
    import numpy as np
    import concourse.bacc as bacc
    from concourse.bass_utils import run_bass_kernel_spmd

    inputs = {k: np.asarray(v) for k, v in inputs.items()}
    L = range(DEPTH)
    w_in = inputs["w_in"]
    x = np.concatenate([inputs["x_prompt"][0], inputs["x_sample"][0]], axis=0)
    arrays = {
        "par": np.stack([_parameters(inputs, l)[0] for l in L]),
        "early": np.stack([_parameters(inputs, l)[1] for l in L]),
        "cst": _constants(inputs),
        "x": np.ascontiguousarray(x.T.reshape(KD, P, T).transpose(1, 0, 2)),
        "wmod": np.concatenate([_by_partition(inputs["w_mod"][l], W) for l in L]),
        "wch": np.concatenate([_by_partition(w_in[l][:, _STARTS[s]:_STARTS[s] + W], W) for l in L for s in range(NCH)]),
        "wtok": np.concatenate([_by_partition(w_in[l][:, s:s + W], W) for l in L for s in _TOKEN_STARTS]),
        "wgate": np.concatenate([_by_partition(w_in[l][:, 6192 + n * D:6192 + (n + 1) * D], W)
                                 for l in L for n in _MERGE_ORDER]),
        "wbr": np.concatenate([_by_partition(inputs["w_branch"][l, n], D) for l in L for n in _MERGE_ORDER]),
        "wout": np.concatenate([_by_partition(inputs["w_out"][l], W) for l in L]),
        "we13": np.concatenate([_by_partition(inputs[k][l, e // EPG, e % EPG], W)
                                for l in L for e in range(NE) for k in ("w_e1", "w_e3")]),
        "we2": np.concatenate([_by_partition(inputs["w_e2"][l, e // EPG, e % EPG], D) for l in L for e in range(NE)]),
    }
    outputs = {"y": (P, KD, T), "ko": (DEPTH, P, H, P), "vo": (DEPTH, P, W), "co": (DEPTH * 8, P, DV + 1),
               "mo": (DEPTH * 2, H, 1), "so": (DEPTH * 8, 64, P)}
    nc = bacc.Bacc("TRN2", target_bir_lowering=False, num_devices=1)
    args = [nc.dram_tensor(f"{n}_in", a.shape, F32, kind="ExternalInput").ap() for n, a in arrays.items()]
    args += [nc.dram_tensor(f"{n}_out", s, F32, kind="ExternalOutput").ap() for n, s in outputs.items()]
    hybrid_step(nc, *args)
    r = run_bass_kernel_spmd(nc, [{f"{n}_in": a for n, a in arrays.items()}], core_ids=[0]).results[0]
    y = r["y_out"].transpose(1, 0, 2).reshape(D, T).T
    ko = r["ko_out"].transpose(0, 3, 2, 1)
    vo = r["vo_out"].reshape(DEPTH, SEQ, H, DV)
    co = r["co_out"].reshape(DEPTH, 2, H, P, DV + 1)
    so = r["so_out"].reshape(DEPTH, 2, 2, 2, 64, P).transpose(0, 2, 1, 3, 4, 5).reshape(DEPTH, 2, H, 64, P)
    out = (y[:SEQ], y[SEQ:], ko, vo, co[..., :DV], co[..., DV], r["mo_out"].reshape(DEPTH, 2, H), so)
    return tuple(np.ascontiguousarray(v)[None] for v in out)
```

```python
import math
from contextlib import ExitStack

import concourse.bass as bass
from concourse import mybir

F32 = mybir.dt.float32
ACT = mybir.ActivationFunctionType
ALU = mybir.AluOpType
AX = mybir.AxisListType

P = 128
D = 1024
DEPTH = 2
SEQ = 128
DEC = 256
T = SEQ + DEC
NT = T // P
KD = D // P
W = 512
H = 4
DK_M, DQK, DK_G, DV = 128, 64, 64, 128
CW = 31
PAD = CW // 2
UPAD = PAD + SEQ + PAD + DEC + PAD
NG, EPG, DE = 4, 4, 512
NE = NG * EPG
EPS = 1e-6
LEVELS = 7
M_SCALE = DK_M ** -0.5
D_SCALE = DQK ** -0.5
G_SCALE = DK_G ** -0.5
MASKED = -1e30

GR, CA, CB, GQK, DQ, DKK, MO, MQ, MK = range(9)
NCH = 9
NTOK = 3
NMOD = 12
RING = 3

PAR = {}
_c = 0
for _n, _w in (("norm1", KD), ("norm2", KD), ("bmod", 6 * KD), ("taps", 4 * CW), ("ln_g", 4), ("ln_b", 4),
               ("hn_m", 4), ("hn_d", 4), ("hn_g", 4), ("lam", 4), ("b_i", 1), ("b_f", 1), ("m0", 1),
               ("router", KD * 20), ("w_up", 512),
               ("S0", 2 * 2 * P), ("C0", 2 * H * (DV + 1)), ("k_cache", H * P), ("v_cache", H * P)):
    PAR[_n] = (_c, _c + _w)
    _c += _w
NPAR = _c
NEARLY = KD * (P + 32)

CST = {}
_c = 0
for _n, _w in (("ident", P), ("swap", P), ("cos", DEC), ("sin", DEC), ("tri_f", P), ("tri_b", P), ("ones", P),
               ("neg_f", P), ("neg_b", P), ("lev_f", 8 * P), ("lev_b", 8 * P), ("sixteenth", P), ("slots", P), ("zero", 1), ("final", KD),
               ("lam_init", DEPTH), ("one_less", DEPTH), ("order", NG), ("cond", KD * 2)):
    CST[_n] = (_c, _c + _w)
    _c += _w
NCST = _c


def tok(t):
    return slice(t * P, (t + 1) * P)


CTX, LAT = slice(0, SEQ), slice(SEQ, T)


class Signal:

    def __init__(self, sem, per_layer, credit=0):
        self.sem, self.per_layer, self.credit = sem, per_layer, credit

    def at(self, layer, k):
        return layer * self.per_layer + (k + self.credit)


class Chain:

    def __init__(self, engine, sem, per_layer):
        self.engine, self.sem, self.per_layer, self.n = engine, sem, per_layer, 0
        self.layer = 0

    def step(self, instruction):
        instruction.then_inc(self.sem, 1)
        self.n += 1

    def settle(self, but=0):
        self.engine.wait_ge(self.sem, self.layer * self.per_layer + (self.n - but))


ACT_STEPS, DVE_STEPS = 51, 556


def hybrid_step(nc, par_d, early_d, cst_d, x_d, wmod_d, wch_d, wtok_d, wgate_d, wbr_d, wout_d, we13_d, we2_d,
                y_d, ko_d, vo_d, co_d, mo_d, so_d):
    nc.disable_value_cache = True
    with ExitStack() as ctx:
        def sb(name, shape):
            return ctx.enter_context(nc.sbuf_tensor(name, shape, F32))

        def sig(name, per_layer, credit=0):
            return Signal(ctx.enter_context(nc.semaphore(name)), per_layer, credit)

        psum = [ctx.enter_context(nc.psum_tensor(f"psum{i}", [P, 1024], F32)) for i in range(4)]

        def bank(b):
            return psum[b // 2][:, (b % 2) * 512:(b % 2) * 512 + 512]

        xT = sb("xT", [P, KD, T])
        hT = sb("hT", [P, KD, T])
        ring = [sb(f"ring{i}", [P, 4096]) for i in range(RING)]
        pc_flat = sb("pc", [P, NCH * 4 * T])
        pc = pc_flat[:, :].rearrange("p (s c t) -> p s c t", s=NCH, c=4)
        ring = [r[:, :] for r in ring]
        ring += [pc_flat[:, i * 4096:(i + 1) * 4096] for i in range(3)]
        merged = pc_flat[:, MQ * 4 * T:(MQ + 2) * 4 * T].rearrange("p (k t) -> p k t", k=KD)
        mva = sb("mva", [P, NT, H, DV + 1])
        dv = sb("dv", [P, NT, W])
        gv = sb("gv", [P, NT, W])
        par = sb("par", [P, NPAR])
        cst = sb("cst", [P, NCST])
        scr = sb("scr", [P, 2 * 4 * T])
        scrA, scrB = scr[:, 0:4 * T], scr[:, 4 * T:8 * T]
        mod_rows = scr[0:2, 0:RING * W]
        upad = scr[:, 0:4 * UPAD].rearrange("p (c t) -> p c t", c=4)
        ytok = sb("ytok", [P, NT, W])
        mod = sb("mod", [P, 6 * KD, 2])
        amp = sb("amp", [P, 2, KD, 2])
        rstd = sb("rstd", [P, T])
        gaT = sb("gaT", [P, T])
        cols = sb("cols", [P, 10, 36])
        small = sb("small", [P, 64])
        eps = sb("eps", [P, 1])
        rt = sb("rt", [P, 160])
        rw = sb("rw", [P, NT, NE + 1])
        rk = sb("rk", [P, NT, NE + 1])
        sel = sb("sel", [P, NT, NE])
        spill = ctx.enter_context(nc.sbuf_tensor("spill", [1, 1], mybir.dt.int32))
        wT = ytok[0:NE, 1, 0:T]
        wm = ytok[0:NE, 2, 0:T]

        def pp(name, a=None, b=None):
            lo, hi = PAR[name]
            return par[:, lo + (a or 0):(lo + b if b is not None else hi)]

        def cc(name, a=None, b=None):
            lo, hi = CST[name]
            return cst[:, lo + (a or 0):(lo + b if b is not None else hi)]

        ident, ones = cc("ident"), cc("ones")
        early = ytok[:, :, :].rearrange("p t n -> p (t n)")[:, 0:NEARLY]
        w_rows = early[:, 0:KD * P].rearrange("p (k n) -> p k n", k=KD)
        w_ga = early[:, KD * P:NEARLY].rearrange("p (k n) -> p k n", k=KD)
        w_router = pp("router").rearrange("p (k n) -> p k n", k=KD)
        w_up = pp("w_up")[0:33]
        S0 = pp("S0").rearrange("p (d a n) -> p d a n", d=2, a=2)
        C0 = pp("C0").rearrange("p (d h n) -> p d h n", d=2, h=H)
        k_cache = pp("k_cache").rearrange("p (h n) -> p h n", h=H)
        v_cache = pp("v_cache").rearrange("p (h n) -> p h n", h=H)
        taps = pp("taps").rearrange("p (c j) -> p c j", c=4)
        bmod = pp("bmod")
        cond = cc("cond").rearrange("p (k c) -> p k c", k=KD)
        lev = [cc("lev_f"), cc("lev_b")]
        tri = [cc("tri_f"), cc("tri_b")]
        neg = [cc("neg_f"), cc("neg_b")]

        rows = sb("rows", [64, 5, T])
        R_I, R_F, R_T, R_B, R_NG = range(5)
        R_U, R_EM, R_A = R_I, R_F, R_B

        m_exp = [scrA[:, i * 512:(i + 1) * 512] for i in range(2)]
        m_s = [scrB[:, i * 512:(i + 1) * 512] for i in range(2)]
        free = CB * 4 * T
        m_x = pc_flat[:, free:free + 4 * (DV + 1)].rearrange("p (a n) -> p a n", a=2)
        m_nd = pc_flat[:, free + 516:free + 516 + 3 * (DV + 1)].rearrange("p (a n) -> p a n", a=3)
        kstate = pc_flat[:, free + 904:free + 1032]
        st_out = pc_flat[:, free + 1032:free + 1032 + DV + 1]
        cmean = scrB[:, 0:T]
        mktok = scrB[:, 1024:1536].rearrange("p (h n) -> p h n", h=H)

        la = scrA.rearrange("p (t n) -> p t n", t=NT)
        gT = scrB.rearrange("p (u t) -> p u t", u=4)
        g_x = pc_flat[:, MQ * 1536:MQ * 1536 + 896].rearrange("p (l t) -> p l t", l=LEVELS)
        g_q = pc_flat[:, MQ * 1536 + 1024:MQ * 1536 + 2048].rearrange("p (l t) -> p l t", l=8)
        g_k = pc_flat[:, MQ * 1536 + 2048:MQ * 1536 + 3072].rearrange("p (l t) -> p l t", l=8)
        g_m = pc_flat[:, DKK * 1536:DKK * 1536 + 1024]
        g_att = [pc_flat[:, DKK * 1536 + 1024 + i * 128:DKK * 1536 + 1152 + i * 128] for i in range(2)]
        g_kd = scrA[:, 0:128]
        g_kt = scrA[:, 128:256]
        g_xx = scrA[:, 256:512]
        g_qx = scrA[:, 512:640]
        g_kx = scrA[:, 640:768]
        g_qs = scrA[:, 768:1024]
        g_so = scrA[:, 1024:1152]

        d_p = [scr[:, i * 768:i * 768 + 768].rearrange("p (c t) -> p c t", c=2) for i in range(2)]
        d_w = scr[:, 1536:1920]
        d_wt = scr[:, 1920:2304]

        x_h = scr[:, 0:1024].rearrange("p (k n) -> p k n", k=KD)
        x_y = scr[:, 1024:2048]
        x_s, x_g = scr[:, 2048:2560], scr[:, 2560:3072]
        yflat = ytok[:, :, :].rearrange("p t n -> p (t n)")
        x_gT = yflat[:, 0:512]
        x_p = yflat[:, 512:896].rearrange("p (t n) -> p t n", t=NT)
        x_pw = yflat[:, 896:1280].rearrange("p (t n) -> p t n", t=NT)
        x_pT = [pc_flat[:, 12288 + i * T:12288 + (i + 1) * T] for i in range(2)]
        htok = [dv, gv]
        wb = ytok[:, 0, 0:T]
        e_t = scrA.rearrange("p (a t) -> p a t", a=4)
        gu = scrB.rearrange("p (a t) -> p a t", a=4)

        loaded = sig("constants_loaded", 0)
        setup_s = sig("setup_step", 0)
        params_in = sig("params_in", 32)
        params_free = sig("params_free", 1, 1)
        slot_in = [sig(f"slot{i}_in", n * 16) for i, n in enumerate((21, 21, 20, 8, 8, 8))]
        FILLS_MIX = (13, 13, 12, 0, 0, 0)
        mod_done = sig("mod_done", NMOD)
        mod_row = sig("mod_row", NMOD)
        mod_turned = sig("mod_turned", NMOD // RING)
        mod_used = sig("mod_used", NMOD // RING, 1)
        merge_x = sig("merge_product", 32)
        x_ready = sig("x_ready", 2, 1)
        squares_ready = sig("squares_ready", 2)
        sumsq_done = sig("sumsq_done", 2)
        rstd_ready = sig("rstd_ready", 2)
        xn_ready = sig("xn_ready", 16)
        h_ready = sig("h_ready", 2)
        small_done = sig("small_done", 2)
        ch_done = sig("ch_done", 36)
        ch_copied = sig("ch_copied", 36, 2)
        tok_done = sig("tok_done", 9)
        tok_copied = sig("tok_copied", 9, 2)
        cb_sig = sig("cb_sig", 1)
        rows_ready = sig("rows_ready", 1)
        rows_exp = sig("rows_exp", 1)
        cols_done = sig("cols_done", 1)
        cols_ready = sig("cols_ready", 1)
        kt_done = sig("kt_done", 1)
        kt_ready = sig("kt_ready", 1)
        bc_done = sig("bc_done", 8)
        qk_done = sig("qk_done", 8)
        mexp_ready = sig("mexp_ready", 8)
        s_ready = sig("s_ready", 8)
        pv_done = sig("pv_done", 8)
        inter_ready = sig("inter_ready", 8)
        m_out = sig("m_out", 8)
        kw_ready = sig("kw_ready", 8)
        st_done = sig("st_done", 8)
        st_copied = sig("st_copied", 8)
        outs = sig("dram_written", (2 + 8 + 2 + 8) * 16)
        fin_sq = sig("fin_sq", 3)
        fin_rs = sig("fin_rs", 3)
        fin_n = sig("fin_n", 3)
        fin_t = sig("fin_t", 3)
        fin_sigm = sig("fin_sig", 2)
        fin_done = sig("fin_done", 3)
        rot_done = sig("rot_done", 8)
        rot_used = sig("rot_used", 8)
        sc_done = sig("sc_done", 24)
        negmax = sig("negmax", 24)
        p_ready = sig("p_ready", 24)
        dw_ready = sig("dw_ready", 12)
        dwt_done = sig("dwt_done", 12)
        dwt_ready = sig("dwt_ready", 12)
        dpv_done = sig("dpv_done", 12)
        dpv_copied = sig("dpv_copied", 12)
        lamp_ready = sig("lamp_ready", 1)
        lams_done = sig("lams_done", 1)
        lame_ready = sig("lame_ready", 1)
        ga_ready = sig("ga_ready", 1)
        la_done = sig("la_done", 1)
        la_exp = sig("la_exp", 1)
        la_ready = sig("la_ready", 1)
        g_done = sig("g_done", 4)
        g_ready = sig("g_ready", 4)
        gd_ready = sig("gd_ready", 12)
        gx_ready = sig("gx_ready", 12)
        gqk_ready = sig("gqk_ready", 12)
        ga_done = sig("gla_scores_done", 24)
        gatt_ready = sig("gatt_ready", 24)
        gcd_ready = sig("gcd_ready", 4)
        gcx_ready = sig("gcx_ready", 4)
        gcq_ready = sig("gcq_ready", 4)
        gc_done = sig("gla_cross_done", 8)
        gc_copied = sig("gc_copied", 8)
        go_done = sig("gla_o_done", 8)
        gs_t = sig("gla_state_t", 4)
        gs_tc = sig("gla_state_tc", 4)
        gs_done = sig("gla_state_done", 4)
        gs_copied = sig("gla_state_copied", 8)
        go_copied = sig("gla_o_copied", 4)
        conv_acc = sig("conv_acc", 1)
        conv_sum = sig("conv_sum", 2)
        conv_mean = sig("conv_mean", 1)
        conv_sq = sig("conv_sq", 1)
        conv_rs = sig("conv_rs", 1)
        conv_n = sig("conv_n", 1)
        conv_done = sig("conv_done", 1)
        gate_done = sig("gate_done", 32)
        br_done = sig("br_done", 32)
        gate_sig = sig("gate_sig", 32, 2)
        merged_s = sig("merged", 32, 2)
        out_done = sig("out_done", 8)
        out_used = sig("out_used", 8, 2)
        rt_done = sig("router_done", 1)
        rt_ready = sig("router_ready", 1)
        rt_exp = sig("router_exp", 6)
        rt_step = sig("router_dve", 6)
        sel_ready = sig("sel_ready", 1)
        rank_done = sig("rank_done", 1)
        rank_ready = sig("rank_ready", 1)
        ht_done = sig("ht_done", 6, 2)
        ht_copied = sig("ht_copied", 6, 2)
        p_built = sig("slots_built", NE + 1)
        xh_done = sig("gathered", NE + 1)
        xh_ready = sig("gathered_ready", NE + 1)
        pt_done = sig("slots_turned", NE + 1)
        pt_ready = sig("slots_turned_ready", NE + 1)
        xab_done = sig("hidden_done", NE)
        xs_ready = sig("silu_ready", NE)
        xg_ready = sig("hidden_ready", NE)
        xgt_done = sig("hidden_turned", NE)
        xgt_ready = sig("hidden_turned_ready", NE)
        xy_done = sig("expert_out_done", NE)
        xy_ready = sig("expert_out_ready", NE)
        back_done = sig("scattered", NE * KD)
        back_used = sig("scattered_used", NE * KD, 2)
        spill_known = sig("spill_known", 1)
        spill_asked = sig("spill_asked", 4)
        sp_slot = [sig(f"spill_slot{i}_in", 8 * 16) for i in range(6)]
        sp_free = sig("spill_weights_may_load", 1)
        sp_rw = sig("spill_weights", 1)
        rtt_done = sig("router_t", 1)
        wT_ready = sig("wT_ready", 1)
        wm_ready = sig("wm_ready", NE + 1)
        wb_done = sig("wb_done", 16)
        wb_ready = sig("wb_ready", 16)
        ab_done = sig("ab_done", 64)
        a_exp = sig("a_silu", 64)
        gu_ready = sig("gu_ready", 64, 4)
        y_done = sig("y_done", 128)
        y_used = sig("y_used", 128, 2)
        e_x = sig("spill_product", 64)
        act_chain = ctx.enter_context(nc.semaphore("act_step"))
        dve_chain = ctx.enter_context(nc.semaphore("dve_step"))
        final_s = sig("final", 0)

        block = ctx.enter_context(nc.Block())

        def bflip(d, t):
            return 32 * d + t

        @block.sync
        def _(sp):
            sp.dma_start(cst[:, :], cst_d).then_inc(loaded.sem, 16)
            sp.dma_start(xT[:, :, :], x_d).then_inc(loaded.sem, 16)

            def fill(slot, src, l, k):
                sp.dma_start(ring[slot], src).then_inc(slot_in[slot].sem, 16)

            def rearr(a):
                return a.rearrange("a p n -> (a p) n")

            with sp.Fori(0, DEPTH) as l:
                sp.wait_ge(params_free.sem, params_free.at(l, 0))
                sp.dma_start(par[:, :], rearr(par_d[bass.ds(l, 1)])).then_inc(params_in.sem, 16)
                sp.dma_start(early, rearr(early_d[bass.ds(l, 1)])).then_inc(params_in.sem, 16)
                for j in range(RING):
                    fill(j, rearr(wmod_d[bass.ds(l * NMOD + j, 1)]), l, 0)
                with sp.Fori(1, NMOD // RING) as i:
                    for j in range(RING):
                        sp.wait_ge(mod_done.sem, l * NMOD + i * RING + (j - RING + 1))
                        fill(j, rearr(wmod_d[bass.ds(l * NMOD + i * RING + j, 1)]), l, 0)
                for j in range(RING):
                    sp.wait_ge(mod_done.sem, mod_done.at(l, NMOD - RING + j + 1))
                    fill(j, rearr(wch_d[bass.ds(l * NCH + j, 1)]), l, 0)
                with sp.Fori(1, NCH // RING) as i:
                    for j in range(RING):
                        sp.wait_ge(ch_done.sem, l * 36 + i * 12 + (4 * (j + 1) - 12))
                        fill(j, rearr(wch_d[bass.ds(l * NCH + i * RING + j, 1)]), l, 0)
                for j in range(NTOK):
                    sp.wait_ge(ch_done.sem, ch_done.at(l, 24 + 4 * (j + 1)))
                    fill(j, rearr(wtok_d[bass.ds(l * NTOK + j, 1)]), l, 0)
                def merge_fill(i, j):
                    if j < 2:
                        fill(j, rearr(wgate_d[bass.ds(l * 8 + i * 2 + j, 1)]), l, 0)
                    else:
                        fill(j, rearr(wbr_d[bass.ds(l * 4 + i, 1)]), l, 0)
                for j in range(RING):
                    sp.wait_ge(tok_done.sem, tok_done.at(l, 3 * (j + 1)))
                    merge_fill(0, j)
                sp.wait_ge(ch_copied.sem, ch_copied.at(l, 36))
                sp.dma_start(ko_d[bass.ds(l, 1)].rearrange("a p h n -> (a p) h n"), pc[:, DKK, :, CTX]).then_inc(outs.sem, 16)
                sp.wait_ge(tok_copied.sem, tok_copied.at(l, 9))
                sp.dma_start(rearr(vo_d[bass.ds(l, 1)]), dv[:, 0, :]).then_inc(outs.sem, 16)
                sp.wait_ge(rows_ready.sem, rows_ready.at(l, 1))
                for d in range(2):
                    sp.dma_start(mo_d[bass.ds(l * 2 + d, 1)].rearrange("a h n -> (a h) n"),
                                 small[32 * d:32 * d + 4, 60:61]).then_inc(outs.sem, 16)
                for n in range(8):
                    sp.wait_ge(st_copied.sem, st_copied.at(l, n + 1))
                    sp.dma_start(rearr(co_d[bass.ds(l * 8 + n, 1)]), st_out).then_inc(outs.sem, 16)
                for n in range(8):
                    sp.wait_ge(gs_copied.sem, gs_copied.at(l, n + 1))
                    sp.dma_start(rearr(so_d[bass.ds(l * 8 + n, 1)]),
                                 g_so[(n % 2) * 64:(n % 2) * 64 + 64, :]).then_inc(outs.sem, 16)
                with sp.Fori(1, 4) as i:
                    for j in range(2):
                        sp.wait_ge(gate_done.sem, l * 32 + i * 8 + (4 * (j + 1) - 8))
                        merge_fill(i, j)
                    sp.wait_ge(br_done.sem, l * 32 + i * 8)
                    merge_fill(i, 2)
                for j in range(2):
                    sp.wait_ge(gate_done.sem, gate_done.at(l, 28 + 4 * j))
                    fill(j, rearr(wout_d[bass.ds(l * 2 + j, 1)]), l, 0)
                def expert_fill(e, par_, j):
                    src = we13_d[bass.ds(l * 32 + e * 2 + j, 1)] if j < 2 else we2_d[bass.ds(l * 16 + e, 1)]
                    fill(3 * par_ + j, rearr(src), l, 0)
                sp.wait_ge(out_done.sem, out_done.at(l, 8))
                for p in range(2):
                    for j in range(3):
                        expert_fill(p, p, j)
                with sp.Fori(1, NE // 2) as i:
                    for p in range(2):
                        sp.wait_ge(xab_done.sem, l * NE + i * 2 + (p - 1))
                        expert_fill(i * 2 + p, p, 0)
                        expert_fill(i * 2 + p, p, 1)
                        sp.wait_ge(xy_done.sem, l * NE + i * 2 + (p - 1))
                        expert_fill(i * 2 + p, p, 2)
                sp.wait_ge(spill_known.sem, spill_known.at(l, 1))
                sp.sem_inc(spill_asked.sem, 1)
                spilled = sp.value_load(spill[0:1, 0:1], min_val=0, max_val=1)
                with sp.If(spilled > 0):
                    def spill_fill(e, p, j):
                        src = we13_d[bass.ds(l * 32 + e * 2 + j, 1)] if j < 2 else we2_d[bass.ds(l * 16 + e, 1)]
                        sp.dma_start(ring[3 * p + j], rearr(src)).then_inc(sp_slot[3 * p + j].sem, 16)
                    sp.wait_ge(sp_free.sem, sp_free.at(l, 1))
                    for p in range(2):
                        for j in range(3):
                            spill_fill(p, p, j)
                    with sp.Fori(1, NE // 2) as i:
                        for p in range(2):
                            sp.wait_ge(ab_done.sem, l * 64 + i * 8 + (4 * p + 4 - 8))
                            spill_fill(i * 2 + p, p, 0)
                            spill_fill(i * 2 + p, p, 1)
                            sp.wait_ge(y_done.sem, l * 128 + i * 16 + (8 * p + 8 - 16))
                            spill_fill(i * 2 + p, p, 2)
                with sp.Else():
                    for s in sp_slot:
                        sp.sem_inc(s.sem, s.per_layer)
            sp.wait_ge(final_s.sem, 4)
            sp.dma_start(y_d, hT[:, :, :]).then_inc(outs.sem, 16)
            sp.wait_ge(outs.sem, DEPTH * outs.per_layer + 16)

        @block.tensor
        def _(pe):
            pe.wait_ge(loaded.sem, 32)

            def sum_squares():
                for k in range(KD):
                    mm = pe.matmul(bank(0)[:, 0:T], ones, hT[:, k, :], start=k == 0, stop=k == KD - 1)
                mm.then_inc(sumsq_done.sem, 1)

            def finish_transposes(l, b):
                pe.wait_ge(fin_n.sem, fin_n.at(l, b + 1))
                for h in range(H):
                    for t in range(NT):
                        mm = pe.transpose(bank(h)[:, tok(t)], ytok[:, t, h * P:(h + 1) * P], ident)
                mm.then_inc(fin_t.sem, 1)

            with pe.Fori(0, DEPTH) as l:
                pe.wait_ge(setup_s.sem, 7)
                with pe.Fori(0, NMOD // RING) as i:
                    for j in range(RING):
                        pe.wait_ge(slot_in[j].sem, (l * slot_in[j].per_layer + i * 16) + 16)
                        wv = ring[j].rearrange("p (k n) -> p k n", k=KD)
                        for k in range(KD):
                            mm = pe.matmul(bank(5 + j)[0:2, :], cond[:, k, :], wv[:, k, :],
                                           start=k == 0, stop=k == KD - 1)
                        mm.then_inc(mod_done.sem, 1)
                    pe.wait_ge(mod_row.sem, l * NMOD + i * RING + RING)
                    pe.wait_ge(mod_used.sem, l * (NMOD // RING) + i + 1)
                    for n in range(4 * RING):
                        mm = pe.matmul(bank(4)[:, 2 * n:2 * n + 2], mod_rows[:, n * P:(n + 1) * P], ident[0:2, 0:2],
                                       start=True, stop=True, skip_group_check=True)
                    mm.then_inc(mod_turned.sem, 1)
                pe.wait_ge(squares_ready.sem, squares_ready.at(l, 1))
                sum_squares()

                pe.wait_ge(h_ready.sem, h_ready.at(l, 1))
                for k in range(KD):
                    mm = pe.matmul(bank(4)[:, 0:T], w_rows[:, k, :], hT[:, k, :], start=k == 0, stop=k == KD - 1)
                mm.then_inc(small_done.sem, 1)
                for k in range(KD):
                    mm = pe.matmul(bank(5)[0:32, 0:T], w_ga[:, k, :], hT[:, k, :], start=k == 0, stop=k == KD - 1)
                mm.then_inc(small_done.sem, 1)

                with pe.Fori(0, NCH // RING) as i:
                    for j in range(RING):
                        pe.wait_ge(slot_in[j].sem, l * slot_in[j].per_layer + i * 16 + (4 * 16 + 16))
                        wv = ring[j].rearrange("p (k n) -> p k n", k=KD)
                        for n in range(4):
                            g = j * 4 + n
                            pe.wait_ge(ch_copied.sem, l * 36 + i * 12 + (g + 1))
                            for k in range(KD):
                                mm = pe.matmul(bank(g % 2)[:, 0:T], wv[:, k, n * P:(n + 1) * P], hT[:, k, :],
                                               start=k == 0, stop=k == KD - 1)
                            mm.then_inc(ch_done.sem, 1)
                for j in range(NTOK):
                    pe.wait_ge(slot_in[j].sem, slot_in[j].at(l, 7 * 16 + 16))
                    wv = ring[j].rearrange("p (k n) -> p k n", k=KD)
                    for t in range(NT):
                        g = j * 3 + t
                        pe.wait_ge(tok_copied.sem, tok_copied.at(l, g - 1))
                        for k in range(KD):
                            mm = pe.matmul(bank(2 + g % 2), hT[:, k, tok(t)], wv[:, k, :],
                                           start=k == 0, stop=k == KD - 1)
                        mm.then_inc(tok_done.sem, 1)

                pe.wait_ge(lamp_ready.sem, lamp_ready.at(l, 1))
                pe.matmul(bank(7)[:, 256:258], ones[0:64, :], small[0:64, 40:42], start=True, stop=True)\
                  .then_inc(lams_done.sem, 1)

                pe.wait_ge(rows_exp.sem, rows_exp.at(l, 1))
                pe.wait_ge(ch_copied.sem, ch_copied.at(l, 36))
                for h in range(H):
                    mm = pe.transpose(bank(5)[:, h * P:(h + 1) * P], pc[:, MK, h, CTX], ident)
                mm.then_inc(kt_done.sem, 1)
                for q, r in enumerate((R_U, R_A, R_EM)):
                    for t in range(NT):
                        pe.transpose(bank(4)[:, (q * 3 + t) * 36:(q * 3 + t) * 36 + 36],
                                     rows[0:36, r, tok(t)], ident[0:36, 0:36])
                pe.transpose(bank(4)[:, 324:360], rows[0:36, R_T, CTX], ident[0:36, 0:36])\
                  .then_inc(cols_done.sem, 1)
                pe.wait_ge(cols_ready.sem, cols_ready.at(l, 1))
                pe.wait_ge(kt_ready.sem, kt_ready.at(l, 1))
                pe.wait_ge(tok_copied.sem, tok_copied.at(l, 9))

                def m_front(i):
                    d, h = divmod(i, H)
                    E, Q = bank(i % 2), bank(2 + i % 2)
                    q, k = pc[:, MQ, h, :], pc[:, MK, h, :]
                    r = bflip(d, h)
                    sel = ident[0:36, r:r + 1].to_broadcast([36, P])
                    if i >= 2:
                        pe.wait_ge(s_ready.sem, s_ready.at(l, i - 1))
                    off_s, off_t = (1, 2) if d == 0 else (2, 1)
                    ng = rows[0:36, R_NG, :]
                    pe.matmul(E[:, 0:T], sel, ng, start=True, stop=False)
                    pe.matmul(E[:, 0:T], ident, neg[d].rearrange("p (a t) -> p a t", a=1).to_broadcast([P, NT, P]),
                              start=False, stop=True)
                    pe.matmul(E[:, T:512], sel, ng[:, tok(off_t)], start=True, stop=True, skip_group_check=True)\
                      .then_inc(bc_done.sem, 1)
                    for n, (s, t) in enumerate(((0, 0), (1, 1), (2, 2), (off_s, off_t))):
                        mm = pe.matmul(Q[:, n * P:(n + 1) * P], k[:, tok(s)], q[:, tok(t)], start=True, stop=True,
                                       skip_group_check=True)
                    mm.then_inc(qk_done.sem, 1)

                def m_back(i):
                    d, h = divmod(i, H)
                    V, I = bank(4 + i % 2), bank(6 + i % 2)
                    S = m_s[i % 2]
                    N = DV + 1
                    pe.wait_ge(s_ready.sem, s_ready.at(l, i + 1))
                    if i >= 2:
                        pe.wait_ge(m_out.sem, m_out.at(l, i - 1))
                    off_s, off_t = (1, 2) if d == 0 else (2, 1)
                    for t in range(NT):
                        two = t == off_t
                        pe.matmul(V[:, t * N:(t + 1) * N], S[:, tok(t)], mva[:, t, h, :], start=True, stop=not two,
                                  skip_group_check=True)
                        if two:
                            pe.matmul(V[:, t * N:(t + 1) * N], S[:, T:512], mva[:, off_s, h, :],
                                      start=False, stop=True, skip_group_check=True)
                    for t in (1, 2):
                        mm = pe.matmul(I[:, (t - 1) * N:t * N], pc[:, MQ, h, tok(t)], C0[:, d, h, :],
                                       start=True, stop=True, skip_group_check=True)
                    mm.then_inc(pv_done.sem, 1)

                for i in range(8):
                    m_front(i)
                    if i >= 1:
                        m_back(i - 1)
                m_back(7)
                for i in range(8):
                    d, h = divmod(i, H)
                    pe.wait_ge(kw_ready.sem, kw_ready.at(l, i + 1))
                    if i >= 1:
                        pe.wait_ge(st_copied.sem, st_copied.at(l, i))
                    pe.matmul(bank(0)[:, 0:DV + 1], kstate, mva[:, 0, h, :], start=True, stop=True)\
                      .then_inc(st_done.sem, 1)
                finish_transposes(l, 0)

                pe.wait_ge(fin_done.sem, fin_done.at(l, 1))
                for n in range(8):
                    slot, h = (DQ, DKK)[n // 4], n % 4
                    if n >= 2:
                        pe.wait_ge(rot_used.sem, rot_used.at(l, n - 1))
                    pe.matmul(bank(n % 2)[:, 0:DEC], cc("swap"), pc[:, slot, h, LAT], start=True, stop=True)\
                      .then_inc(rot_done.sem, 1)
                pe.wait_ge(rot_used.sem, rot_used.at(l, 8))

                def d_scores(u):
                    h, t, c = u // 6, (u // 2) % 3, u % 2
                    if u >= 2:
                        pe.wait_ge(p_ready.sem, p_ready.at(l, u - 1))
                    B = bank(u % 2)
                    half = slice(64 * c, 64 * c + 64)
                    q = pc[half, DQ, h, tok(t)]
                    if t == 0:
                        mm = pe.matmul(B[:, 0:P], q, pc[half, DKK, h, CTX], start=True, stop=True)
                    else:
                        pe.matmul(B[:, 0:DEC], q, pc[half, DKK, h, LAT], start=True, stop=True)
                        mm = pe.matmul(B[:, DEC:T], q, k_cache[half, h, :], start=True, stop=True,
                                       skip_group_check=True)
                    mm.then_inc(sc_done.sem, 1)

                def d_out(v):
                    h, t = divmod(v, 3)
                    nk = 1 if t == 0 else 3
                    pe.wait_ge(dw_ready.sem, dw_ready.at(l, v + 1))
                    for s in range(nk):
                        mm = pe.transpose(bank(2)[:, tok(s)], d_w[:, tok(s)], ident)
                    mm.then_inc(dwt_done.sem, 1)
                    pe.wait_ge(dwt_ready.sem, dwt_ready.at(l, v + 1))
                    if v >= 2:
                        pe.wait_ge(dpv_copied.sem, dpv_copied.at(l, v - 1))
                    for s in range(nk):
                        vals = dv[:, 0, h * P:(h + 1) * P] if t == 0 else (
                            dv[:, s + 1, h * P:(h + 1) * P] if s < 2 else v_cache[:, h, :])
                        mm = pe.matmul(bank(4 + v % 2)[:, 0:P], d_wt[:, tok(s)], vals, start=s == 0, stop=s == nk - 1)
                    mm.then_inc(dpv_done.sem, 1)

                for v in range(12):
                    d_scores(2 * v)
                    d_scores(2 * v + 1)
                    if v >= 1:
                        d_out(v - 1)
                d_out(11)
                finish_transposes(l, 1)

                pe.wait_ge(ga_ready.sem, ga_ready.at(l, 1))
                for t in range(NT):
                    mm = pe.matmul(bank(4 + t), gaT[0:33, tok(t)], w_up, start=True, stop=True)
                mm.then_inc(la_done.sem, 1)
                pe.wait_ge(la_ready.sem, la_ready.at(l, 1))
                pe.wait_ge(fin_done.sem, fin_done.at(l, 2))
                for u in range(4):
                    pair, d = divmod(u, 2)
                    if u >= 2:
                        pe.wait_ge(g_ready.sem, g_ready.at(l, u - 1))
                    B = bank(u % 2)
                    lc = slice(d * 256 + pair * P, d * 256 + pair * P + P)
                    near, far = (1, 2) if d == 0 else (2, 1)
                    pe.matmul(B[:, CTX], la[:, 0, lc], tri[d], start=True, stop=True)
                    pe.matmul(B[:, tok(near)], la[:, near, lc], tri[d], start=True, stop=True, skip_group_check=True)
                    pe.matmul(B[:, tok(far)], la[:, near, lc], cc("sixteenth"), start=True, stop=False, skip_group_check=True)
                    pe.matmul(B[:, tok(far)], la[:, far, lc], tri[d], start=False, stop=True, skip_group_check=True)\
                      .then_inc(g_done.sem, 1)

                for pair in range(2):
                    for d in range(2):
                        u = pair * 2 + d
                        for t in range(NT):
                            n = u * 3 + t
                            pe.wait_ge(gqk_ready.sem, gqk_ready.at(l, n + 1))
                            for hh in range(2):
                                A = psum[hh]
                                rows_ = slice(64 * hh, 64 * hh + 64)
                                for lv in range(8):
                                    mm = pe.matmul(A[:, lv * P:(lv + 1) * P], g_k[rows_, lv, :], g_q[rows_, lv, :],
                                                   start=True, stop=True, skip_group_check=True)
                                mm.then_inc(ga_done.sem, 1)
                            if pair == 1 and d == 0 and t == 0:
                                pe.wait_ge(go_copied.sem, go_copied.at(l, 2))
                            for hh in range(2):
                                head = pair * 2 + hh
                                pe.wait_ge(gatt_ready.sem, gatt_ready.at(l, 2 * n + hh + 1))
                                mm = pe.matmul(bank(4 + hh)[:, tok(t)], g_att[hh], gv[:, t, head * P:(head + 1) * P],
                                               start=(d == 0 and t == 0), stop=False, skip_group_check=True)
                        pe.wait_ge(gcq_ready.sem, gcq_ready.at(l, u + 1))
                        tq, tk = (2, 1) if d == 0 else (1, 2)
                        for hh in range(2):
                            head = pair * 2 + hh
                            rows_ = slice(64 * hh, 64 * hh + 64)
                            if u * 2 + hh >= 1:
                                pe.wait_ge(gc_copied.sem, gc_copied.at(l, u * 2 + hh))
                            pe.matmul(bank(6)[:, 0:P], g_kx[rows_, :], g_qx[rows_, :], start=True, stop=True)\
                              .then_inc(gc_done.sem, 1)
                            for t in (1, 2):
                                pe.matmul(bank(4 + hh)[:, tok(t)], g_qs[rows_, tok(t - 1)], S0[rows_, d, pair, :],
                                          start=False, stop=False, skip_group_check=True)
                            pe.wait_ge(gc_copied.sem, gc_copied.at(l, u * 2 + hh + 1))
                            pe.matmul(bank(4 + hh)[:, tok(tq)], g_att[hh], gv[:, tk, head * P:(head + 1) * P],
                                      start=False, stop=d == 1, skip_group_check=True).then_inc(go_done.sem, 1)
                        pe.transpose(bank(7)[:, 0:P], g_kd, ident).then_inc(gs_t.sem, 1)
                        pe.wait_ge(gs_tc.sem, gs_tc.at(l, u + 1))
                        pe.matmul(bank(7)[:, 0:256], g_kt, gv[:, 0, pair * 256:pair * 256 + 256],
                                  start=True, stop=True).then_inc(gs_done.sem, 1)
                finish_transposes(l, 2)

                pe.wait_ge(conv_acc.sem, conv_acc.at(l, 1))
                for c in range(4):
                    mm = pe.matmul(bank(6)[:, 0:T], ones, pc[:, CA, c, :], start=c == 0, stop=c == 3)
                mm.then_inc(conv_sum.sem, 1)
                pe.wait_ge(conv_sq.sem, conv_sq.at(l, 1))
                for c in range(4):
                    mm = pe.matmul(bank(7)[:, 0:T], ones, e_t[:, c, :], start=c == 0, stop=c == 3)
                mm.then_inc(conv_sum.sem, 1)

                with pe.Fori(0, 4) as i:
                    pe.wait_ge(fin_done.sem, fin_done.at(l, 3))
                    pe.wait_ge(conv_done.sem, conv_done.at(l, 1))
                    for n in range(8):
                        j = n // 4
                        if n % 4 == 0:
                            pe.wait_ge(slot_in[j].sem, l * slot_in[j].per_layer + i * 16 + (8 * 16 + 16))
                        wv = ring[j].rearrange("p (k n) -> p k n", k=KD)
                        pe.wait_ge(merged_s.sem, l * 32 + i * 8 + (n + 1))
                        for k in range(KD):
                            mm = pe.matmul(bank(n % 2)[:, 0:T], wv[:, k, (n % 4) * P:(n % 4 + 1) * P], hT[:, k, :],
                                           start=k == 0, stop=k == KD - 1)
                        mm.then_inc(gate_done.sem, 1)
                        if n == 0:
                            pe.wait_ge(slot_in[2].sem, l * slot_in[2].per_layer + i * 16 + (8 * 16 + 16))
                        wb_v = ring[2].rearrange("p (c n) -> p c n", c=4)
                        for c in range(4):
                            mm = pe.matmul(bank(2 + n % 2)[:, 0:T], wb_v[:, c, n * P:(n + 1) * P],
                                           pc_flat[:, bass.ds(i * (2 * 4 * T) + c * T, T)],
                                           start=c == 0, stop=c == 3)
                        mm.then_inc(br_done.sem, 1)
                pe.wait_ge(merged_s.sem, merged_s.at(l, 32))
                for n in range(8):
                    j = n // 4
                    if n % 4 == 0:
                        pe.wait_ge(slot_in[j].sem, slot_in[j].at(l, 12 * 16 + 16))
                    wv = ring[j].rearrange("p (k n) -> p k n", k=KD)
                    pe.wait_ge(out_used.sem, out_used.at(l, n - 1))
                    for k in range(KD):
                        mm = pe.matmul(bank(4 + n % 2)[:, 0:T], wv[:, k, (n % 4) * P:(n % 4 + 1) * P],
                                       merged[:, k, :], start=k == 0, stop=k == KD - 1)
                    mm.then_inc(out_done.sem, 1)

                pe.wait_ge(squares_ready.sem, squares_ready.at(l, 2))
                sum_squares()
                pe.wait_ge(h_ready.sem, h_ready.at(l, 2))
                for t in range(NT):
                    for k in range(KD):
                        mm = pe.matmul(bank(6)[:, t * 20:t * 20 + 20], hT[:, k, tok(t)], w_router[:, k, :],
                                       start=k == 0, stop=k == KD - 1, skip_group_check=True)
                mm.then_inc(rt_done.sem, 1)
                for n in range(6):
                    half, t = divmod(n, 3)
                    pe.wait_ge(ht_copied.sem, ht_copied.at(l, n - 1))
                    for k in range(4):
                        mm = pe.transpose(bank(2 + n % 2)[:, k * P:(k + 1) * P], hT[:, half * 4 + k, tok(t)], ident)
                    mm.then_inc(ht_done.sem, 1)
                pe.wait_ge(sel_ready.sem, sel_ready.at(l, 1))
                for t in range(NT):
                    for s in range(t + 1):
                        pe.matmul(bank(7)[:, t * NE:(t + 1) * NE], tri[0] if s == t else cc("sixteenth"), sel[:, s, :],
                                  start=s == 0, stop=s == t, skip_group_check=True)
                for s in range(NT):
                    mm = pe.matmul(bank(7)[:, NT * NE:(NT + 1) * NE], ones, sel[:, s, :], start=s == 0, stop=s == NT - 1,
                                   skip_group_check=True)
                mm.then_inc(rank_done.sem, 1)

                def gather(x):
                    pe.wait_ge(p_built.sem, l * (NE + 1) + x + 1)
                    for k in range(KD):
                        for t in range(NT):
                            mm = pe.matmul(psum[0][:, k * P:(k + 1) * P], htok[k // 4][:, t, (k % 4) * P:(k % 4 + 1) * P],
                                           x_p[:, t, :], start=t == 0, stop=t == NT - 1, skip_group_check=True)
                    mm.then_inc(xh_done.sem, 1)

                def turn_slots():
                    for t in range(NT):
                        mm = pe.transpose(bank(7)[:, tok(t)], x_pw[:, t, :], ident)
                    mm.then_inc(pt_done.sem, 1)

                pe.wait_ge(ht_copied.sem, ht_copied.at(l, 6))
                gather(0)
                turn_slots()
                with pe.Fori(0, NE // 2) as i:
                    for p in range(2):
                        w1, w3 = (ring[3 * p + j].rearrange("p (k n) -> p k n", k=KD) for j in range(2))
                        w2 = ring[3 * p + 2].rearrange("p (c n) -> p c n", c=4)
                        pe.wait_ge(xh_ready.sem, l * (NE + 1) + i * 2 + (p + 1))
                        for j, w in ((0, w1), (1, w3)):
                            s = slot_in[3 * p + j]
                            pe.wait_ge(s.sem, l * s.per_layer + i * 16 + (FILLS_MIX[3 * p + j] * 16 + 16))
                            for k in range(KD):
                                mm = pe.matmul(bank(2 + j), x_h[:, k, :], w[:, k, :], start=k == 0, stop=k == KD - 1)
                        mm.then_inc(xab_done.sem, 1)
                        pe.wait_ge(back_used.sem, l * 128 + i * 16 + (8 * p + 2))
                        gather(i * 2 + (p + 1))
                        pe.wait_ge(xg_ready.sem, l * NE + i * 2 + (p + 1))
                        for f in range(4):
                            mm = pe.transpose(bank(4)[:, f * P:(f + 1) * P], x_g[:, f * P:(f + 1) * P], ident)
                        mm.then_inc(xgt_done.sem, 1)
                        s = slot_in[3 * p + 2]
                        pe.wait_ge(s.sem, l * s.per_layer + i * 16 + (FILLS_MIX[3 * p + 2] * 16 + 16))
                        pe.wait_ge(xgt_ready.sem, l * NE + i * 2 + (p + 1))
                        for n in range(2):
                            for f in range(4):
                                mm = pe.matmul(bank(5 + n), x_gT[:, f * P:(f + 1) * P], w2[:, f, n * 512:(n + 1) * 512],
                                               start=f == 0, stop=f == 3)
                        mm.then_inc(xy_done.sem, 1)
                        pe.wait_ge(pt_ready.sem, l * (NE + 1) + i * 2 + (p + 1))
                        turn_slots()
                        pe.wait_ge(xy_ready.sem, l * NE + i * 2 + (p + 1))
                        pe.wait_ge(xh_ready.sem, l * (NE + 1) + i * 2 + (p + 2))
                        for n in range(KD):
                            pe.wait_ge(back_used.sem, l * 128 + i * 16 + (8 * p + n + 1))
                            pe.matmul(bank(n % 2)[:, 0:T], x_y[:, n * P:(n + 1) * P], x_pT[p], start=True, stop=True)\
                              .then_inc(back_done.sem, 1)

                pe.wait_ge(pt_ready.sem, pt_ready.at(l, NE + 1))
                pe.wait_ge(spill_known.sem, spill_known.at(l, 1))
                pe.sem_inc(spill_asked.sem, 1)
                spilled = pe.value_load(spill[0:1, 0:1], min_val=0, max_val=1)
                with pe.If(spilled > 0):
                    pe.wait_ge(sp_rw.sem, sp_rw.at(l, 1))
                    for t in range(NT):
                        mm = pe.transpose(bank(7)[0:NE, tok(t)], rw[:, t, 0:NE], ident)
                    mm.then_inc(rtt_done.sem, 1)

                    with pe.Fori(0, NE // 2) as i:
                        for p in range(2):
                            w1 = ring[3 * p]
                            w3 = ring[3 * p + 1]
                            w2 = ring[3 * p + 2]
                            w1 = w1.rearrange("p (k n) -> p k n", k=KD)
                            w3 = w3.rearrange("p (k n) -> p k n", k=KD)
                            w2 = w2.rearrange("p (c n) -> p c n", c=4)
                            pe.wait_ge(wm_ready.sem, l * (NE + 1) + i * 2 + (p + 1))
                            pe.matmul(bank(6)[:, 0:T], ones[0:NE, :], wm, start=True, stop=True)\
                              .then_inc(wb_done.sem, 1)
                            for j in range(2):
                                s = sp_slot[3 * p + j]
                                pe.wait_ge(s.sem, l * s.per_layer + i * 16 + 16)
                            for f in range(4):
                                pe.wait_ge(gu_ready.sem, l * 64 + i * 8 + (4 * p + f + 3))
                                for k in range(KD):
                                    pe.matmul(bank(f % 2)[:, 0:T], w1[:, k, f * P:(f + 1) * P], hT[:, k, :],
                                              start=k == 0, stop=k == KD - 1)
                                for k in range(KD):
                                    mm = pe.matmul(bank(2 + f % 2)[:, 0:T], w3[:, k, f * P:(f + 1) * P], hT[:, k, :],
                                                   start=k == 0, stop=k == KD - 1)
                                mm.then_inc(ab_done.sem, 1)
                            s = sp_slot[3 * p + 2]
                            pe.wait_ge(s.sem, l * s.per_layer + i * 16 + 16)
                            pe.wait_ge(gu_ready.sem, l * 64 + i * 8 + (4 * p + 4 + 4))
                            for n in range(KD):
                                pe.wait_ge(y_used.sem, l * 128 + i * 16 + (8 * p + n + 1))
                                for f in range(4):
                                    mm = pe.matmul(bank(4 + n % 2)[:, 0:T], w2[:, f, n * P:(n + 1) * P], gu[:, f, :],
                                                   start=f == 0, stop=f == 3)
                                mm.then_inc(y_done.sem, 1)
                with pe.Else():
                    for s in (rtt_done, wb_done, ab_done, y_done):
                        pe.sem_inc(s.sem, s.per_layer)
            pe.wait_ge(squares_ready.sem, 2 * DEPTH + 1)
            sum_squares()

        @block.scalar
        def _(ac):
            def d_copy(v):
                h, t = divmod(v, 3)
                ac.wait_ge(dpv_done.sem, dpv_done.at(l, v + 1))
                ac.activation(ytok[:, t, h * P:(h + 1) * P], bank(4 + v % 2)[:, 0:P], ACT.Copy)\
                  .then_inc(dpv_copied.sem, 1)

            chain = Chain(ac, act_chain, ACT_STEPS)
            ac.sem_inc(ch_copied.sem, 2)
            ac.sem_inc(tok_copied.sem, 2)
            ac.sem_inc(gate_sig.sem, 2)
            ac.wait_ge(loaded.sem, 32)
            ac.activation(small[:, 0:16], cc("cond"), ACT.Exp, scale=-1.0).then_inc(setup_s.sem, 1)

            def squares():
                for k in range(KD):
                    o = ac.activation(hT[:, k, :], xT[:, k, :], ACT.Square)
                o.then_inc(squares_ready.sem, 1)

            def inverse_rms(l, n):
                ac.wait_ge(sumsq_done.sem, n)
                chain.step(ac.activation(rstd[:, :], bank(0)[:, 0:T], ACT.Ln, scale=1.0 / D, bias=eps[:, 0:1]))
                chain.settle()
                ac.activation(rstd[:, :], rstd[:, :], ACT.Exp, scale=-0.5).then_inc(rstd_ready.sem, 1)

            def norm(l, which):
                ac.wait_ge(x_ready.sem, l * 2 + (which + 1))
                squares()
                inverse_rms(l, l * 2 + (which + 1))
                for k in range(KD):
                    ac.wait_ge(xn_ready.sem, l * 16 + (8 * which + k + 1))
                    for c, cols_ in enumerate((CTX, LAT)):
                        o = ac.activation(hT[:, k, cols_], hT[:, k, cols_], ACT.Identity,
                                          scale=amp[:, which, k, c:c + 1],
                                          bias=mod[:, 24 * which + k, c:c + 1])
                o.then_inc(h_ready.sem, 1)

            def finish(l, b):
                ac.wait_ge(fin_sq.sem, fin_sq.at(l, b + 1))
                chain.step(ac.activation(small[:, 12:24], small[:, 0:12], ACT.Ln, scale=1.0 / DV, bias=eps[:, 0:1]))
                chain.settle()
                ac.activation(small[:, 12:24], small[:, 12:24], ACT.Exp, scale=-0.5).then_inc(fin_rs.sem, 1)

            def ch_copy(l, i):
                for g in range(12):
                    ac.wait_ge(ch_done.sem, l * 36 + i * 12 + (g + 1))
                    ac.activation(pc_flat[:, bass.ds(i * (12 * T) + g * T, T)], bank(g % 2)[:, 0:T], ACT.Copy)\
                      .then_inc(ch_copied.sem, 1)

            ac.wait_ge(setup_s.sem, 7)
            with ac.Fori(0, DEPTH) as l:
                chain.layer, chain.n = l, 0
                norm(l, 0)
                ac.wait_ge(small_done.sem, small_done.at(l, 2))
                chain.step(ac.activation(rows[:, R_I, :], bank(4)[0:64, 0:T], ACT.Identity, bias=pp("b_i")[0:64]))
                chain.step(ac.activation(rows[:, R_F, :], bank(4)[64:128, 0:T], ACT.Identity,
                                         bias=pp("b_f")[64:128]))
                chain.step(ac.activation(gaT[0:32, :], bank(5)[0:32, 0:T], ACT.Copy))
                chain.settle()
                chain.step(ac.activation(rows[:, R_T, :], rows[:, R_F, :], ACT.Abs))
                chain.settle()
                chain.step(ac.activation(rows[:, R_T, :], rows[:, R_T, :], ACT.Exp, scale=-1.0))
                chain.settle()
                ac.activation(rows[:, R_T, :], rows[:, R_T, :], ACT.Ln, bias=ones[0:64, 0:1]).then_inc(ga_ready.sem, 1)
                ch_copy(l, 0)
                ac.wait_ge(ch_copied.sem, ch_copied.at(l, 12))
                ac.activation(pc[:, CB, :, :], pc[:, CB, :, :], ACT.Sigmoid).then_inc(cb_sig.sem, 1)
                with ac.Fori(1, NCH // RING) as i:
                    ch_copy(l, i)
                for j in range(NTOK):
                    for t in range(NT):
                        g = j * 3 + t
                        ac.wait_ge(tok_done.sem, tok_done.at(l, g + 1))
                        B = bank(2 + g % 2)
                        if j == 0:
                            o = ac.activation(mva[:, t, :, 0:DV], B.rearrange("p (h n) -> p h n", h=H), ACT.Copy)
                        else:
                            o = ac.activation((dv, gv)[j - 1][:, t, :], B, ACT.Copy)
                        o.then_inc(tok_copied.sem, 1)
                ac.wait_ge(lams_done.sem, lams_done.at(l, 1))
                ac.activation(small[:, 42:44], bank(7)[:, 256:258], ACT.Exp).then_inc(lame_ready.sem, 1)
                ac.wait_ge(ch_copied.sem, ch_copied.at(l, 36))
                chain.step(ac.activation(pc[:, MO, :, :], pc[:, MO, :, :], ACT.Sigmoid))
                chain.step(ac.activation(pc[:, GR, :, :], pc[:, GR, :, :], ACT.Silu))
                ac.wait_ge(rows_ready.sem, rows_ready.at(l, 1))
                chain.step(ac.activation(rows[0:36, R_A, :], rows[0:36, R_NG, :], ACT.Exp, bias=pp("m0")[0:36]))
                chain.step(ac.activation(rows[0:36, R_EM, :], rows[0:36, R_EM, :], ACT.Exp, scale=-1.0))
                ac.activation(rows[0:36, R_T, CTX], rows[0:36, R_U, CTX], ACT.Exp, bias=small[0:36, 61:62])\
                  .then_inc(rows_exp.sem, 1)
                ac.wait_ge(cols_ready.sem, cols_ready.at(l, 1))
                for i in range(9):
                    if i < 8:
                        d, h = divmod(i, H)
                        off_s = 1 if d == 0 else 2
                        ac.wait_ge(bc_done.sem, bc_done.at(l, i + 1))
                        if i >= 2:
                            ac.wait_ge(s_ready.sem, s_ready.at(l, i - 1))
                        for n, s in enumerate((0, 1, 2, off_s)):
                            r = bflip(d, h)
                            o = ac.activation(m_exp[i % 2][:, n * P:(n + 1) * P], bank(i % 2)[:, n * P:(n + 1) * P],
                                              ACT.Exp, bias=cols[:, s, r:r + 1])
                        o.then_inc(mexp_ready.sem, 1)
                    if i >= 1:
                        d, h = divmod(i - 1, H)
                        r, N = bflip(d, h), DV + 1
                        ac.wait_ge(pv_done.sem, pv_done.at(l, i))
                        if i >= 3:
                            ac.wait_ge(m_out.sem, m_out.at(l, i - 2))
                        for t in (1, 2):
                            o = ac.activation(m_x[:, (i - 1) % 2, (t - 1) * N:t * N],
                                              bank(6 + (i - 1) % 2)[:, (t - 1) * N:t * N],
                                              ACT.Copy, scale=cols[:, 3 + t, r:r + 1])
                        o.then_inc(inter_ready.sem, 1)
                for i in range(8):
                    ac.wait_ge(st_done.sem, st_done.at(l, i + 1))
                    ac.wait_ge(outs.sem, l * outs.per_layer + 16 * (4 + i))
                    ac.activation(st_out, bank(0)[:, 0:DV + 1], ACT.Copy).then_inc(st_copied.sem, 1)
                finish(l, 0)

                for u in range(24):
                    h, t, c = u // 6, (u // 2) % 3, u % 2
                    nk = P if t == 0 else T
                    ac.wait_ge(negmax.sem, negmax.at(l, u + 1))
                    if u >= 4:
                        ac.wait_ge(dw_ready.sem, dw_ready.at(l, u // 2 - 1))
                    ac.activation(d_p[(u // 2) % 2][:, c, 0:nk], bank(u % 2)[:, 0:nk], ACT.Exp, scale=D_SCALE,
                                  bias=small[:, 24 + u % 4:25 + u % 4],
                                  accum_out=small[:, 28 + u % 4:29 + u % 4]).then_inc(p_ready.sem, 1)
                    if u % 2 and u >= 3:
                        v = u // 2 - 1
                        d_copy(v)
                d_copy(11)
                finish(l, 1)

                ac.wait_ge(la_done.sem, la_done.at(l, 1))
                ac.wait_ge(fin_n.sem, fin_n.at(l, 2))
                for t in range(NT):
                    chain.step(ac.activation(scrB[:, t * 512:(t + 1) * 512], bank(4 + t), ACT.Abs))
                chain.settle()
                chain.step(ac.activation(scrB, scrB, ACT.Exp, scale=-1.0))
                chain.settle()
                ac.activation(scrB, scrB, ACT.Ln, bias=ones[:, 0:1]).then_inc(la_exp.sem, 1)
                for u in range(4):
                    ac.wait_ge(g_done.sem, g_done.at(l, u + 1))
                    if u == 0:
                        ac.wait_ge(la_ready.sem, la_ready.at(l, 1))
                    ac.activation(gT[:, u, :], bank(u % 2)[:, 0:T], ACT.Copy).then_inc(g_ready.sem, 1)
                for u in range(4):
                    for t in range(NT):
                        n = u * 3 + t
                        ac.wait_ge(gd_ready.sem, gd_ready.at(l, n + 1))
                        chain.step(ac.activation(g_x, g_x, ACT.Abs))
                        chain.settle()
                        ac.activation(g_x, g_x, ACT.Exp, scale=-1.0).then_inc(gx_ready.sem, 1)
                    ac.wait_ge(gcd_ready.sem, gcd_ready.at(l, u + 1))
                    chain.step(ac.activation(g_xx, g_xx, ACT.Abs))
                    chain.step(ac.activation(g_kd, g_kd, ACT.Abs))
                    chain.settle()
                    chain.step(ac.activation(g_xx, g_xx, ACT.Exp, scale=-1.0))
                    chain.step(ac.activation(g_kd, g_kd, ACT.Exp, scale=-1.0))
                    ac.activation(g_qs, gT[:, u, LAT], ACT.Exp).then_inc(gcx_ready.sem, 1)
                    for hh in range(2):
                        ac.wait_ge(gc_done.sem, gc_done.at(l, u * 2 + hh + 1))
                        ac.activation(g_att[hh], bank(6)[:, 0:P], ACT.Copy).then_inc(gc_copied.sem, 1)
                    ac.wait_ge(gs_t.sem, gs_t.at(l, u + 1))
                    ac.activation(g_kt, bank(7)[:, 0:P], ACT.Copy).then_inc(gs_tc.sem, 1)
                    ac.wait_ge(gs_done.sem, gs_done.at(l, u + 1))
                    ac.wait_ge(outs.sem, l * outs.per_layer + 16 * (12 + 2 * u))
                    for hh in range(2):
                        ac.activation(g_so[64 * hh:64 * hh + 64, :], bank(7)[64 * hh:64 * hh + 64, hh * P:(hh + 1) * P],
                                      ACT.Copy).then_inc(gs_copied.sem, 1)
                    if u % 2:
                        for hh in range(2):
                            head = (u // 2) * 2 + hh
                            ac.wait_ge(go_done.sem, go_done.at(l, u * 2 + hh + 1))
                            ac.activation(ytok[:, :, head * P:(head + 1) * P],
                                          bank(4 + hh)[:, 0:T].rearrange("p (t n) -> p t n", t=NT), ACT.Copy)\
                              .then_inc(go_copied.sem, 1)
                finish(l, 2)

                ac.wait_ge(conv_mean.sem, conv_mean.at(l, 1))
                ac.wait_ge(outs.sem, l * outs.per_layer + outs.per_layer)
                ac.activation(e_t[:, :, :], pc[:, CA, :, :], ACT.Square).then_inc(conv_sq.sem, 1)
                ac.wait_ge(conv_sum.sem, conv_sum.at(l, 2))
                chain.step(ac.activation(rstd[:, :], bank(7)[:, 0:T], ACT.Ln, scale=1.0 / W, bias=eps[:, 0:1]))
                chain.settle()
                ac.activation(rstd[:, :], rstd[:, :], ACT.Exp, scale=-0.5).then_inc(conv_rs.sem, 1)
                ac.wait_ge(conv_n.sem, conv_n.at(l, 1))
                for c in range(4):
                    chain.step(ac.activation(pc[:, CB, c, :], pc[:, CB, c, :], ACT.Identity,
                                             scale=pp("ln_g")[:, c:c + 1], bias=pp("ln_b")[:, c:c + 1]))
                chain.settle()
                ac.activation(pc[:, CB, :, :], pc[:, CB, :, :], ACT.Silu).then_inc(conv_done.sem, 1)

                with ac.Fori(0, 4) as i:
                    for n in range(8):
                        ac.wait_ge(gate_done.sem, l * 32 + i * 8 + (n + 1))
                        ac.wait_ge(merged_s.sem, l * 32 + i * 8 + (n + 1))
                        ac.activation(e_t[:, n % 2, :], bank(n % 2)[:, 0:T], ACT.Sigmoid).then_inc(gate_sig.sem, 1)
                norm(l, 1)
                for t in range(NT):
                    ac.wait_ge(rt_step.sem, rt_step.at(l, 2 * t + 1))
                    ac.activation(rt[:, 100:104], rt[:, 100:104], ACT.Exp,
                                  accum_out=rt[:, 104:105]).then_inc(rt_exp.sem, 1)
                    ac.wait_ge(rt_step.sem, rt_step.at(l, 2 * t + 2))
                    ac.activation(rt[:, 105:106], rt[:, 105:106], ACT.Exp).then_inc(rt_exp.sem, 1)
                def copy_gathered(x):
                    ac.wait_ge(xh_done.sem, l * (NE + 1) + x + 1)
                    ac.activation(scr[:, 0:1024], psum[0][:, :], ACT.Copy).then_inc(xh_ready.sem, 1)

                copy_gathered(0)
                ac.wait_ge(pt_done.sem, pt_done.at(l, 1))
                ac.activation(x_pT[0], bank(7)[:, 0:T], ACT.Copy).then_inc(pt_ready.sem, 1)
                with ac.Fori(0, NE // 2) as i:
                    for p in range(2):
                        ac.wait_ge(xab_done.sem, l * NE + i * 2 + (p + 1))
                        ac.activation(x_s, bank(2), ACT.Silu).then_inc(xs_ready.sem, 1)
                        copy_gathered(i * 2 + (p + 1))
                        ac.wait_ge(xgt_done.sem, l * NE + i * 2 + (p + 1))
                        ac.activation(x_gT, bank(4), ACT.Copy).then_inc(xgt_ready.sem, 1)
                        ac.wait_ge(xy_done.sem, l * NE + i * 2 + (p + 1))
                        for n in range(2):
                            o = ac.activation(x_y[:, n * 512:(n + 1) * 512], bank(5 + n), ACT.Copy)
                        o.then_inc(xy_ready.sem, 1)
                        ac.wait_ge(pt_done.sem, l * (NE + 1) + i * 2 + (p + 2))
                        ac.activation(x_pT[1 - p], bank(7)[:, 0:T], ACT.Copy).then_inc(pt_ready.sem, 1)
                ac.wait_ge(spill_known.sem, spill_known.at(l, 1))
                ac.sem_inc(spill_asked.sem, 1)
                spilled = ac.value_load(spill[0:1, 0:1], min_val=0, max_val=1)
                with ac.If(spilled > 0):
                    with ac.Fori(0, NE // 2) as i:
                        for p in range(2):
                            ac.wait_ge(wb_done.sem, l * 16 + i * 2 + (p + 1))
                            ac.wait_ge(gu_ready.sem, l * 64 + i * 8 + (4 * p + 4))
                            ac.activation(wb, bank(6)[:, 0:T], ACT.Copy).then_inc(wb_ready.sem, 1)
                            for f in range(4):
                                ac.wait_ge(ab_done.sem, l * 64 + i * 8 + (4 * p + f + 1))
                                ac.wait_ge(gu_ready.sem, l * 64 + i * 8 + (4 * p + f + 3))
                                ac.activation(e_t[:, f % 2, :], bank(f % 2)[:, 0:T], ACT.Silu).then_inc(a_exp.sem, 1)
                with ac.Else():
                    for s in (wb_ready, a_exp):
                        ac.sem_inc(s.sem, s.per_layer)
            assert chain.n == ACT_STEPS, chain.n
            ac.wait_ge(x_ready.sem, 2 * DEPTH + 1)
            squares()
            ac.wait_ge(sumsq_done.sem, 2 * DEPTH + 1)
            ac.activation(rstd[:, :], bank(0)[:, 0:T], ACT.Ln, scale=1.0 / D, bias=eps[:, 0:1]).then_inc(final_s.sem, 1)
            ac.wait_ge(final_s.sem, 1)
            ac.activation(rstd[:, :], rstd[:, :], ACT.Exp, scale=-0.5).then_inc(final_s.sem, 1)

        @block.vector
        def _(ve):
            chain = Chain(ve, dve_chain, DVE_STEPS)
            for s, n in ((params_free, 1), (mod_used, 1), (merged_s, 2), (out_used, 2), (ht_copied, 2), (back_used, 2), (gu_ready, 4), (y_used, 2)):
                ve.sem_inc(s.sem, n)
            ve.memset(mva[:, :, :, DV:DV + 1], 1.0)
            ve.memset(gaT[32:33, :], 1.0)
            ve.memset(eps[:, :], EPS)
            ve.memset(rw[:, :, NE:NE + 1], 0.0)
            ve.memset(rk[:, :, NE:NE + 1], 0.0)
            ve.wait_ge(loaded.sem, 32)
            ve.sem_inc(x_ready.sem, 1)
            ve.wait_ge(setup_s.sem, 1)
            ve.tensor_scalar(small[:, 0:16], small[:, 0:16], 1.0, None, ALU.add).then_inc(setup_s.sem, 1)
            ve.wait_ge(setup_s.sem, 2)
            ve.reciprocal(small[:, 0:16], small[:, 0:16]).then_inc(setup_s.sem, 1)
            ve.wait_ge(setup_s.sem, 3)
            ve.tensor_tensor(cc("cond"), cc("cond"), small[:, 0:16], ALU.mult).then_inc(setup_s.sem, 1)
            ve.wait_ge(setup_s.sem, 4)
            ve.memset(rows[:, :, :], 0.0).then_inc(setup_s.sem, 1)
            ve.memset(merged[:, :, :], 0.0).then_inc(setup_s.sem, 1)
            ve.memset(small[:, 60:62], 0.0).then_inc(setup_s.sem, 1)
            ve.wait_ge(setup_s.sem, 7)

            def step(o):
                chain.step(o)

            def scaled(l, which):
                for k in range(KD):
                    if k == 0:
                        ve.wait_ge(rstd_ready.sem, l * 2 + (which + 1))
                    ve.tensor_tensor(hT[:, k, :], xT[:, k, :], rstd[:, :], ALU.mult).then_inc(xn_ready.sem, 1)

            def finish_sums(l, b):
                step(ve.tensor_tensor(scrB, ytok[:, :, :].rearrange("p t n -> p (t n)"),
                                      ytok[:, :, :].rearrange("p t n -> p (t n)"), ALU.mult))
                chain.settle()
                o = ve.tensor_reduce(small[:, 0:12], scrB.rearrange("p (a n) -> p a n", n=P), AX.X, ALU.add)
                o.then_inc(fin_sq.sem, 1)
                ve.wait_ge(fin_rs.sem, fin_rs.at(l, b + 1))
                yv = ytok[:, :, :].rearrange("p t (h n) -> p (t h) n", h=H)
                ve.tensor_tensor(yv, yv, small[:, 12:24].rearrange("p (a b) -> p a b", b=1)
                                 .to_broadcast([P, 12, P]), ALU.mult).then_inc(fin_n.sem, 1)

            with ve.Fori(0, DEPTH) as l:
                chain.layer, chain.n = l, 0
                with ve.Fori(0, NMOD // RING) as i:
                    for j in range(RING):
                        ve.wait_ge(mod_done.sem, l * NMOD + i * RING + (j + 1))
                        ve.tensor_copy(mod_rows[:, j * W:(j + 1) * W], bank(5 + j)[0:2, :]).then_inc(mod_row.sem, 1)
                    ve.wait_ge(params_in.sem, params_in.at(l, 32))
                    ve.wait_ge(mod_turned.sem, l * (NMOD // RING) + i + 1)
                    bias = par[:, bass.ds(i * 12 + PAR["bmod"][0], 12)]
                    ve.tensor_tensor(mod[:, bass.ds(i * 12, 12), :],
                                     bank(4)[:, 0:24].rearrange("p (a b) -> p a b", b=2),
                                     bias.rearrange("p (a b) -> p a b", b=1).to_broadcast([P, 12, 2]), ALU.add)\
                      .then_inc(mod_used.sem, 1)
                ve.wait_ge(mod_used.sem, mod_used.at(l, NMOD // RING))
                for w, nm in enumerate(("norm1", "norm2")):
                    g = pp(nm).rearrange("p (a b) -> p a b", b=1).to_broadcast([P, KD, 2])
                    step(ve.scalar_tensor_tensor(amp[:, w, :, :], mod[:, 24 * w + 8:24 * w + 16, :], 1.0, g,
                                                 ALU.add, ALU.mult))
                ve.tensor_tensor(small[0:64, 40:42], pp("lam")[0:64, 0:4:2], pp("lam")[0:64, 1:4:2], ALU.mult)\
                  .then_inc(lamp_ready.sem, 1)
                scaled(l, 0)

                ve.wait_ge(ga_ready.sem, ga_ready.at(l, 1))
                step(ve.scalar_tensor_tensor(rows[:, R_F, :], rows[:, R_F, :], 0.0, rows[:, R_T, :],
                                             ALU.min, ALU.subtract))
                chain.settle()

                def scans(fn):
                    for d in range(2):
                        rs = slice(32 * d, 32 * d + 4)
                        for grp, (a, b) in enumerate(((0, SEQ), (SEQ, T))):
                            back = slice(b - 1, a - 1 if a else None, -1)
                            fn(rs, grp, slice(a, b) if d == 0 else back)
                scans(lambda rs, grp, s: step(ve.tensor_tensor_scan(
                    rows[rs, R_B, s], ones[rs, 0:1].to_broadcast([4, (P, DEC)[grp]]), rows[rs, R_F, s], 0.0, ALU.mult, ALU.add)))
                chain.settle()
                step(ve.tensor_tensor(rows[0:36, R_U, :], rows[0:36, R_I, :], rows[0:36, R_B, :], ALU.subtract))
                chain.settle()
                scans(lambda rs, grp, s: step(ve.tensor_tensor_scan(
                    rows[rs, R_T, s], cc("zero")[rs, 0:1].to_broadcast([4, (P, DEC)[grp]]), rows[rs, R_U, s],
                    0.0 if grp == 0 else pp("m0")[rs, :], ALU.add, ALU.max)))
                chain.settle()
                step(ve.tensor_scalar(rows[0:36, R_NG, :], rows[0:36, R_T, :], -1.0, None, ALU.mult))
                step(ve.tensor_tensor(rows[0:36, R_EM, :], rows[0:36, R_T, :], rows[0:36, R_B, :], ALU.add))
                chain.settle()
                for d in range(2):
                    rs, last = slice(32 * d, 32 * d + 4), SEQ - 1 if d == 0 else 0
                    step(ve.tensor_copy(small[rs, 60:61], rows[rs, R_EM, last:last + 1]))
                    o = ve.tensor_copy(small[rs, 61:62], rows[rs, R_NG, last:last + 1])
                    if d == 0:
                        step(o)
                o.then_inc(rows_ready.sem, 1)

                ve.wait_ge(cb_sig.sem, cb_sig.at(l, 1))
                step(ve.tensor_tensor(upad[:, :, PAD:PAD + SEQ], pc[:, CA, :, CTX], pc[:, CB, :, CTX], ALU.mult))
                step(ve.tensor_tensor(upad[:, :, 2 * PAD + SEQ:2 * PAD + T], pc[:, CA, :, LAT], pc[:, CB, :, LAT],
                                      ALU.mult))
                for z in (0, PAD + SEQ, 2 * PAD + T):
                    step(ve.memset(upad[:, :, z:z + PAD], 0.0))
                chain.settle()
                for j in range(CW):
                    for c in range(4):
                        for first, g in ((0, CTX), (PAD, LAT)):
                            src = upad[:, c, g.start + first + j:g.stop + first + j]
                            dst = pc[:, CA, c, g]
                            if j == 0:
                                step(ve.tensor_scalar(dst, src, taps[:, c, 0:1], None, ALU.mult))
                                continue
                            chain.settle(but=7)
                            o = ve.scalar_tensor_tensor(dst, src, taps[:, c, j:j + 1], dst, ALU.mult, ALU.add)
                            if j == CW - 1 and c == 3 and g is LAT:
                                o.then_inc(conv_acc.sem, 1)
                            else:
                                step(o)

                ve.wait_ge(lame_ready.sem, lame_ready.at(l, 1))
                chain.settle()
                step(ve.tensor_tensor(small[:, 44:45], small[:, 42:43], small[:, 43:44], ALU.subtract))
                chain.settle()
                step(ve.tensor_tensor(small[:, 44:45], small[:, 44:45],
                                      cst[:, bass.ds(l + CST["lam_init"][0], 1)], ALU.add))

                ve.wait_ge(cols_done.sem, cols_done.at(l, 1))
                ve.tensor_copy(cols[:, :, :], bank(4)[:, 0:360].rearrange("p (a b) -> p a b", a=10))\
                  .then_inc(cols_ready.sem, 1)
                ve.wait_ge(kt_done.sem, kt_done.at(l, 1))
                ve.tensor_copy(mktok, bank(5).rearrange("p (h n) -> p h n", h=H)).then_inc(kt_ready.sem, 1)
                for i in range(9):
                    if i < 8:
                        ve.wait_ge(mexp_ready.sem, mexp_ready.at(l, i + 1))
                        ve.wait_ge(qk_done.sem, qk_done.at(l, i + 1))
                        if i >= 2:
                            ve.wait_ge(pv_done.sem, pv_done.at(l, i - 1))
                        ve.scalar_tensor_tensor(m_s[i % 2], bank(2 + i % 2), M_SCALE, m_exp[i % 2],
                                                ALU.mult, ALU.mult).then_inc(s_ready.sem, 1)
                    if i >= 1:
                        n, N = i - 1, DV + 1
                        d, h = divmod(n, H)
                        r = bflip(d, h)
                        ve.wait_ge(inter_ready.sem, inter_ready.at(l, n + 1))
                        V = bank(4 + n % 2)
                        if n >= 1:
                            ve.wait_ge(m_out.sem, m_out.at(l, n))
                        step(ve.tensor_copy(m_nd[:, 0, :], V[:, 0:N]))
                        step(ve.tensor_tensor(m_nd[:, 1:3, :], V[:, N:3 * N].rearrange("p (t n) -> p t n", t=2),
                                              m_x[:, n % 2, :].rearrange("p (t n) -> p t n", t=2), ALU.add))
                        chain.settle()
                        den = m_nd[:, :, DV:N].rearrange("p t n -> p (t n)")
                        step(ve.scalar_tensor_tensor(small[:, 45:48], den, -1.0, den, ALU.mult, ALU.max))
                        chain.settle()
                        step(ve.tensor_tensor(small[:, 45:48], small[:, 45:48],
                                              cols[:, 6:9, r:r + 1].rearrange("p t n -> p (t n)"), ALU.max))
                        chain.settle()
                        step(ve.reciprocal(small[:, 45:48], small[:, 45:48]))
                        chain.settle()
                        for t in range(NT):
                            y = ytok[:, t, h * P:(h + 1) * P]
                            if d == 0:
                                o = ve.tensor_scalar(y, m_nd[:, t, 0:DV], small[:, 45 + t:46 + t], None, ALU.mult)
                            else:
                                o = ve.scalar_tensor_tensor(y, m_nd[:, t, 0:DV], small[:, 45 + t:46 + t], y,
                                                            ALU.mult, ALU.add)
                            if t < NT - 1:
                                step(o)
                        o.then_inc(m_out.sem, 1)
                        chain.settle()
                for i in range(8):
                    d, h = divmod(i, H)
                    r = bflip(d, h)
                    if i >= 1:
                        ve.wait_ge(st_done.sem, st_done.at(l, i))
                    ve.tensor_scalar(kstate, mktok[:, h, :], cols[:, 9, r:r + 1], M_SCALE,
                                     ALU.mult, ALU.mult).then_inc(kw_ready.sem, 1)
                ve.wait_ge(m_out.sem, m_out.at(l, 8))
                ve.wait_ge(kw_ready.sem, kw_ready.at(l, 8))
                finish_sums(l, 0)
                ve.wait_ge(fin_t.sem, fin_t.at(l, 1))
                chain.settle()
                for h in range(H):
                    o = ve.scalar_tensor_tensor(pc[:, MO, h, :], bank(h)[:, 0:T], pp("hn_m")[:, h:h + 1],
                                                pc[:, MO, h, :], ALU.mult, ALU.mult)
                o.then_inc(fin_done.sem, 1)

                for n in range(8):
                    slot, h = (DQ, DKK)[n // 4], n % 4
                    v = pc[:, slot, h, LAT]
                    ve.wait_ge(rot_done.sem, rot_done.at(l, n + 1))
                    step(ve.tensor_tensor(scr[:, 0:DEC], bank(n % 2)[:, 0:DEC], cc("sin"), ALU.mult))
                    step(ve.tensor_tensor(v, v, cc("cos"), ALU.mult))
                    chain.settle()
                    ve.tensor_tensor(v, v, scr[:, 0:DEC], ALU.add).then_inc(rot_used.sem, 1)
                    ve.wait_ge(rot_used.sem, rot_used.at(l, n + 1))

                def d_weights(v):
                    h, t = divmod(v, 3)
                    nk = P if t == 0 else T
                    q = (v % 2) * 2
                    dp = d_p[v % 2]
                    ve.wait_ge(p_ready.sem, p_ready.at(l, 2 * v + 2))
                    step(ve.reciprocal(small[:, 32:34], small[:, 28 + q:30 + q]))
                    chain.settle()
                    step(ve.tensor_tensor(small[:, 34:35], small[:, 33:34], small[:, 44:45], ALU.mult))
                    chain.settle()
                    step(ve.tensor_scalar(dp[:, 1, 0:nk], dp[:, 1, 0:nk], small[:, 34:35], None, ALU.mult))
                    if v >= 1:
                        ve.wait_ge(dwt_done.sem, dwt_done.at(l, v))
                    chain.settle()
                    ve.scalar_tensor_tensor(d_w[:, 0:nk], dp[:, 0, 0:nk], small[:, 32:33], dp[:, 1, 0:nk],
                                            ALU.mult, ALU.subtract).then_inc(dw_ready.sem, 1)
                    ve.wait_ge(dwt_done.sem, dwt_done.at(l, v + 1))
                    if v >= 1:
                        ve.wait_ge(dpv_done.sem, dpv_done.at(l, v))
                    ve.tensor_copy(d_wt[:, 0:nk], bank(2)[:, 0:nk]).then_inc(dwt_ready.sem, 1)

                for u in range(24):
                    h, t, c = u // 6, (u // 2) % 3, u % 2
                    nk = P if t == 0 else T
                    ve.wait_ge(sc_done.sem, sc_done.at(l, u + 1))
                    if u >= 4:
                        ve.wait_ge(p_ready.sem, p_ready.at(l, u - 3))
                    step(ve.tensor_reduce(small[:, 35:36], bank(u % 2)[:, 0:nk], AX.X, ALU.max))
                    chain.settle()
                    ve.tensor_scalar(small[:, 24 + u % 4:25 + u % 4], small[:, 35:36], -D_SCALE, None, ALU.mult)\
                      .then_inc(negmax.sem, 1)
                    ve.wait_ge(negmax.sem, negmax.at(l, u + 1))
                    if u % 2 and u >= 3:
                        d_weights(u // 2 - 1)
                d_weights(11)
                ve.wait_ge(dpv_copied.sem, dpv_copied.at(l, 12))
                finish_sums(l, 1)
                step(ve.tensor_scalar(small[:, 36:40], pp("hn_d"), cst[:, bass.ds(l + CST["one_less"][0], 1)], None,
                                      ALU.mult))
                ve.wait_ge(fin_t.sem, fin_t.at(l, 2))
                chain.settle()
                for h in range(H):
                    o = ve.tensor_scalar(pc[:, DQ, h, :], bank(h)[:, 0:T], small[:, 36 + h:37 + h], None, ALU.mult)
                o.then_inc(fin_done.sem, 1)

                ve.wait_ge(la_exp.sem, la_exp.at(l, 1))
                for t in range(NT):
                    o = ve.scalar_tensor_tensor(la[:, t, :], bank(4 + t), 0.0, scrB[:, t * 512:(t + 1) * 512],
                                                ALU.min, ALU.subtract)
                o.then_inc(la_ready.sem, 1)
                step(ve.tensor_scalar(pc[:, GQK, 0:2, :], pc[:, GQK, 0:2, :], G_SCALE, None, ALU.mult))
                ve.wait_ge(g_ready.sem, g_ready.at(l, 4))
                ve.wait_ge(outs.sem, l * outs.per_layer + 16 * 12)
                for u in range(4):
                    pair, d = divmod(u, 2)
                    q, k = pc[:, GQK, pair, :], pc[:, GQK, 2 + pair, :]
                    for t in range(NT):
                        n = u * 3 + t
                        for lv in range(LEVELS):
                            w = 1 << lv
                            gv_ = gT[:, u, tok(t)].rearrange("p (b w) -> p b w", w=2 * w)
                            mid = w - 1 if d == 0 else w
                            o = ve.tensor_tensor(g_x[:, lv, :].rearrange("p (b w) -> p b w", w=2 * w), gv_,
                                                 gv_[:, :, mid:mid + 1].to_broadcast([P, P // (2 * w), 2 * w]),
                                                 ALU.subtract)
                        o.then_inc(gd_ready.sem, 1)
                        ve.wait_ge(gx_ready.sem, gx_ready.at(l, n + 1))
                        if n >= 1:
                            ve.wait_ge(ga_done.sem, ga_done.at(l, 2 * n))
                        chain.settle()
                        for dst, src in ((g_q, q), (g_k, k)):
                            s3 = src[:, tok(t)].rearrange("p (a b) -> p a b", a=1).to_broadcast([P, LEVELS, P])
                            step(ve.tensor_tensor(dst[:, 0:LEVELS, :], s3, g_x, ALU.mult))
                            o = ve.tensor_copy(dst[:, LEVELS, :], src[:, tok(t)])
                            if dst is g_q:
                                step(o)
                        o.then_inc(gqk_ready.sem, 1)
                        for hh in range(2):
                            ve.wait_ge(ga_done.sem, ga_done.at(l, 2 * n + hh + 1))
                            chain.settle()
                            if n >= 1:
                                ve.wait_ge(gatt_ready.sem, gatt_ready.at(l, 2 * n + hh))
                            step(ve.tensor_tensor(g_m, psum[hh][:, :], lev[d], ALU.mult))
                            chain.settle()
                            ve.tensor_reduce(g_att[hh], g_m.rearrange("p (l t) -> p t l", l=8), AX.X, ALU.add)\
                              .then_inc(gatt_ready.sem, 1)
                            ve.wait_ge(gatt_ready.sem, gatt_ready.at(l, 2 * n + hh + 1))
                    ref = 2 * P - 1 if d == 0 else 2 * P
                    last = SEQ - 1 if d == 0 else 0
                    tq, tk = (2, 1) if d == 0 else (1, 2)
                    if u >= 1:
                        ve.wait_ge(go_done.sem, go_done.at(l, 2 * u))
                        ve.wait_ge(gs_copied.sem, gs_copied.at(l, 2 * u))
                    gr = gT[:, u, :]
                    step(ve.tensor_tensor(g_xx, gr[:, LAT], gr[:, ref:ref + 1].to_broadcast([P, DEC]), ALU.subtract))
                    ve.tensor_tensor(g_kd, gr[:, CTX], gr[:, last:last + 1].to_broadcast([P, P]), ALU.subtract)\
                      .then_inc(gcd_ready.sem, 1)
                    ve.wait_ge(gcx_ready.sem, gcx_ready.at(l, u + 1))
                    step(ve.tensor_tensor(g_qx, q[:, tok(tq)], g_xx[:, tok(tq - 1)], ALU.mult))
                    step(ve.tensor_tensor(g_kx, k[:, tok(tk)], g_xx[:, tok(tk - 1)], ALU.mult))
                    step(ve.tensor_tensor(g_kd, k[:, CTX], g_kd, ALU.mult))
                    ve.tensor_tensor(g_qs, q[:, LAT], g_qs, ALU.mult).then_inc(gcq_ready.sem, 1)
                    ve.wait_ge(go_done.sem, go_done.at(l, 2 * u + 2))
                ve.wait_ge(go_copied.sem, go_copied.at(l, 4))
                finish_sums(l, 2)
                ve.wait_ge(fin_t.sem, fin_t.at(l, 3))
                chain.settle()
                for h in range(H):
                    o = ve.scalar_tensor_tensor(pc[:, GR, h, :], bank(h)[:, 0:T], pp("hn_g")[:, h:h + 1],
                                                pc[:, GR, h, :], ALU.mult, ALU.mult)
                o.then_inc(fin_done.sem, 1)

                ve.wait_ge(conv_sum.sem, conv_sum.at(l, 1))
                step(ve.tensor_scalar(cmean, bank(6)[:, 0:T], 1.0 / W, None, ALU.mult))
                chain.settle()
                ve.tensor_tensor(pc[:, CA, :, :], pc[:, CA, :, :],
                                 cmean.rearrange("p (a b) -> p a b", a=1).to_broadcast([P, 4, T]),
                                 ALU.subtract).then_inc(conv_mean.sem, 1)
                ve.wait_ge(conv_mean.sem, conv_mean.at(l, 1))
                ve.wait_ge(conv_rs.sem, conv_rs.at(l, 1))
                ve.tensor_tensor(pc[:, CB, :, :], pc[:, CA, :, :],
                                 rstd[:, :].rearrange("p (a b) -> p a b", a=1).to_broadcast([P, 4, T]),
                                 ALU.mult).then_inc(conv_n.sem, 1)

                step(ve.memset(merged[:, :, :], 0.0))
                with ve.Fori(0, 4) as i:
                    for n in range(8):
                        e = e_t[:, n % 2, :]
                        gg = e_t[:, 2 + n % 2, :]
                        ve.wait_ge(gate_sig.sem, l * 32 + i * 8 + (n + 3))
                        ve.wait_ge(br_done.sem, l * 32 + i * 8 + (n + 1))
                        ve.tensor_tensor(gg, e, bank(2 + n % 2)[:, 0:T], ALU.mult).then_inc(merge_x.sem, 1)
                        ve.wait_ge(merge_x.sem, l * 32 + i * 8 + (n + 1))
                        ve.wait_ge(merged_s.sem, l * 32 + i * 8 + (n + 2))
                        ve.tensor_tensor(merged[:, n, :], merged[:, n, :], gg, ALU.add).then_inc(merged_s.sem, 1)
                for n in range(8):
                    ve.wait_ge(out_done.sem, out_done.at(l, n + 1))
                    for c, s in enumerate((CTX, LAT)):
                        o = ve.scalar_tensor_tensor(xT[:, n, s], bank(4 + n % 2)[:, s], mod[:, 16 + n, c:c + 1],
                                                    xT[:, n, s], ALU.mult, ALU.add)
                        if c == 0:
                            step(o)
                    o.then_inc(out_used.sem, 1)
                ve.wait_ge(out_used.sem, out_used.at(l, 8))
                ve.sem_inc(x_ready.sem, 1)
                scaled(l, 1)

                ve.wait_ge(rt_done.sem, rt_done.at(l, 1))
                step(ve.tensor_copy(rt[:, 0:60], bank(6)[:, 0:60]))
                chain.settle()

                def first_best(score, best, sel, tmp):
                    step(ve.tensor_reduce(best, score, AX.X, ALU.max))
                    chain.settle()
                    step(ve.scalar_tensor_tensor(sel, score, best, cc("order"), ALU.is_equal, ALU.mult))
                    chain.settle()
                    step(ve.tensor_reduce(tmp, sel, AX.X, ALU.max))
                    chain.settle()
                    step(ve.tensor_scalar(sel, sel, tmp, None, ALU.is_equal))
                    chain.settle()

                for t in range(NT):
                    gl, el = rt[:, t * 20:t * 20 + 4], rt[:, t * 20 + 4:t * 20 + 20]
                    best, gsel, tmp = rt[:, 60:61], rt[:, 61:65], rt[:, 65:66]
                    first_best(gl, best, gsel, tmp)
                    ve.tensor_scalar(rt[:, 100:104], gl, best, None, ALU.subtract).then_inc(rt_step.sem, 1)
                    g3 = gsel.rearrange("p (a b) -> p a b", b=1).to_broadcast([P, NG, EPG])
                    step(ve.tensor_tensor(rt[:, 70:86].rearrange("p (a b) -> p a b", a=NG),
                                          el.rearrange("p (a b) -> p a b", a=NG), g3, ALU.mult))
                    chain.settle()
                    es = rt[:, 86:90]
                    step(ve.tensor_reduce(es, rt[:, 70:86].rearrange("p (a b) -> p b a", a=NG), AX.X, ALU.add))
                    chain.settle()
                    v1, s1, v2, s2 = rt[:, 90:91], rt[:, 106:110], rt[:, 91:92], rt[:, 110:114]
                    first_best(es, v1, s1, tmp)
                    step(ve.scalar_tensor_tensor(es, s1, -3e38, es, ALU.mult, ALU.add))
                    chain.settle()
                    first_best(es, v2, s2, tmp)
                    ve.wait_ge(rt_exp.sem, rt_exp.at(l, 2 * t + 1))
                    ve.tensor_tensor(rt[:, 105:106], v2, v1, ALU.subtract).then_inc(rt_step.sem, 1)
                    ve.wait_ge(rt_exp.sem, rt_exp.at(l, 2 * t + 2))
                    step(ve.scalar_tensor_tensor(rt[:, 92:93], rt[:, 105:106], 1.0, rt[:, 104:105],
                                                 ALU.add, ALU.mult))
                    chain.settle()
                    step(ve.reciprocal(rt[:, 92:93], rt[:, 92:93]))
                    chain.settle()
                    step(ve.scalar_tensor_tensor(s1, s2, rt[:, 105:106], s1, ALU.mult, ALU.add))
                    chain.settle()
                    step(ve.tensor_scalar(s1, s1, rt[:, 92:93], None, ALU.mult))
                    chain.settle()
                    o = ve.tensor_tensor(rw[:, t, 0:NE].rearrange("p (a b) -> p a b", a=NG), g3,
                                         s1.rearrange("p (a b) -> p a b", a=1).to_broadcast([P, NG, EPG]), ALU.mult)
                    if t < NT - 1:
                        step(o)
                        chain.settle()
                o.then_inc(rt_ready.sem, 1)
                ve.wait_ge(rt_ready.sem, rt_ready.at(l, 1))
                ve.tensor_scalar(sel[:, :, :], rw[:, :, 0:NE], 0.0, None, ALU.not_equal).then_inc(sel_ready.sem, 1)
                for n in range(6):
                    half, t = divmod(n, 3)
                    ve.wait_ge(ht_done.sem, l * 6 + n + 1)
                    ve.tensor_copy(htok[half][:, t, :], bank(2 + n % 2)).then_inc(ht_copied.sem, 1)
                ve.wait_ge(rank_done.sem, rank_done.at(l, 1))
                step(ve.scalar_tensor_tensor(rk[:, :, 0:NE], bank(7)[:, 0:NT * NE].rearrange("p (t e) -> p t e", t=NT),
                                             16.0, sel[:, :, :], ALU.mult, ALU.mult))
                step(ve.tensor_reduce(rt[0:1, 120:121], bank(7)[0:1, NT * NE:(NT + 1) * NE], AX.X, ALU.max))
                chain.settle()
                ve.tensor_scalar(spill[0:1, 0:1], rt[0:1, 120:121], float(P), None, ALU.is_gt)\
                  .then_inc(spill_known.sem, 1)

                def build_slots(x):
                    for t in range(NT):
                        ve.tensor_scalar(x_p[:, t, :], cc("slots"), rk[:, t, bass.ds(x, 1)], None, ALU.is_equal)
                        o = ve.tensor_scalar(x_pw[:, t, :], cc("slots"), rk[:, t, bass.ds(x, 1)],
                                             rw[:, t, bass.ds(x, 1)], ALU.is_equal, ALU.mult)
                    o.then_inc(p_built.sem, 1)

                build_slots(0)
                with ve.Fori(0, NE // 2) as i:
                    for p in range(2):
                        ve.wait_ge(pt_done.sem, l * (NE + 1) + i * 2 + (p + 1))
                        build_slots(i * 2 + (p + 1))
                        ve.wait_ge(xs_ready.sem, l * NE + i * 2 + (p + 1))
                        ve.tensor_tensor(x_g, x_s, bank(3), ALU.mult).then_inc(xg_ready.sem, 1)
                        for n in range(KD):
                            ve.wait_ge(back_done.sem, l * 128 + i * 16 + (8 * p + n + 1))
                            for c, s in enumerate((CTX, LAT)):
                                o = ve.scalar_tensor_tensor(xT[:, n, s], bank(n % 2)[:, s],
                                                            mod[:, 40 + n, c:c + 1], xT[:, n, s], ALU.mult, ALU.add)
                            o.then_inc(back_used.sem, 1)
                ve.wait_ge(spill_known.sem, spill_known.at(l, 1))
                ve.sem_inc(spill_asked.sem, 1)
                spilled = ve.value_load(spill[0:1, 0:1], min_val=0, max_val=1)
                with ve.If(spilled > 0):
                    ve.wait_ge(back_used.sem, l * 128 + (128 + 2))
                    ve.tensor_scalar(sel[:, :, :], rk[:, :, 0:NE], float(P), None, ALU.is_gt).then_inc(sp_free.sem, 1)
                    ve.wait_ge(sp_free.sem, sp_free.at(l, 1))
                    ve.tensor_tensor(rw[:, :, 0:NE], rw[:, :, 0:NE], sel[:, :, :], ALU.mult).then_inc(sp_rw.sem, 1)
                    ve.wait_ge(rtt_done.sem, rtt_done.at(l, 1))
                    ve.tensor_copy(wT, bank(7)[0:NE, 0:T]).then_inc(wT_ready.sem, 1)
                    ve.wait_ge(wT_ready.sem, wT_ready.at(l, 1))
                    ve.tensor_scalar(wm, wT, ident[0:NE, 0:1], None, ALU.mult).then_inc(wm_ready.sem, 1)
                    with ve.Fori(0, NE // 2) as i:
                        for p in range(2):
                            for f in range(4):
                                e, s = e_t[:, f % 2, :], e_t[:, 2 + f % 2, :]
                                ve.wait_ge(a_exp.sem, l * 64 + i * 8 + (4 * p + f + 1))
                                ve.tensor_tensor(s, e, bank(2 + f % 2)[:, 0:T], ALU.mult).then_inc(e_x.sem, 1)
                                ve.wait_ge(e_x.sem, l * 64 + i * 8 + (4 * p + f + 1))
                                if f == 0:
                                    ve.wait_ge(wb_ready.sem, l * 16 + i * 2 + (p + 1))
                                    ve.wait_ge(y_used.sem, l * 128 + i * 16 + (8 * p + 2))
                                ve.tensor_tensor(gu[:, f, :], s, wb, ALU.mult).then_inc(gu_ready.sem, 1)
                            ve.tensor_scalar(wm, wT, cst[0:NE, bass.ds(i * 2 + (p + 1 + CST["ident"][0]), 1)], None,
                                             ALU.mult).then_inc(wm_ready.sem, 1)
                            for n in range(KD):
                                ve.wait_ge(y_done.sem, l * 128 + i * 16 + (8 * p + n + 1))
                                for c, s in enumerate((CTX, LAT)):
                                    o = ve.scalar_tensor_tensor(xT[:, n, s], bank(4 + n % 2)[:, s],
                                                                mod[:, 40 + n, c:c + 1], xT[:, n, s],
                                                                ALU.mult, ALU.add)
                                o.then_inc(y_used.sem, 1)
                with ve.Else():
                    ve.wait_ge(back_used.sem, l * 128 + (128 + 2))
                    for s in (sp_free, sp_rw, wT_ready, wm_ready, e_x, gu_ready, y_used):
                        ve.sem_inc(s.sem, s.per_layer)
                ve.wait_ge(y_used.sem, l * 128 + (128 + 2))
                ve.sem_inc(x_ready.sem, 1)
                ve.sem_inc(params_free.sem, 1)
            assert chain.n == DVE_STEPS, chain.n
            ve.wait_ge(final_s.sem, 2)
            for k in range(KD):
                o = ve.tensor_tensor(hT[:, k, :], xT[:, k, :], rstd[:, :], ALU.mult)
            o.then_inc(final_s.sem, 1)
            ve.wait_ge(final_s.sem, 3)
            for k in range(KD):
                o = ve.tensor_scalar(hT[:, k, :], hT[:, k, :], cc("final")[:, k:k + 1], None, ALU.mult)
            o.then_inc(final_s.sem, 1)


_STARTS = {GR: 4656, CA: 5168, CB: 5680, GQK: 3600, DQ: 2064, DKK: 2576, MO: 1536, MQ: 0, MK: 512}
_TOKEN_STARTS = (1024, 3088, 4112)
_MERGE_ORDER = (2, 3, 1, 0)


def _by_partition(w, n):
    import numpy as np
    k, cols = w.shape
    return np.ascontiguousarray(w.reshape(k // P, P, cols // n, n).transpose(2, 1, 0, 3)).reshape(cols // n, P, -1)


def _constants(inputs):
    import numpy as np
    c = np.zeros((P, NCST), np.float32)

    def put(name, v):
        c[:, CST[name][0]:CST[name][1]] = np.asarray(v, np.float32).reshape(P, -1)

    s, t = np.arange(P)[:, None], np.arange(P)[None, :]
    put("ident", s == t)
    put("swap", (s // 64 == t // 64) & (s % 32 == t % 32) & (s != t))
    n_freq = DQK // 4
    inv = 10000.0 ** (-np.arange(n_freq, dtype=np.float32) / n_freq)
    r, col = np.divmod(np.arange(DEC), 64)
    ang = np.concatenate([r[:, None] * inv, col[:, None] * inv], axis=1).astype(np.float32)
    part = np.arange(P)
    put("cos", np.cos(ang).T[part % 32])
    put("sin", np.sin(ang).T[part % 32] * np.where(part % 64 < 32, -1.0, 1.0)[:, None])
    put("tri_f", (s <= t) / 16.0)
    put("tri_b", (s >= t) / 16.0)
    put("sixteenth", np.full((P, P), 1 / 16.0))
    put("ones", np.ones((P, P)))
    put("neg_f", np.where(s <= t, 0.0, MASKED))
    put("neg_b", np.where(s >= t, 0.0, MASKED))
    for name, a, b in (("lev_f", s, t), ("lev_b", t, s)):
        m = np.zeros((P, 8, P))
        for lv in range(LEVELS):
            w = 1 << lv
            m[:, lv] = (s // (2 * w) == t // (2 * w)) & (a % (2 * w) < w) & (b % (2 * w) >= w)
        m[:, LEVELS] = s == t
        put(name, m)
    put("slots", np.tile(np.arange(1, P + 1), (P, 1)))
    put("order", np.tile(np.arange(NG, 0, -1), (P, 1)))
    lam = [0.8 - 0.6 * math.exp(-0.3 * l) for l in range(DEPTH)]
    put("lam_init", np.tile(lam, (P, 1)))
    put("one_less", np.tile([1.0 - v for v in lam], (P, 1)))
    put("final", inputs["final_norm"].reshape(KD, P).T)
    put("cond", np.stack([inputs["c_ctx"].reshape(KD, P).T, inputs["c"][0].reshape(KD, P).T], axis=2))
    return c


def _parameters(inputs, l):
    import numpy as np
    a = np.zeros((P, NPAR), np.float32)

    def view(name):
        return a[:, PAR[name][0]:PAR[name][1]]

    def chunks(v):
        return v.reshape(-1, P).T

    for name, key in (("norm1", "norm1"), ("norm2", "norm2"), ("bmod", "b_mod"), ("ln_g", "conv_ln_g"),
                      ("ln_b", "conv_ln_b"), ("hn_m", "hnorm_m"), ("hn_d", "hnorm_d"), ("hn_g", "hnorm_g")):
        view(name)[:] = chunks(inputs[key][l])
    view("taps")[:] = inputs["w_dw"][l].reshape(CW, 4, P).transpose(2, 1, 0).reshape(P, -1)
    for i, key in enumerate(("lam_q1", "lam_k1", "lam_q2", "lam_k2")):
        view("lam")[0:64, i] = inputs[key][l]
    w = inputs["w_in"][l]
    rows, bi, bf = np.zeros((D, P), np.float32), inputs["b_m_i"][l], inputs["b_m_f"][l]
    for d in range(2):
        rows[:, 32 * d:32 * d + 4] = w[:, 2048 + 4 * d:2052 + 4 * d]
        rows[:, 64 + 32 * d:68 + 32 * d] = w[:, 2056 + 4 * d:2060 + 4 * d]
        view("b_i")[32 * d:32 * d + 4, 0] = bi[4 * d:4 * d + 4]
        view("b_f")[64 + 32 * d:68 + 32 * d, 0] = bf[4 * d:4 * d + 4]
        view("m0")[32 * d:32 * d + 4, 0] = inputs["state_mlstm_m"][0, l, d]
    early = np.concatenate([_by_partition(rows, P)[0], _by_partition(w[:, 4624:4656], 32)[0]], axis=1)
    view("router")[:] = _by_partition(np.concatenate([inputs["w_group_router"][l], inputs["w_expert_router"][l]], 1), 20)[0]
    for d in range(2):
        view("w_up")[16 * d:16 * d + 16, 256 * d:256 * d + 256] = inputs["w_gla_up"][l, d]
        view("w_up")[32, 256 * d:256 * d + 256] = inputs["b_gla_gate"][l, d]
    view("S0")[:] = inputs["state_gla_S"][0, l].reshape(2, 2, 2, 64, P).transpose(2, 3, 0, 1, 4).reshape(P, -1)
    cn = np.concatenate([inputs["state_mlstm_C"][0, l], inputs["state_mlstm_n"][0, l][..., None]], axis=3)
    view("C0")[:] = cn.transpose(2, 0, 1, 3).reshape(P, -1)
    view("k_cache")[:] = inputs["cache_diff_k"][0, l].transpose(2, 1, 0).reshape(P, -1)
    view("v_cache")[:] = inputs["cache_diff_v"][0, l].reshape(P, -1)
    return a, early


def kernel(**inputs):
    import numpy as np
    import concourse.bacc as bacc
    from concourse.bass_utils import run_bass_kernel_spmd

    inputs = {k: np.asarray(v) for k, v in inputs.items()}
    L = range(DEPTH)
    w_in = inputs["w_in"]
    x = np.concatenate([inputs["x_prompt"][0], inputs["x_sample"][0]], axis=0)
    arrays = {
        "par": np.stack([_parameters(inputs, l)[0] for l in L]),
        "early": np.stack([_parameters(inputs, l)[1] for l in L]),
        "cst": _constants(inputs),
        "x": np.ascontiguousarray(x.T.reshape(KD, P, T).transpose(1, 0, 2)),
        "wmod": np.concatenate([_by_partition(inputs["w_mod"][l], W) for l in L]),
        "wch": np.concatenate([_by_partition(w_in[l][:, _STARTS[s]:_STARTS[s] + W], W) for l in L for s in range(NCH)]),
        "wtok": np.concatenate([_by_partition(w_in[l][:, s:s + W], W) for l in L for s in _TOKEN_STARTS]),
        "wgate": np.concatenate([_by_partition(w_in[l][:, 6192 + n * D:6192 + (n + 1) * D], W)
                                 for l in L for n in _MERGE_ORDER]),
        "wbr": np.concatenate([_by_partition(inputs["w_branch"][l, n], D) for l in L for n in _MERGE_ORDER]),
        "wout": np.concatenate([_by_partition(inputs["w_out"][l], W) for l in L]),
        "we13": np.concatenate([_by_partition(inputs[k][l, e // EPG, e % EPG], W)
                                for l in L for e in range(NE) for k in ("w_e1", "w_e3")]),
        "we2": np.concatenate([_by_partition(inputs["w_e2"][l, e // EPG, e % EPG], D) for l in L for e in range(NE)]),
    }
    outputs = {"y": (P, KD, T), "ko": (DEPTH, P, H, P), "vo": (DEPTH, P, W), "co": (DEPTH * 8, P, DV + 1),
               "mo": (DEPTH * 2, H, 1), "so": (DEPTH * 8, 64, P)}
    nc = bacc.Bacc("TRN2", target_bir_lowering=False, num_devices=1)
    args = [nc.dram_tensor(f"{n}_in", a.shape, F32, kind="ExternalInput").ap() for n, a in arrays.items()]
    args += [nc.dram_tensor(f"{n}_out", s, F32, kind="ExternalOutput").ap() for n, s in outputs.items()]
    hybrid_step(nc, *args)
    r = run_bass_kernel_spmd(nc, [{f"{n}_in": a for n, a in arrays.items()}], core_ids=[0]).results[0]
    y = r["y_out"].transpose(1, 0, 2).reshape(D, T).T
    ko = r["ko_out"].transpose(0, 3, 2, 1)
    vo = r["vo_out"].reshape(DEPTH, SEQ, H, DV)
    co = r["co_out"].reshape(DEPTH, 2, H, P, DV + 1)
    so = r["so_out"].reshape(DEPTH, 2, 2, 2, 64, P).transpose(0, 2, 1, 3, 4, 5).reshape(DEPTH, 2, H, 64, P)
    out = (y[:SEQ], y[SEQ:], ko, vo, co[..., :DV], co[..., DV], r["mo_out"].reshape(DEPTH, 2, H), so)
    return tuple(np.ascontiguousarray(v)[None] for v in out)
```

```python
import math
from contextlib import ExitStack

import concourse.bass as bass
from concourse import mybir

F32 = mybir.dt.float32
ACT = mybir.ActivationFunctionType
ALU = mybir.AluOpType
AX = mybir.AxisListType

P = 128
D = 1024
DEPTH = 2
SEQ = 128
DEC = 256
T = SEQ + DEC
NT = T // P
KD = D // P
W = 512
H = 4
DK_M, DQK, DK_G, DV = 128, 64, 64, 128
CW = 31
PAD = CW // 2
UPAD = PAD + SEQ + PAD + DEC + PAD
NG, EPG, DE = 4, 4, 512
NE = NG * EPG
EPS = 1e-6
LEVELS = 7
SUB = 32
NLEV = 6
M_SCALE = DK_M ** -0.5
D_SCALE = DQK ** -0.5
G_SCALE = DK_G ** -0.5
MASKED = -1e30

GR, GQK, CB, CA, DQ, DKK, MO, MQ, MK = range(9)
NCH = 9
EARLY = 7
LATE = 11
NTOK = 3
NMOD = 12
RING = 3

PAR = {}
_c = 0
for _n, _w in (("norm1", KD), ("norm2", KD), ("bmod", 6 * KD), ("taps", 4 * CW), ("ln_g", 4), ("ln_b", 4),
               ("hn_m", 4), ("hn_d", 4), ("hn_g", 4), ("lam", 4), ("b_i", 1), ("b_f", 1), ("m0", 1),
               ("router", KD * 20), ("w_up", 512),
               ("S0", 2 * 2 * P), ("C0", 2 * H * (DV + 1)), ("k_cache", H * P), ("v_cache", H * P)):
    PAR[_n] = (_c, _c + _w)
    _c += _w
NPAR = _c
NEARLY = KD * (P + 32)

CST = {}
_c = 0
for _n, _w in (("ident", P), ("swap", P), ("cos", DEC), ("sin", DEC), ("tri_f", P), ("tri_b", P), ("ones", P),
               ("neg_f", P), ("neg_b", P), ("lev_f", NLEV * SUB), ("lev_b", NLEV * SUB), ("sixteenth", P), ("slots", P), ("zero", 1), ("final", KD),
               ("lam_init", DEPTH), ("one_less", DEPTH), ("order", NG), ("cond", KD * 2)):
    CST[_n] = (_c, _c + _w)
    _c += _w
NCST = _c


def tok(t):
    return slice(t * P, (t + 1) * P)


CTX, LAT = slice(0, SEQ), slice(SEQ, T)


class Signal:

    def __init__(self, sem, per_layer, credit=0):
        self.sem, self.per_layer, self.credit = sem, per_layer, credit

    def at(self, layer, k):
        return layer * self.per_layer + (k + self.credit)


class Chain:

    def __init__(self, engine, sem, per_layer):
        self.engine, self.sem, self.per_layer, self.n = engine, sem, per_layer, 0
        self.layer = 0

    def step(self, instruction):
        instruction.then_inc(self.sem, 1)
        self.n += 1

    def settle(self, but=0):
        self.engine.wait_ge(self.sem, self.layer * self.per_layer + (self.n - but))


ACT_STEPS, DVE_STEPS = 45, 499


def hybrid_step(nc, par_d, early_d, cst_d, x_d, wmod_d, wch_d, wtok_d, wgate_d, wbr_d, wout_d, we13_d, we2_d,
                y_d, ko_d, vo_d, co_d, mo_d, so_d):
    nc.disable_value_cache = True
    with ExitStack() as ctx:
        def sb(name, shape):
            return ctx.enter_context(nc.sbuf_tensor(name, shape, F32))

        def sig(name, per_layer, credit=0):
            return Signal(ctx.enter_context(nc.semaphore(name)), per_layer, credit)

        psum = [ctx.enter_context(nc.psum_tensor(f"psum{i}", [P, 1024], F32)) for i in range(4)]

        def bank(b):
            return psum[b // 2][:, (b % 2) * 512:(b % 2) * 512 + 512]

        xT = sb("xT", [P, KD, T])
        hT = sb("hT", [P, KD, T])
        ring = [sb(f"ring{i}", [P, 4096]) for i in range(RING)]
        pc_flat = sb("pc", [P, NCH * 4 * T])
        pc = pc_flat[:, :].rearrange("p (s c t) -> p s c t", s=NCH, c=4)
        ring = [r[:, :] for r in ring]
        ring += [pc_flat[:, i * 4096:(i + 1) * 4096] for i in range(3)]
        merged = pc_flat[:, MQ * 4 * T:(MQ + 2) * 4 * T].rearrange("p (k t) -> p k t", k=KD)
        mva = sb("mva", [P, NT, H, DV + 1])
        dv = sb("dv", [P, NT, W])
        gv = sb("gv", [P, NT, W])
        par = sb("par", [P, NPAR])
        cst = sb("cst", [P, NCST])
        scr = sb("scr", [P, 2 * 4 * T])
        scrA, scrB = scr[:, 0:4 * T], scr[:, 4 * T:8 * T]
        mod_rows = scr[0:2, 0:RING * W]
        upad = scr[:, 0:4 * UPAD].rearrange("p (c t) -> p c t", c=4)
        ytok = sb("ytok", [P, NT, W])
        mod = sb("mod", [P, 6 * KD, 2])
        amp = sb("amp", [P, 2, KD, 2])
        rstd = sb("rstd", [P, T])
        gaT = sb("gaT", [P, T])
        cols = sb("cols", [P, 10, 36])
        small = sb("small", [P, 64])
        eps = sb("eps", [P, 1])
        rt = sb("rt", [P, 160])
        rw = sb("rw", [P, NT, NE + 1])
        rk = sb("rk", [P, NT, NE + 1])
        sel = sb("sel", [P, NT, NE])
        spill = ctx.enter_context(nc.sbuf_tensor("spill", [1, 1], mybir.dt.int32))
        wT = ytok[0:NE, 1, 0:T]
        wm = ytok[0:NE, 2, 0:T]

        def pp(name, a=None, b=None):
            lo, hi = PAR[name]
            return par[:, lo + (a or 0):(lo + b if b is not None else hi)]

        def cc(name, a=None, b=None):
            lo, hi = CST[name]
            return cst[:, lo + (a or 0):(lo + b if b is not None else hi)]

        ident, ones = cc("ident"), cc("ones")
        early = ytok[:, :, :].rearrange("p t n -> p (t n)")[:, 0:NEARLY]
        w_rows = early[:, 0:KD * P].rearrange("p (k n) -> p k n", k=KD)
        w_ga = early[:, KD * P:NEARLY].rearrange("p (k n) -> p k n", k=KD)
        w_router = pp("router").rearrange("p (k n) -> p k n", k=KD)
        w_up = pp("w_up")[0:33]
        S0 = pp("S0").rearrange("p (d a n) -> p d a n", d=2, a=2)
        C0 = pp("C0").rearrange("p (d h n) -> p d h n", d=2, h=H)
        k_cache = pp("k_cache").rearrange("p (h n) -> p h n", h=H)
        v_cache = pp("v_cache").rearrange("p (h n) -> p h n", h=H)
        taps = pp("taps").rearrange("p (c j) -> p c j", c=4)
        bmod = pp("bmod")
        cond = cc("cond").rearrange("p (k c) -> p k c", k=KD)
        lev = [cc("lev_f"), cc("lev_b")]
        tri = [cc("tri_f"), cc("tri_b")]
        neg = [cc("neg_f"), cc("neg_b")]

        rows = sb("rows", [64, 5, T])
        R_I, R_F, R_T, R_B, R_NG = range(5)
        R_U, R_EM, R_A = R_I, R_F, R_B

        m_exp = [scrA[:, i * 512:(i + 1) * 512] for i in range(2)]
        m_s = [scrB[:, i * 512:(i + 1) * 512] for i in range(2)]
        free = CB * 4 * T
        m_x = pc_flat[:, free:free + 4 * (DV + 1)].rearrange("p (a n) -> p a n", a=2)
        m_nd = pc_flat[:, free + 516:free + 516 + 3 * (DV + 1)].rearrange("p (a n) -> p a n", a=3)
        kstate = pc_flat[:, free + 904:free + 1032]
        st_out = pc_flat[:, free + 1032:free + 1032 + DV + 1]
        cmean = scrB[:, 0:T]
        mktok = scrB[:, 1024:1536].rearrange("p (h n) -> p h n", h=H)

        la = scrA.rearrange("p (t n) -> p t n", t=NT)
        gT = mva[:, :, :, :].rearrange("p t h n -> p (t h n)")[:, 0:4 * T].rearrange("p (u t) -> p u t", u=4)
        zA = pc_flat[:, MQ * 4 * T:MQ * 4 * T + LEVELS * T].rearrange("p (l t) -> p l t", l=LEVELS)
        zB = pc_flat[:, CB * 4 * T:CB * 4 * T + 4 * T].rearrange("p (l t) -> p l t", l=4)
        zC = scrB[:, 0:3 * T].rearrange("p (l t) -> p l t", l=3)
        g_z = [[(range(7), zA)], [(range(4), zB), (range(4, 7), zC)]]
        g_zl = [[zA[:, lv, :] for lv in range(7)],
                [zB[:, lv, :] if lv < 4 else zC[:, lv - 4, :] for lv in range(7)]]
        g_ca = pc_flat[:, MQ * 4 * T + LEVELS * T:MQ * 4 * T + LEVELS * T + 2 * P]
        dv_flat = dv[:, :, :].rearrange("p t n -> p (t n)")
        g_m = dv_flat[:, 0:6 * NLEV * SUB]
        g_c = dv_flat[:, 6 * NLEV * SUB:6 * NLEV * SUB + 6 * SUB].rearrange("p (x t) -> p x t", x=6)
        g_att = [pc_flat[:, DKK * 4 * T + d * 6 * P:DKK * 4 * T + (d + 1) * 6 * P].rearrange("p (x t) -> p x t", x=6)
                 for d in range(2)]
        g_kd = scrA[:, 0:128]
        g_kt = scrA[:, 128:256]
        g_xx = scrA[:, 256:512]
        g_qx = scrA[:, 512:640]
        g_kx = scrA[:, 640:768]
        g_qs = [scrA[:, 768:1024], scrA[:, 1152:1408]]
        g_so = scrA[:, 1024:1152]

        d_p = [scr[:, i * 768:i * 768 + 768].rearrange("p (c t) -> p c t", c=2) for i in range(2)]
        d_w = scr[:, 1536:1920]
        d_wt = scr[:, 1920:2304]

        x_h = scr[:, 0:1024].rearrange("p (k n) -> p k n", k=KD)
        x_y = scr[:, 1024:2048]
        x_s, x_g = scr[:, 2048:2560], scr[:, 2560:3072]
        yflat = ytok[:, :, :].rearrange("p t n -> p (t n)")
        x_gT = yflat[:, 0:512]
        x_p = yflat[:, 512:896].rearrange("p (t n) -> p t n", t=NT)
        x_pw = yflat[:, 896:1280].rearrange("p (t n) -> p t n", t=NT)
        x_pT = [pc_flat[:, 12288 + i * T:12288 + (i + 1) * T] for i in range(2)]
        htok = [dv, gv]
        wb = ytok[:, 0, 0:T]
        e_t = scrA.rearrange("p (a t) -> p a t", a=4)
        gu = scrB.rearrange("p (a t) -> p a t", a=4)

        loaded = sig("constants_loaded", 0)
        setup_s = sig("setup_step", 0)
        params_in = sig("params_in", 32)
        params_free = sig("params_free", 1, 1)
        slot_in = [sig(f"slot{i}_in", n * 16) for i, n in enumerate((21, 21, 20, 8, 8, 8))]
        FILLS_MIX = (13, 13, 12, 0, 0, 0)
        mod_done = sig("mod_done", NMOD)
        mod_row = sig("mod_row", NMOD)
        mod_turned = sig("mod_turned", NMOD // RING)
        mod_used = sig("mod_used", NMOD // RING, 1)
        merge_x = sig("merge_product", 32)
        x_ready = sig("x_ready", 2, 1)
        squares_ready = sig("squares_ready", 2)
        sumsq_done = sig("sumsq_done", 2)
        rstd_ready = sig("rstd_ready", 2)
        xn_ready = sig("xn_ready", 16)
        h_ready = sig("h_ready", 2)
        small_done = sig("small_done", 2)
        ch_done = sig("ch_done", 36)
        ch_copied = sig("ch_copied", 36, 2)
        tok_done = sig("tok_done", 9)
        tok_copied = sig("tok_copied", 9, 2)
        cb_sig = sig("cb_sig", 1)
        rows_ready = sig("rows_ready", 1)
        rows_exp = sig("rows_exp", 1)
        cols_done = sig("cols_done", 1)
        cols_ready = sig("cols_ready", 1)
        kt_done = sig("kt_done", 1)
        kt_ready = sig("kt_ready", 1)
        bc_done = sig("bc_done", 8)
        qk_done = sig("qk_done", 8)
        mexp_ready = sig("mexp_ready", 8)
        s_ready = sig("s_ready", 8)
        pv_done = sig("pv_done", 8)
        inter_ready = sig("inter_ready", 8)
        m_out = sig("m_out", 8)
        kw_ready = sig("kw_ready", 8)
        st_done = sig("st_done", 8)
        st_copied = sig("st_copied", 8)
        outs = sig("dram_written", (2 + 8 + 2 + 8) * 16)
        fin_sq = sig("fin_sq", 3)
        fin_rs = sig("fin_rs", 3)
        fin_n = sig("fin_n", 3)
        fin_t = sig("fin_t", 3)
        fin_sigm = sig("fin_sig", 2)
        fin_done = sig("fin_done", 3)
        rot_done = sig("rot_done", 8)
        rot_used = sig("rot_used", 8)
        sc_done = sig("sc_done", 24)
        negmax = sig("negmax", 24)
        p_ready = sig("p_ready", 24)
        dw_ready = sig("dw_ready", 12)
        dwt_done = sig("dwt_done", 12)
        dwt_ready = sig("dwt_ready", 12)
        dpv_done = sig("dpv_done", 12)
        dpv_copied = sig("dpv_copied", 12)
        lamp_ready = sig("lamp_ready", 1)
        lams_done = sig("lams_done", 1)
        lame_ready = sig("lame_ready", 1)
        ga_ready = sig("ga_ready", 1)
        la_done = sig("la_done", 1)
        la_exp = sig("la_exp", 1)
        la_ready = sig("la_ready", 1)
        g_done = sig("g_done", 4)
        g_ready = sig("g_ready", 4)
        gd_ready = sig("gla_differences", 4)
        gx_ready = sig("gla_factors", 4)
        gz_ready = sig("gla_scaled_q_k", 4)
        ga_asked = sig("gla_scores_asked", 8)
        ga_done = sig("gla_scores_done", 8)
        gm_ready = sig("gla_masked", 16)
        gsum_ready = sig("gla_level_sums", 4)
        g64_copied = sig("gla_64_copied", 4)
        g32_copied = sig("gla_32_copied", 4)
        gatt_ready = sig("gla_scores_ready", 4)
        gcd_ready = sig("gcd_ready", 4)
        gcx_ready = sig("gcx_ready", 4)
        gcq_ready = sig("gcq_ready", 4)
        gc_done = sig("gla_cross_done", 8)
        gc_copied = sig("gc_copied", 4)
        go_done = sig("gla_o_done", 8)
        gs_t = sig("gla_state_t", 4)
        gs_tc = sig("gla_state_tc", 4)
        gs_done = sig("gla_state_done", 4)
        gs_copied = sig("gla_state_copied", 8)
        go_copied = sig("gla_o_copied", 4)
        conv_acc = sig("conv_acc", 1)
        conv_sum = sig("conv_sum", 2)
        conv_mean = sig("conv_mean", 1)
        conv_sq = sig("conv_sq", 1)
        conv_rs = sig("conv_rs", 1)
        conv_n = sig("conv_n", 1)
        conv_done = sig("conv_done", 1)
        gate_done = sig("gate_done", 32)
        br_done = sig("br_done", 32)
        gate_sig = sig("gate_sig", 32, 2)
        merged_s = sig("merged", 32, 2)
        out_done = sig("out_done", 8)
        out_used = sig("out_used", 8, 2)
        rt_done = sig("router_done", 1)
        rt_ready = sig("router_ready", 1)
        rt_exp = sig("router_exp", 6)
        rt_step = sig("router_dve", 6)
        sel_ready = sig("sel_ready", 1)
        rank_done = sig("rank_done", 1)
        rank_ready = sig("rank_ready", 1)
        ht_done = sig("ht_done", 6, 2)
        ht_copied = sig("ht_copied", 6, 2)
        p_built = sig("slots_built", NE + 1)
        xh_done = sig("gathered", NE + 1)
        xh_ready = sig("gathered_ready", NE + 1)
        pt_done = sig("slots_turned", NE + 1)
        pt_ready = sig("slots_turned_ready", NE + 1)
        xab_done = sig("hidden_done", NE)
        xs_ready = sig("silu_ready", NE)
        xg_ready = sig("hidden_ready", NE)
        xgt_done = sig("hidden_turned", NE)
        xgt_ready = sig("hidden_turned_ready", NE)
        xy_done = sig("expert_out_done", 2 * NE)
        xy_ready = sig("expert_out_ready", 2 * NE)
        back_done = sig("scattered", NE * KD)
        back_used = sig("scattered_used", NE * KD, 2)
        spill_known = sig("spill_known", 1)
        spill_asked = sig("spill_asked", 4)
        sp_slot = [sig(f"spill_slot{i}_in", 8 * 16) for i in range(6)]
        sp_free = sig("spill_weights_may_load", 1)
        sp_rw = sig("spill_weights", 1)
        rtt_done = sig("router_t", 1)
        wT_ready = sig("wT_ready", 1)
        wm_ready = sig("wm_ready", NE + 1)
        wb_done = sig("wb_done", 16)
        wb_ready = sig("wb_ready", 16)
        ab_done = sig("ab_done", 64)
        a_exp = sig("a_silu", 64)
        gu_ready = sig("gu_ready", 64, 4)
        y_done = sig("y_done", 128)
        y_used = sig("y_used", 128, 2)
        e_x = sig("spill_product", 64)
        act_chain = ctx.enter_context(nc.semaphore("act_step"))
        dve_chain = ctx.enter_context(nc.semaphore("dve_step"))
        final_s = sig("final", 0)

        block = ctx.enter_context(nc.Block())

        def bflip(d, t):
            return 32 * d + t

        @block.sync
        def _(sp):
            sp.dma_start(cst[:, :], cst_d).then_inc(loaded.sem, 16)
            sp.dma_start(xT[:, :, :], x_d).then_inc(loaded.sem, 16)

            def fill(slot, src, l, k):
                sp.dma_start(ring[slot], src).then_inc(slot_in[slot].sem, 16)

            def rearr(a):
                return a.rearrange("a p n -> (a p) n")

            with sp.Fori(0, DEPTH) as l:
                sp.wait_ge(params_free.sem, params_free.at(l, 0))
                sp.dma_start(par[:, :], rearr(par_d[bass.ds(l, 1)])).then_inc(params_in.sem, 16)
                sp.dma_start(early, rearr(early_d[bass.ds(l, 1)])).then_inc(params_in.sem, 16)
                for j in range(RING):
                    fill(j, rearr(wmod_d[bass.ds(l * NMOD + j, 1)]), l, 0)
                with sp.Fori(1, NMOD // RING) as i:
                    for j in range(RING):
                        sp.wait_ge(mod_done.sem, l * NMOD + i * RING + (j - RING + 1))
                        fill(j, rearr(wmod_d[bass.ds(l * NMOD + i * RING + j, 1)]), l, 0)
                for b in range(EARLY):
                    j = b % RING
                    if b < RING:
                        sp.wait_ge(mod_done.sem, mod_done.at(l, NMOD - RING + j + 1))
                    else:
                        sp.wait_ge(ch_done.sem, ch_done.at(l, 4 * (b - RING + 1)))
                    fill(j, rearr(wch_d[bass.ds(l * NCH + b, 1)]), l, 0)
                for j in range(2):
                    sp.wait_ge(ch_done.sem, ch_done.at(l, 20 + 4 * j))
                    fill(1 + j, rearr(wtok_d[bass.ds(l * NTOK + j, 1)]), l, 0)
                sp.wait_ge(ch_done.sem, ch_done.at(l, 28))
                fill(0, rearr(wch_d[bass.ds(l * NCH + EARLY, 1)]), l, 0)
                sp.wait_ge(tok_done.sem, tok_done.at(l, 3))
                fill(1, rearr(wch_d[bass.ds(l * NCH + EARLY + 1, 1)]), l, 0)
                sp.wait_ge(tok_done.sem, tok_done.at(l, 6))
                fill(2, rearr(wtok_d[bass.ds(l * NTOK + 2, 1)]), l, 0)
                def merge_fill(i, j):
                    if j < 2:
                        fill(j, rearr(wgate_d[bass.ds(l * 8 + i * 2 + j, 1)]), l, 0)
                    else:
                        fill(j, rearr(wbr_d[bass.ds(l * 4 + i, 1)]), l, 0)
                sp.wait_ge(ch_copied.sem, ch_copied.at(l, 28))
                sp.dma_start(ko_d[bass.ds(l, 1)].rearrange("a p h n -> (a p) h n"), pc[:, DKK, :, CTX]).then_inc(outs.sem, 16)
                sp.wait_ge(tok_copied.sem, tok_copied.at(l, 6))
                sp.dma_start(rearr(vo_d[bass.ds(l, 1)]), dv[:, 0, :]).then_inc(outs.sem, 16)
                sp.wait_ge(rows_ready.sem, rows_ready.at(l, 1))
                for d in range(2):
                    sp.dma_start(mo_d[bass.ds(l * 2 + d, 1)].rearrange("a h n -> (a h) n"),
                                 small[32 * d:32 * d + 4, 60:61]).then_inc(outs.sem, 16)
                for n in range(8):
                    sp.wait_ge(st_copied.sem, st_copied.at(l, n + 1))
                    sp.dma_start(rearr(co_d[bass.ds(l * 8 + n, 1)]), st_out).then_inc(outs.sem, 16)
                for j, (done, k) in enumerate(((ch_done, 32), (ch_done, 36), (tok_done, 9))):
                    sp.wait_ge(done.sem, done.at(l, k))
                    merge_fill(0, j)
                for n in range(8):
                    sp.wait_ge(gs_copied.sem, gs_copied.at(l, n + 1))
                    sp.dma_start(rearr(so_d[bass.ds(l * 8 + n, 1)]),
                                 g_so[(n % 2) * 64:(n % 2) * 64 + 64, :]).then_inc(outs.sem, 16)
                with sp.Fori(1, 4) as i:
                    for j in range(2):
                        sp.wait_ge(gate_done.sem, l * 32 + i * 8 + (4 * (j + 1) - 8))
                        merge_fill(i, j)
                    sp.wait_ge(br_done.sem, l * 32 + i * 8)
                    merge_fill(i, 2)
                for j in range(2):
                    sp.wait_ge(gate_done.sem, gate_done.at(l, 28 + 4 * j))
                    fill(j, rearr(wout_d[bass.ds(l * 2 + j, 1)]), l, 0)
                def expert_fill(e, par_, j):
                    src = we13_d[bass.ds(l * 32 + e * 2 + j, 1)] if j < 2 else we2_d[bass.ds(l * 16 + e, 1)]
                    fill(3 * par_ + j, rearr(src), l, 0)
                sp.wait_ge(out_done.sem, out_done.at(l, 8))
                for p in range(2):
                    for j in range(3):
                        expert_fill(p, p, j)
                with sp.Fori(1, NE // 2) as i:
                    for p in range(2):
                        sp.wait_ge(xab_done.sem, l * NE + i * 2 + (p - 1))
                        expert_fill(i * 2 + p, p, 0)
                        expert_fill(i * 2 + p, p, 1)
                        sp.wait_ge(xy_done.sem, l * 2 * NE + i * 4 + (2 * p - 2))
                        expert_fill(i * 2 + p, p, 2)
                sp.wait_ge(spill_known.sem, spill_known.at(l, 1))
                sp.sem_inc(spill_asked.sem, 1)
                spilled = sp.value_load(spill[0:1, 0:1], min_val=0, max_val=1)
                with sp.If(spilled > 0):
                    def spill_fill(e, p, j):
                        src = we13_d[bass.ds(l * 32 + e * 2 + j, 1)] if j < 2 else we2_d[bass.ds(l * 16 + e, 1)]
                        sp.dma_start(ring[3 * p + j], rearr(src)).then_inc(sp_slot[3 * p + j].sem, 16)
                    sp.wait_ge(sp_free.sem, sp_free.at(l, 1))
                    for p in range(2):
                        for j in range(3):
                            spill_fill(p, p, j)
                    with sp.Fori(1, NE // 2) as i:
                        for p in range(2):
                            sp.wait_ge(ab_done.sem, l * 64 + i * 8 + (4 * p + 4 - 8))
                            spill_fill(i * 2 + p, p, 0)
                            spill_fill(i * 2 + p, p, 1)
                            sp.wait_ge(y_done.sem, l * 128 + i * 16 + (8 * p + 8 - 16))
                            spill_fill(i * 2 + p, p, 2)
                with sp.Else():
                    for s in sp_slot:
                        sp.sem_inc(s.sem, s.per_layer)
            sp.wait_ge(final_s.sem, 4)
            sp.dma_start(y_d, hT[:, :, :]).then_inc(outs.sem, 16)
            sp.wait_ge(outs.sem, DEPTH * outs.per_layer + 16)

        @block.tensor
        def _(pe):
            pe.wait_ge(loaded.sem, 32)

            def sum_squares():
                for k in range(KD):
                    mm = pe.matmul(bank(0)[:, 0:T], ones, hT[:, k, :], start=k == 0, stop=k == KD - 1)
                mm.then_inc(sumsq_done.sem, 1)

            def finish_transposes(l, b):
                pe.wait_ge(fin_n.sem, fin_n.at(l, b + 1))
                for h in range(H):
                    for t in range(NT):
                        mm = pe.transpose(bank(h)[:, tok(t)], ytok[:, t, h * P:(h + 1) * P], ident)
                mm.then_inc(fin_t.sem, 1)

            with pe.Fori(0, DEPTH) as l:
                pe.wait_ge(setup_s.sem, 7)
                with pe.Fori(0, NMOD // RING) as i:
                    for j in range(RING):
                        pe.wait_ge(slot_in[j].sem, (l * slot_in[j].per_layer + i * 16) + 16)
                        wv = ring[j].rearrange("p (k n) -> p k n", k=KD)
                        for k in range(KD):
                            mm = pe.matmul(bank(5 + j)[0:2, :], cond[:, k, :], wv[:, k, :],
                                           start=k == 0, stop=k == KD - 1)
                        mm.then_inc(mod_done.sem, 1)
                    pe.wait_ge(mod_row.sem, l * NMOD + i * RING + RING)
                    pe.wait_ge(mod_used.sem, l * (NMOD // RING) + i + 1)
                    for n in range(4 * RING):
                        mm = pe.matmul(bank(4)[:, 2 * n:2 * n + 2], mod_rows[:, n * P:(n + 1) * P], ident[0:2, 0:2],
                                       start=True, stop=True, skip_group_check=True)
                    mm.then_inc(mod_turned.sem, 1)
                pe.wait_ge(squares_ready.sem, squares_ready.at(l, 1))
                sum_squares()

                pe.wait_ge(h_ready.sem, h_ready.at(l, 1))
                for k in range(KD):
                    mm = pe.matmul(bank(4)[:, 0:T], w_rows[:, k, :], hT[:, k, :], start=k == 0, stop=k == KD - 1)
                mm.then_inc(small_done.sem, 1)
                for k in range(KD):
                    mm = pe.matmul(bank(5)[0:32, 0:T], w_ga[:, k, :], hT[:, k, :], start=k == 0, stop=k == KD - 1)
                mm.then_inc(small_done.sem, 1)

                def ch_block(i, j):
                    pe.wait_ge(slot_in[j].sem, l * slot_in[j].per_layer + i * 16 + (4 * 16 + 16))
                    wv = ring[j].rearrange("p (k n) -> p k n", k=KD)
                    for n in range(4):
                        g = j * 4 + n
                        pe.wait_ge(ch_copied.sem, l * 36 + i * 12 + (g + 1))
                        for k in range(KD):
                            mm = pe.matmul(bank(g % 2)[:, 0:T], wv[:, k, n * P:(n + 1) * P], hT[:, k, :],
                                           start=k == 0, stop=k == KD - 1)
                        mm.then_inc(ch_done.sem, 1)

                with pe.Fori(0, EARLY // RING) as i:
                    for j in range(RING):
                        ch_block(i, j)
                ch_block(EARLY // RING, 0)
                for j in range(2):
                    pe.wait_ge(slot_in[1 + j].sem, slot_in[1 + j].at(l, 6 * 16 + 16))
                    wv = ring[1 + j].rearrange("p (k n) -> p k n", k=KD)
                    for t in range(NT):
                        g = j * 3 + t
                        pe.wait_ge(tok_copied.sem, tok_copied.at(l, g - 1))
                        for k in range(KD):
                            mm = pe.matmul(bank(2 + g % 2), hT[:, k, tok(t)], wv[:, k, :],
                                           start=k == 0, stop=k == KD - 1)
                        mm.then_inc(tok_done.sem, 1)

                def late(g, halves=(0, 1)):
                    j, n = g // 4, g % 4
                    if n == 0 and 0 in halves:
                        pe.wait_ge(slot_in[j].sem, slot_in[j].at(l, 7 * 16 + 16))
                    if 0 not in halves:
                        pass
                    elif g >= 10:
                        pe.wait_ge(tok_copied.sem, tok_copied.at(l, 7))
                    elif g >= 2:
                        pe.wait_ge(ch_copied.sem, ch_copied.at(l, 28 + g - 1))
                    wv = ring[j].rearrange("p (k n) -> p k n", k=KD)
                    for k in range(4 * halves[0], 4 * halves[-1] + 4):
                        if j < 2:
                            mm = pe.matmul(bank(6 + g % 2)[:, 0:T], wv[:, k, n * P:(n + 1) * P], hT[:, k, :],
                                           start=k == 0, stop=k == KD - 1)
                        else:
                            mm = pe.matmul(bank(6 + g % 2), hT[:, k, tok(n)], wv[:, k, :],
                                           start=k == 0, stop=k == KD - 1)
                    if 1 in halves:
                        mm.then_inc((ch_done if j < 2 else tok_done).sem, 1)

                pe.wait_ge(lamp_ready.sem, lamp_ready.at(l, 1))
                pe.matmul(bank(7)[:, 256:258], ones[0:64, :], small[0:64, 40:42], start=True, stop=True)\
                  .then_inc(lams_done.sem, 1)

                pe.wait_ge(rows_exp.sem, rows_exp.at(l, 1))
                pe.wait_ge(ch_copied.sem, ch_copied.at(l, 28))
                for h in range(H):
                    mm = pe.transpose(bank(5)[:, h * P:(h + 1) * P], pc[:, MK, h, CTX], ident)
                mm.then_inc(kt_done.sem, 1)
                for q, r in enumerate((R_U, R_A, R_EM)):
                    for t in range(NT):
                        pe.transpose(bank(4)[:, (q * 3 + t) * 36:(q * 3 + t) * 36 + 36],
                                     rows[0:36, r, tok(t)], ident[0:36, 0:36])
                pe.transpose(bank(4)[:, 324:360], rows[0:36, R_T, CTX], ident[0:36, 0:36])\
                  .then_inc(cols_done.sem, 1)
                pe.wait_ge(cols_ready.sem, cols_ready.at(l, 1))
                pe.wait_ge(kt_ready.sem, kt_ready.at(l, 1))
                pe.wait_ge(tok_copied.sem, tok_copied.at(l, 6))

                def m_front(i):
                    d, h = divmod(i, H)
                    E, Q = bank(i % 2), bank(2 + i % 2)
                    q, k = pc[:, MQ, h, :], pc[:, MK, h, :]
                    r = bflip(d, h)
                    sel = ident[0:36, r:r + 1].to_broadcast([36, P])
                    if i >= 2:
                        pe.wait_ge(s_ready.sem, s_ready.at(l, i - 1))
                    off_s, off_t = (1, 2) if d == 0 else (2, 1)
                    ng = rows[0:36, R_NG, :]
                    pe.matmul(E[:, 0:T], sel, ng, start=True, stop=False)
                    pe.matmul(E[:, 0:T], ident, neg[d].rearrange("p (a t) -> p a t", a=1).to_broadcast([P, NT, P]),
                              start=False, stop=True)
                    pe.matmul(E[:, T:512], sel, ng[:, tok(off_t)], start=True, stop=True, skip_group_check=True)\
                      .then_inc(bc_done.sem, 1)
                    for n, (s, t) in enumerate(((0, 0), (1, 1), (2, 2), (off_s, off_t))):
                        mm = pe.matmul(Q[:, n * P:(n + 1) * P], k[:, tok(s)], q[:, tok(t)], start=True, stop=True,
                                       skip_group_check=True)
                    mm.then_inc(qk_done.sem, 1)

                def m_back(i):
                    d, h = divmod(i, H)
                    V, I = bank(4 + i % 2), bank(6 + i % 2)
                    S = m_s[i % 2]
                    N = DV + 1
                    pe.wait_ge(s_ready.sem, s_ready.at(l, i + 1))
                    if i >= 2:
                        pe.wait_ge(m_out.sem, m_out.at(l, i - 1))
                    off_s, off_t = (1, 2) if d == 0 else (2, 1)
                    for t in range(NT):
                        two = t == off_t
                        pe.matmul(V[:, t * N:(t + 1) * N], S[:, tok(t)], mva[:, t, h, :], start=True, stop=not two,
                                  skip_group_check=True)
                        if two:
                            pe.matmul(V[:, t * N:(t + 1) * N], S[:, T:512], mva[:, off_s, h, :],
                                      start=False, stop=True, skip_group_check=True)
                    for t in (1, 2):
                        mm = pe.matmul(I[:, (t - 1) * N:t * N], pc[:, MQ, h, tok(t)], C0[:, d, h, :],
                                       start=True, stop=True, skip_group_check=True)
                    mm.then_inc(pv_done.sem, 1)

                for i in range(8):
                    m_front(i)
                    if i >= 1:
                        m_back(i - 1)
                m_back(7)
                for i in range(8):
                    d, h = divmod(i, H)
                    pe.wait_ge(kw_ready.sem, kw_ready.at(l, i + 1))
                    if i >= 1:
                        pe.wait_ge(st_copied.sem, st_copied.at(l, i))
                    pe.matmul(bank(0)[:, 0:DV + 1], kstate, mva[:, 0, h, :], start=True, stop=True)\
                      .then_inc(st_done.sem, 1)
                    if i == 0:
                        pe.wait_ge(conv_acc.sem, conv_acc.at(l, 1))
                        for c in range(4):
                            mm = pe.matmul(bank(1)[:, 0:T], ones, pc[:, CA, c, :], start=c == 0, stop=c == 3)
                        mm.then_inc(conv_sum.sem, 1)
                        pe.wait_ge(inter_ready.sem, inter_ready.at(l, 8))
                    if i == 2:
                        pe.wait_ge(conv_sq.sem, conv_sq.at(l, 1))
                        for c in range(4):
                            mm = pe.matmul(bank(2)[:, 0:T], ones, e_t[:, c, :], start=c == 0, stop=c == 3)
                        mm.then_inc(conv_sum.sem, 1)
                    if i % 2:
                        late(i // 2)
                pe.wait_ge(conv_rs.sem, conv_rs.at(l, 1))
                finish_transposes(l, 0)

                pe.wait_ge(ga_ready.sem, ga_ready.at(l, 1))
                pe.wait_ge(ch_copied.sem, ch_copied.at(l, 31))
                for t in range(NT):
                    mm = pe.matmul(bank(4 + t), gaT[0:33, tok(t)], w_up, start=True, stop=True)
                mm.then_inc(la_done.sem, 1)

                pe.wait_ge(fin_done.sem, fin_done.at(l, 1))
                for n in range(8):
                    slot, h = (DQ, DKK)[n // 4], n % 4
                    if n >= 2:
                        pe.wait_ge(rot_used.sem, rot_used.at(l, n - 1))
                    pe.matmul(bank(n % 2)[:, 0:DEC], cc("swap"), pc[:, slot, h, LAT], start=True, stop=True)\
                      .then_inc(rot_done.sem, 1)
                pe.wait_ge(rot_used.sem, rot_used.at(l, 8))
                pe.wait_ge(la_ready.sem, la_ready.at(l, 1))
                for u in range(4):
                    pair, d = divmod(u, 2)
                    if u >= 2:
                        pe.wait_ge(g_ready.sem, g_ready.at(l, u - 1))
                    B = bank(u % 2)
                    lc = slice(d * 256 + pair * P, d * 256 + pair * P + P)
                    near, far = (1, 2) if d == 0 else (2, 1)
                    pe.matmul(B[:, CTX], la[:, 0, lc], tri[d], start=True, stop=True)
                    pe.matmul(B[:, tok(near)], la[:, near, lc], tri[d], start=True, stop=True, skip_group_check=True)
                    pe.matmul(B[:, tok(far)], la[:, near, lc], cc("sixteenth"), start=True, stop=False, skip_group_check=True)
                    pe.matmul(B[:, tok(far)], la[:, far, lc], tri[d], start=False, stop=True, skip_group_check=True)\
                      .then_inc(g_done.sem, 1)
                late(4)
                pe.wait_ge(g_ready.sem, g_ready.at(l, 4))

                def d_scores(u):
                    h, t, c = u // 6, (u // 2) % 3, u % 2
                    if u >= 2:
                        pe.wait_ge(p_ready.sem, p_ready.at(l, u - 1))
                    B = bank(u % 2)
                    half = slice(64 * c, 64 * c + 64)
                    q = pc[half, DQ, h, tok(t)]
                    if t == 0:
                        mm = pe.matmul(B[:, 0:P], q, pc[half, DKK, h, CTX], start=True, stop=True)
                    else:
                        pe.matmul(B[:, 0:DEC], q, pc[half, DKK, h, LAT], start=True, stop=True)
                        mm = pe.matmul(B[:, DEC:T], q, k_cache[half, h, :], start=True, stop=True,
                                       skip_group_check=True)
                    mm.then_inc(sc_done.sem, 1)

                def d_out(v):
                    h, t = divmod(v, 3)
                    nk = 1 if t == 0 else 3
                    pe.wait_ge(dw_ready.sem, dw_ready.at(l, v + 1))
                    for s in range(nk):
                        mm = pe.transpose(bank(2)[:, tok(s)], d_w[:, tok(s)], ident)
                    mm.then_inc(dwt_done.sem, 1)
                    pe.wait_ge(dwt_ready.sem, dwt_ready.at(l, v + 1))
                    if v >= 2:
                        pe.wait_ge(dpv_copied.sem, dpv_copied.at(l, v - 1))
                    for s in range(nk):
                        vals = dv[:, 0, h * P:(h + 1) * P] if t == 0 else (
                            dv[:, s + 1, h * P:(h + 1) * P] if s < 2 else v_cache[:, h, :])
                        mm = pe.matmul(bank(4 + v % 2)[:, 0:P], d_wt[:, tok(s)], vals, start=s == 0, stop=s == nk - 1)
                    mm.then_inc(dpv_done.sem, 1)

                for v in range(12):
                    d_scores(2 * v)
                    d_scores(2 * v + 1)
                    late(5 + v // 2, (v % 2,))
                    if v >= 1:
                        d_out(v - 1)
                d_out(11)
                finish_transposes(l, 1)

                def scores(u):
                    pair, d = divmod(u, 2)
                    z = g_zl[u % 2]
                    pe.wait_ge(gz_ready.sem, gz_ready.at(l, u + 1))

                    def diagonal(t, column):
                        for b in range(4):
                            c = slice(t * P + SUB * b, t * P + SUB * b + SUB)
                            for lv in range(NLEV):
                                for hh in range(2):
                                    r = slice(64 * hh, 64 * hh + 64)
                                    if lv < NLEV - 1:
                                        ks, qs = z[lv][r, c], z[lv][r, c]
                                    else:
                                        ks, qs = pc[r, GQK, 2 + pair, c], pc[r, GQK, pair, c]
                                    o = column + lv * SUB
                                    pe.matmul(psum[hh][SUB * b:SUB * b + SUB, o:o + SUB], ks, qs, start=True,
                                              stop=True, skip_group_check=True)

                    def beside(w, column):
                        for t in range(NT):
                            for j in range(P // (2 * w)):
                                s0 = 2 * w * j + (w if d else 0)
                                t0 = 2 * w * j + (0 if d else w)
                                for hh in range(2):
                                    r = slice(64 * hh, 64 * hh + 64)
                                    zw = z[5 if w == 32 else 6]
                                    mm = pe.matmul(psum[hh][s0:s0 + w, column + t * w:column + t * w + w],
                                                   zw[r, t * P + s0:t * P + s0 + w], zw[r, t * P + t0:t * P + t0 + w],
                                                   start=True, stop=True, skip_group_check=True)
                        return mm

                    if u >= 1:
                        pe.wait_ge(g32_copied.sem, g32_copied.at(l, u))
                    pe.sem_inc(ga_asked.sem, 1)
                    diagonal(0, 0)
                    diagonal(1, NLEV * SUB)
                    beside(32, 2 * NLEV * SUB).then_inc(ga_done.sem, 1)
                    if u >= 1:
                        pe.wait_ge(g64_copied.sem, g64_copied.at(l, u))
                    pe.sem_inc(ga_asked.sem, 1)
                    diagonal(2, 512)
                    beside(64, 512 + NLEV * SUB).then_inc(ga_done.sem, 1)

                pe.wait_ge(fin_done.sem, fin_done.at(l, 2))
                pe.wait_ge(tok_copied.sem, tok_copied.at(l, 9))
                scores(0)
                for u in range(4):
                    pair, d = divmod(u, 2)
                    tq, tk = (2, 1) if d == 0 else (1, 2)
                    pe.wait_ge(gcq_ready.sem, gcq_ready.at(l, u + 1))
                    if u >= 1:
                        pe.wait_ge(gc_copied.sem, gc_copied.at(l, u))
                        pe.wait_ge(gs_copied.sem, gs_copied.at(l, 2 * u))
                    for hh in range(2):
                        r = slice(64 * hh, 64 * hh + 64)
                        if hh:
                            pe.wait_ge(gc_done.sem, gc_done.at(l, u * 2 + 1))
                        pe.matmul(bank(6)[:, hh * P:(hh + 1) * P], g_kx[r, :], g_qx[r, :], start=True, stop=True,
                                  skip_group_check=True).then_inc(gc_done.sem, 1)
                    pe.transpose(bank(7)[:, 0:P], g_kd, ident).then_inc(gs_t.sem, 1)
                    if u < 3:
                        scores(u + 1)
                    pe.wait_ge(gs_tc.sem, gs_tc.at(l, u + 1))
                    pe.matmul(bank(7)[:, 0:256], g_kt, gv[:, 0, pair * 256:pair * 256 + 256],
                              start=True, stop=True).then_inc(gs_done.sem, 1)
                    if u == 2:
                        pe.wait_ge(go_copied.sem, go_copied.at(l, 2))
                    pe.wait_ge(gatt_ready.sem, gatt_ready.at(l, u + 1))
                    pe.wait_ge(gc_copied.sem, gc_copied.at(l, u + 1))
                    for hh in range(2):
                        head = pair * 2 + hh
                        r = slice(64 * hh, 64 * hh + 64)
                        for t in range(NT):
                            pe.matmul(bank(4 + hh)[:, tok(t)], g_att[d][:, hh * 3 + t, :], gv[:, t, head * P:(head + 1) * P],
                                      start=(d == 0 and t == 0), stop=False, skip_group_check=True)
                        for t in (1, 2):
                            pe.matmul(bank(4 + hh)[:, tok(t)], g_qs[d][r, tok(t - 1)], S0[r, d, pair, :],
                                      start=False, stop=False, skip_group_check=True)
                        pe.matmul(bank(4 + hh)[:, tok(tq)], g_ca[:, hh * P:(hh + 1) * P], gv[:, tk, head * P:(head + 1) * P],
                                  start=False, stop=d == 1, skip_group_check=True).then_inc(go_done.sem, 1)
                finish_transposes(l, 2)

                with pe.Fori(0, 4) as i:
                    for n in range(8):
                        j = n // 4
                        if n % 4 == 0:
                            pe.wait_ge(slot_in[j].sem, l * slot_in[j].per_layer + i * 16 + (8 * 16 + 16))
                        wv = ring[j].rearrange("p (k n) -> p k n", k=KD)
                        pe.wait_ge(merged_s.sem, l * 32 + i * 8 + (n + 1))
                        for k in range(KD):
                            mm = pe.matmul(bank(4 + n % 2)[:, 0:T], wv[:, k, (n % 4) * P:(n % 4 + 1) * P], hT[:, k, :],
                                           start=k == 0, stop=k == KD - 1)
                        mm.then_inc(gate_done.sem, 1)
                        if n == 0:
                            pe.wait_ge(fin_done.sem, fin_done.at(l, 3))
                            pe.wait_ge(conv_done.sem, conv_done.at(l, 1))
                            pe.wait_ge(slot_in[2].sem, l * slot_in[2].per_layer + i * 16 + (8 * 16 + 16))
                        wb_v = ring[2].rearrange("p (c n) -> p c n", c=4)
                        for c in range(4):
                            mm = pe.matmul(bank(2 + n % 2)[:, 0:T], wb_v[:, c, n * P:(n + 1) * P],
                                           pc_flat[:, bass.ds(i * (2 * 4 * T) + c * T, T)],
                                           start=c == 0, stop=c == 3)
                        mm.then_inc(br_done.sem, 1)
                pe.wait_ge(merged_s.sem, merged_s.at(l, 32))
                for n in range(8):
                    j = n // 4
                    if n % 4 == 0:
                        pe.wait_ge(slot_in[j].sem, slot_in[j].at(l, 12 * 16 + 16))
                    wv = ring[j].rearrange("p (k n) -> p k n", k=KD)
                    pe.wait_ge(out_used.sem, out_used.at(l, n - 1))
                    for k in range(KD):
                        mm = pe.matmul(bank(4 + n % 2)[:, 0:T], wv[:, k, (n % 4) * P:(n % 4 + 1) * P],
                                       merged[:, k, :], start=k == 0, stop=k == KD - 1)
                    mm.then_inc(out_done.sem, 1)

                pe.wait_ge(squares_ready.sem, squares_ready.at(l, 2))
                sum_squares()
                pe.wait_ge(h_ready.sem, h_ready.at(l, 2))
                for t in range(NT):
                    for k in range(KD):
                        mm = pe.matmul(bank(6)[:, t * 20:t * 20 + 20], hT[:, k, tok(t)], w_router[:, k, :],
                                       start=k == 0, stop=k == KD - 1, skip_group_check=True)
                mm.then_inc(rt_done.sem, 1)
                for n in range(6):
                    half, t = divmod(n, 3)
                    pe.wait_ge(ht_copied.sem, ht_copied.at(l, n - 1))
                    for k in range(4):
                        mm = pe.transpose(bank(2 + n % 2)[:, k * P:(k + 1) * P], hT[:, half * 4 + k, tok(t)], ident)
                    mm.then_inc(ht_done.sem, 1)
                pe.wait_ge(sel_ready.sem, sel_ready.at(l, 1))
                for t in range(NT):
                    for s in range(t + 1):
                        pe.matmul(bank(7)[:, t * NE:(t + 1) * NE], tri[0] if s == t else cc("sixteenth"), sel[:, s, :],
                                  start=s == 0, stop=s == t, skip_group_check=True)
                for s in range(NT):
                    mm = pe.matmul(bank(7)[:, NT * NE:(NT + 1) * NE], ones, sel[:, s, :], start=s == 0, stop=s == NT - 1,
                                   skip_group_check=True)
                mm.then_inc(rank_done.sem, 1)

                def gather(x):
                    pe.wait_ge(p_built.sem, l * (NE + 1) + x + 1)
                    for k in range(KD):
                        for t in range(NT):
                            mm = pe.matmul(psum[0][:, k * P:(k + 1) * P], htok[k // 4][:, t, (k % 4) * P:(k % 4 + 1) * P],
                                           x_p[:, t, :], start=t == 0, stop=t == NT - 1, skip_group_check=True)
                    mm.then_inc(xh_done.sem, 1)

                def turn_slots():
                    for t in range(NT):
                        mm = pe.transpose(bank(7)[:, tok(t)], x_pw[:, t, :], ident)
                    mm.then_inc(pt_done.sem, 1)

                pe.wait_ge(ht_copied.sem, ht_copied.at(l, 6))
                gather(0)
                turn_slots()
                with pe.Fori(0, NE // 2) as i:
                    for p in range(2):
                        w1, w3 = (ring[3 * p + j].rearrange("p (k n) -> p k n", k=KD) for j in range(2))
                        w2 = ring[3 * p + 2].rearrange("p (c n) -> p c n", c=4)
                        pe.wait_ge(xh_ready.sem, l * (NE + 1) + i * 2 + (p + 1))
                        for j, w in ((0, w1), (1, w3)):
                            s = slot_in[3 * p + j]
                            pe.wait_ge(s.sem, l * s.per_layer + i * 16 + (FILLS_MIX[3 * p + j] * 16 + 16))
                            for k in range(KD):
                                mm = pe.matmul(bank(2 + j), x_h[:, k, :], w[:, k, :], start=k == 0, stop=k == KD - 1)
                        mm.then_inc(xab_done.sem, 1)
                        pe.wait_ge(back_used.sem, l * 128 + i * 16 + (8 * p + 2))
                        gather(i * 2 + (p + 1))
                        pe.wait_ge(xg_ready.sem, l * NE + i * 2 + (p + 1))
                        for f in range(4):
                            mm = pe.transpose(bank(4)[:, f * P:(f + 1) * P], x_g[:, f * P:(f + 1) * P], ident)
                        mm.then_inc(xgt_done.sem, 1)
                        pe.wait_ge(pt_ready.sem, l * (NE + 1) + i * 2 + (p + 1))
                        turn_slots()
                        s = slot_in[3 * p + 2]
                        pe.wait_ge(s.sem, l * s.per_layer + i * 16 + (FILLS_MIX[3 * p + 2] * 16 + 16))
                        pe.wait_ge(xgt_ready.sem, l * NE + i * 2 + (p + 1))
                        for n in range(2):
                            for f in range(4):
                                mm = pe.matmul(bank(5 + n), x_gT[:, f * P:(f + 1) * P], w2[:, f, n * 512:(n + 1) * 512],
                                               start=f == 0, stop=f == 3)
                            mm.then_inc(xy_done.sem, 1)
                        pe.wait_ge(xh_ready.sem, l * (NE + 1) + i * 2 + (p + 2))
                        for n in range(KD):
                            if n % 4 == 0:
                                pe.wait_ge(xy_ready.sem, l * 2 * NE + i * 4 + (2 * p + n // 4 + 1))
                            pe.wait_ge(back_used.sem, l * 128 + i * 16 + (8 * p + n + 1))
                            pe.matmul(bank(n % 2)[:, 0:T], x_y[:, n * P:(n + 1) * P], x_pT[p], start=True, stop=True)\
                              .then_inc(back_done.sem, 1)

                pe.wait_ge(pt_ready.sem, pt_ready.at(l, NE + 1))
                pe.wait_ge(spill_known.sem, spill_known.at(l, 1))
                pe.sem_inc(spill_asked.sem, 1)
                spilled = pe.value_load(spill[0:1, 0:1], min_val=0, max_val=1)
                with pe.If(spilled > 0):
                    pe.wait_ge(sp_rw.sem, sp_rw.at(l, 1))
                    for t in range(NT):
                        mm = pe.transpose(bank(7)[0:NE, tok(t)], rw[:, t, 0:NE], ident)
                    mm.then_inc(rtt_done.sem, 1)

                    with pe.Fori(0, NE // 2) as i:
                        for p in range(2):
                            w1 = ring[3 * p]
                            w3 = ring[3 * p + 1]
                            w2 = ring[3 * p + 2]
                            w1 = w1.rearrange("p (k n) -> p k n", k=KD)
                            w3 = w3.rearrange("p (k n) -> p k n", k=KD)
                            w2 = w2.rearrange("p (c n) -> p c n", c=4)
                            pe.wait_ge(wm_ready.sem, l * (NE + 1) + i * 2 + (p + 1))
                            pe.matmul(bank(6)[:, 0:T], ones[0:NE, :], wm, start=True, stop=True)\
                              .then_inc(wb_done.sem, 1)
                            for j in range(2):
                                s = sp_slot[3 * p + j]
                                pe.wait_ge(s.sem, l * s.per_layer + i * 16 + 16)
                            for f in range(4):
                                pe.wait_ge(gu_ready.sem, l * 64 + i * 8 + (4 * p + f + 3))
                                for k in range(KD):
                                    pe.matmul(bank(f % 2)[:, 0:T], w1[:, k, f * P:(f + 1) * P], hT[:, k, :],
                                              start=k == 0, stop=k == KD - 1)
                                for k in range(KD):
                                    mm = pe.matmul(bank(2 + f % 2)[:, 0:T], w3[:, k, f * P:(f + 1) * P], hT[:, k, :],
                                                   start=k == 0, stop=k == KD - 1)
                                mm.then_inc(ab_done.sem, 1)
                            s = sp_slot[3 * p + 2]
                            pe.wait_ge(s.sem, l * s.per_layer + i * 16 + 16)
                            pe.wait_ge(gu_ready.sem, l * 64 + i * 8 + (4 * p + 4 + 4))
                            for n in range(KD):
                                pe.wait_ge(y_used.sem, l * 128 + i * 16 + (8 * p + n + 1))
                                for f in range(4):
                                    mm = pe.matmul(bank(4 + n % 2)[:, 0:T], w2[:, f, n * P:(n + 1) * P], gu[:, f, :],
                                                   start=f == 0, stop=f == 3)
                                mm.then_inc(y_done.sem, 1)
                with pe.Else():
                    for s in (rtt_done, wb_done, ab_done, y_done):
                        pe.sem_inc(s.sem, s.per_layer)
            pe.wait_ge(squares_ready.sem, 2 * DEPTH + 1)
            sum_squares()

        @block.scalar
        def _(ac):
            def d_copy(v):
                h, t = divmod(v, 3)
                ac.wait_ge(dpv_done.sem, dpv_done.at(l, v + 1))
                ac.activation(ytok[:, t, h * P:(h + 1) * P], bank(4 + v % 2)[:, 0:P], ACT.Copy)\
                  .then_inc(dpv_copied.sem, 1)

            chain = Chain(ac, act_chain, ACT_STEPS)
            ac.sem_inc(ch_copied.sem, 2)
            ac.sem_inc(tok_copied.sem, 2)
            ac.sem_inc(gate_sig.sem, 2)
            ac.wait_ge(loaded.sem, 32)
            ac.activation(small[:, 0:16], cc("cond"), ACT.Exp, scale=-1.0).then_inc(setup_s.sem, 1)

            def squares():
                for k in range(KD):
                    o = ac.activation(hT[:, k, :], xT[:, k, :], ACT.Square)
                o.then_inc(squares_ready.sem, 1)

            def inverse_rms(l, n):
                ac.wait_ge(sumsq_done.sem, n)
                chain.step(ac.activation(rstd[:, :], bank(0)[:, 0:T], ACT.Ln, scale=1.0 / D, bias=eps[:, 0:1]))
                chain.settle()
                ac.activation(rstd[:, :], rstd[:, :], ACT.Exp, scale=-0.5).then_inc(rstd_ready.sem, 1)

            def norm(l, which):
                ac.wait_ge(x_ready.sem, l * 2 + (which + 1))
                squares()
                inverse_rms(l, l * 2 + (which + 1))
                for k in range(KD):
                    ac.wait_ge(xn_ready.sem, l * 16 + (8 * which + k + 1))
                    for c, cols_ in enumerate((CTX, LAT)):
                        o = ac.activation(hT[:, k, cols_], hT[:, k, cols_], ACT.Identity,
                                          scale=amp[:, which, k, c:c + 1],
                                          bias=mod[:, 24 * which + k, c:c + 1])
                o.then_inc(h_ready.sem, 1)

            def finish(l, b):
                ac.wait_ge(fin_sq.sem, fin_sq.at(l, b + 1))
                chain.step(ac.activation(small[:, 12:24], small[:, 0:12], ACT.Ln, scale=1.0 / DV, bias=eps[:, 0:1]))
                chain.settle()
                ac.activation(small[:, 12:24], small[:, 12:24], ACT.Exp, scale=-0.5).then_inc(fin_rs.sem, 1)

            def ch_copy(l, i, chunks=12):
                for g in range(chunks):
                    ac.wait_ge(ch_done.sem, l * 36 + i * 12 + (g + 1))
                    ac.activation(pc_flat[:, bass.ds(i * (12 * T) + (g + 8) * T, T)], bank(g % 2)[:, 0:T], ACT.Copy)\
                      .then_inc(ch_copied.sem, 1)

            ac.wait_ge(setup_s.sem, 7)
            with ac.Fori(0, DEPTH) as l:
                chain.layer, chain.n = l, 0
                norm(l, 0)
                ac.wait_ge(small_done.sem, small_done.at(l, 2))
                chain.step(ac.activation(rows[:, R_I, :], bank(4)[0:64, 0:T], ACT.Identity, bias=pp("b_i")[0:64]))
                chain.step(ac.activation(rows[:, R_F, :], bank(4)[64:128, 0:T], ACT.Identity,
                                         bias=pp("b_f")[64:128]))
                chain.step(ac.activation(gaT[0:32, :], bank(5)[0:32, 0:T], ACT.Copy))
                chain.settle()
                chain.step(ac.activation(rows[:, R_T, :], rows[:, R_F, :], ACT.Abs))
                chain.settle()
                chain.step(ac.activation(rows[:, R_T, :], rows[:, R_T, :], ACT.Exp, scale=-1.0))
                chain.settle()
                ac.activation(rows[:, R_T, :], rows[:, R_T, :], ACT.Ln, bias=ones[0:64, 0:1]).then_inc(ga_ready.sem, 1)
                ch_copy(l, 0)
                ac.wait_ge(ch_copied.sem, ch_copied.at(l, 12))
                ac.activation(pc[:, CB, :, :], pc[:, CB, :, :], ACT.Sigmoid).then_inc(cb_sig.sem, 1)
                with ac.Fori(1, EARLY // RING) as i:
                    ch_copy(l, i)
                ch_copy(l, EARLY // RING, 4)
                for j in range(2):
                    for t in range(NT):
                        g = j * 3 + t
                        ac.wait_ge(tok_done.sem, tok_done.at(l, g + 1))
                        B = bank(2 + g % 2)
                        if j == 0:
                            o = ac.activation(mva[:, t, :, 0:DV], B.rearrange("p (h n) -> p h n", h=H), ACT.Copy)
                        else:
                            o = ac.activation(dv[:, t, :], B, ACT.Copy)
                        o.then_inc(tok_copied.sem, 1)

                def late_copy(g):
                    if g < 8:
                        ac.wait_ge(ch_done.sem, ch_done.at(l, 28 + g + 1))
                        ac.activation(pc[:, g // 4, g % 4, :], bank(6 + g % 2)[:, 0:T], ACT.Copy)\
                          .then_inc(ch_copied.sem, 1)
                    else:
                        ac.wait_ge(tok_done.sem, tok_done.at(l, 6 + g - 8 + 1))
                        ac.activation(gv[:, g - 8, :], bank(6 + g % 2), ACT.Copy).then_inc(tok_copied.sem, 1)

                ac.wait_ge(lams_done.sem, lams_done.at(l, 1))
                ac.activation(small[:, 42:44], bank(7)[:, 256:258], ACT.Exp).then_inc(lame_ready.sem, 1)
                ac.wait_ge(ch_copied.sem, ch_copied.at(l, 28))
                chain.step(ac.activation(pc[:, MO, :, :], pc[:, MO, :, :], ACT.Sigmoid))
                ac.wait_ge(rows_ready.sem, rows_ready.at(l, 1))
                chain.step(ac.activation(rows[0:36, R_A, :], rows[0:36, R_NG, :], ACT.Exp, bias=pp("m0")[0:36]))
                chain.step(ac.activation(rows[0:36, R_EM, :], rows[0:36, R_EM, :], ACT.Exp, scale=-1.0))
                ac.activation(rows[0:36, R_T, CTX], rows[0:36, R_U, CTX], ACT.Exp, bias=small[0:36, 61:62])\
                  .then_inc(rows_exp.sem, 1)
                ac.wait_ge(cols_ready.sem, cols_ready.at(l, 1))
                for i in range(9):
                    if i < 8:
                        d, h = divmod(i, H)
                        off_s = 1 if d == 0 else 2
                        ac.wait_ge(bc_done.sem, bc_done.at(l, i + 1))
                        if i >= 2:
                            ac.wait_ge(s_ready.sem, s_ready.at(l, i - 1))
                        for n, s in enumerate((0, 1, 2, off_s)):
                            r = bflip(d, h)
                            o = ac.activation(m_exp[i % 2][:, n * P:(n + 1) * P], bank(i % 2)[:, n * P:(n + 1) * P],
                                              ACT.Exp, bias=cols[:, s, r:r + 1])
                        o.then_inc(mexp_ready.sem, 1)
                    if i >= 1:
                        d, h = divmod(i - 1, H)
                        r, N = bflip(d, h), DV + 1
                        ac.wait_ge(pv_done.sem, pv_done.at(l, i))
                        if i >= 3:
                            ac.wait_ge(m_out.sem, m_out.at(l, i - 2))
                        for t in (1, 2):
                            o = ac.activation(m_x[:, (i - 1) % 2, (t - 1) * N:t * N],
                                              bank(6 + (i - 1) % 2)[:, (t - 1) * N:t * N],
                                              ACT.Copy, scale=cols[:, 3 + t, r:r + 1])
                        o.then_inc(inter_ready.sem, 1)
                for i in range(8):
                    ac.wait_ge(st_done.sem, st_done.at(l, i + 1))
                    ac.wait_ge(outs.sem, l * outs.per_layer + 16 * (4 + i))
                    ac.activation(st_out, bank(0)[:, 0:DV + 1], ACT.Copy).then_inc(st_copied.sem, 1)
                    if i == 1:
                        late_copy(0)
                        ac.wait_ge(conv_mean.sem, conv_mean.at(l, 1))
                        ac.activation(e_t[:, :, :], pc[:, CA, :, :], ACT.Square).then_inc(conv_sq.sem, 1)
                    elif i == 2:
                        ac.wait_ge(conv_sum.sem, conv_sum.at(l, 2))
                        chain.step(ac.activation(rstd[:, :], bank(2)[:, 0:T], ACT.Ln, scale=1.0 / W,
                                                 bias=eps[:, 0:1]))
                        chain.settle()
                        ac.activation(rstd[:, :], rstd[:, :], ACT.Exp, scale=-0.5).then_inc(conv_rs.sem, 1)
                    elif i % 2:
                        late_copy(i // 2)
                finish(l, 0)

                ac.wait_ge(la_done.sem, la_done.at(l, 1))
                ac.wait_ge(fin_n.sem, fin_n.at(l, 1))
                for t in range(NT):
                    chain.step(ac.activation(scrB[:, t * 512:(t + 1) * 512], bank(4 + t), ACT.Abs))
                chain.settle()
                chain.step(ac.activation(scrB, scrB, ACT.Exp, scale=-1.0))
                chain.settle()
                ac.activation(scrB, scrB, ACT.Ln, bias=ones[:, 0:1]).then_inc(la_exp.sem, 1)
                ac.wait_ge(ch_copied.sem, ch_copied.at(l, 32))
                chain.step(ac.activation(pc[:, GR, :, :], pc[:, GR, :, :], ACT.Silu))
                for u in range(4):
                    ac.wait_ge(g_done.sem, g_done.at(l, u + 1))
                    if u == 0:
                        ac.wait_ge(la_ready.sem, la_ready.at(l, 1))
                    ac.activation(gT[:, u, :], bank(u % 2)[:, 0:T], ACT.Copy).then_inc(g_ready.sem, 1)
                late_copy(4)

                def factors(u):
                    ac.wait_ge(gd_ready.sem, gd_ready.at(l, u + 1))
                    for _, z in g_z[u % 2]:
                        chain.step(ac.activation(z, z, ACT.Abs))
                    chain.settle()
                    for _, z in g_z[u % 2]:
                        o = ac.activation(z, z, ACT.Exp, scale=-1.0)
                    o.then_inc(gx_ready.sem, 1)


                for u in range(24):
                    h, t, c = u // 6, (u // 2) % 3, u % 2
                    nk = P if t == 0 else T
                    ac.wait_ge(negmax.sem, negmax.at(l, u + 1))
                    if u >= 4:
                        ac.wait_ge(dw_ready.sem, dw_ready.at(l, u // 2 - 1))
                    ac.activation(d_p[(u // 2) % 2][:, c, 0:nk], bank(u % 2)[:, 0:nk], ACT.Exp, scale=D_SCALE,
                                  bias=small[:, 24 + u % 4:25 + u % 4],
                                  accum_out=small[:, 28 + u % 4:29 + u % 4]).then_inc(p_ready.sem, 1)
                    if u % 4 == 3:
                        late_copy(5 + u // 4)
                    if u == 7:
                        factors(0)
                    if u % 2 and u >= 3:
                        d_copy(u // 2 - 1)
                d_copy(11)
                finish(l, 1)

                def cross_factors(u):
                    ac.wait_ge(gcd_ready.sem, gcd_ready.at(l, u + 1))
                    chain.step(ac.activation(g_xx, g_xx, ACT.Abs))
                    chain.step(ac.activation(g_kd, g_kd, ACT.Abs))
                    chain.settle()
                    chain.step(ac.activation(g_xx, g_xx, ACT.Exp, scale=-1.0))
                    chain.step(ac.activation(g_kd, g_kd, ACT.Exp, scale=-1.0))
                    if u >= 2:
                        ac.wait_ge(go_done.sem, go_done.at(l, 2 * u - 2))
                    ac.activation(g_qs[u % 2], gT[:, u, LAT], ACT.Exp).then_inc(gcx_ready.sem, 1)

                cross_factors(0)
                for u in range(4):
                    d = u % 2
                    if u < 3:
                        factors(u + 1)
                    ac.wait_ge(gc_done.sem, gc_done.at(l, 2 * u + 2))
                    if u >= 1:
                        ac.wait_ge(go_done.sem, go_done.at(l, 2 * u))
                    ac.activation(g_ca, bank(6)[:, 0:2 * P], ACT.Copy).then_inc(gc_copied.sem, 1)
                    ac.wait_ge(gs_t.sem, gs_t.at(l, u + 1))
                    if u >= 1:
                        ac.wait_ge(gs_done.sem, gs_done.at(l, u))
                    ac.activation(g_kt, bank(7)[:, 0:P], ACT.Copy).then_inc(gs_tc.sem, 1)
                    att = g_att[d].rearrange("p (h t) n -> p h t n", h=2)
                    for w, column, copied in ((32, 2 * NLEV * SUB, g32_copied), (64, 512 + NLEV * SUB, g64_copied)):
                        for hh in range(2):
                            ac.wait_ge(gm_ready.sem, gm_ready.at(l, u * 4 + (1 if w == 32 else 3) + hh))
                            for j in range(P // (2 * w)):
                                s0 = 2 * w * j + (w if d else 0)
                                t0 = 2 * w * j + (0 if d else w)
                                o = ac.activation(att[s0:s0 + w, hh, :, t0:t0 + w],
                                                  psum[hh][s0:s0 + w, column:column + NT * w]
                                                  .rearrange("p (t n) -> p t n", t=NT), ACT.Copy)
                        o.then_inc(copied.sem, 1)
                    ac.wait_ge(gsum_ready.sem, gsum_ready.at(l, u + 1))
                    for b in range(4):
                        r = slice(SUB * b, SUB * b + SUB)
                        o = ac.activation(g_att[d][r, :, r], g_c[r, :, :], ACT.Copy)
                    o.then_inc(gatt_ready.sem, 1)
                    if u < 3:
                        cross_factors(u + 1)
                    ac.wait_ge(gs_done.sem, gs_done.at(l, u + 1))
                    ac.wait_ge(outs.sem, l * outs.per_layer + 16 * (12 + 2 * u))
                    for hh in range(2):
                        ac.activation(g_so[64 * hh:64 * hh + 64, :], bank(7)[64 * hh:64 * hh + 64, hh * P:(hh + 1) * P],
                                      ACT.Copy).then_inc(gs_copied.sem, 1)
                    if d:
                        for hh in range(2):
                            head = (u // 2) * 2 + hh
                            ac.wait_ge(go_done.sem, go_done.at(l, u * 2 + hh + 1))
                            ac.activation(ytok[:, :, head * P:(head + 1) * P],
                                          bank(4 + hh)[:, 0:T].rearrange("p (t n) -> p t n", t=NT), ACT.Copy)\
                              .then_inc(go_copied.sem, 1)
                finish(l, 2)

                ac.wait_ge(outs.sem, l * outs.per_layer + outs.per_layer)
                ac.wait_ge(conv_n.sem, conv_n.at(l, 1))
                for c in range(4):
                    chain.step(ac.activation(pc[:, CB, c, :], pc[:, CA, c, :], ACT.Identity,
                                             scale=pp("ln_g")[:, c:c + 1], bias=pp("ln_b")[:, c:c + 1]))
                chain.settle()
                ac.activation(pc[:, CB, :, :], pc[:, CB, :, :], ACT.Silu).then_inc(conv_done.sem, 1)

                with ac.Fori(0, 4) as i:
                    for n in range(8):
                        ac.wait_ge(gate_done.sem, l * 32 + i * 8 + (n + 1))
                        ac.wait_ge(merged_s.sem, l * 32 + i * 8 + (n + 1))
                        ac.activation(e_t[:, n % 2, :], bank(4 + n % 2)[:, 0:T], ACT.Sigmoid).then_inc(gate_sig.sem, 1)
                norm(l, 1)
                for t in range(NT):
                    ac.wait_ge(rt_step.sem, rt_step.at(l, 2 * t + 1))
                    ac.activation(rt[:, 100:104], rt[:, 100:104], ACT.Exp,
                                  accum_out=rt[:, 104:105]).then_inc(rt_exp.sem, 1)
                    ac.wait_ge(rt_step.sem, rt_step.at(l, 2 * t + 2))
                    ac.activation(rt[:, 105:106], rt[:, 105:106], ACT.Exp).then_inc(rt_exp.sem, 1)
                def copy_gathered(x):
                    ac.wait_ge(xh_done.sem, l * (NE + 1) + x + 1)
                    ac.activation(scr[:, 0:1024], psum[0][:, :], ACT.Copy).then_inc(xh_ready.sem, 1)

                copy_gathered(0)
                ac.wait_ge(pt_done.sem, pt_done.at(l, 1))
                ac.activation(x_pT[0], bank(7)[:, 0:T], ACT.Copy).then_inc(pt_ready.sem, 1)
                with ac.Fori(0, NE // 2) as i:
                    for p in range(2):
                        ac.wait_ge(xab_done.sem, l * NE + i * 2 + (p + 1))
                        ac.activation(x_s, bank(2), ACT.Silu).then_inc(xs_ready.sem, 1)
                        copy_gathered(i * 2 + (p + 1))
                        ac.wait_ge(xgt_done.sem, l * NE + i * 2 + (p + 1))
                        ac.activation(x_gT, bank(4), ACT.Copy).then_inc(xgt_ready.sem, 1)
                        ac.wait_ge(pt_done.sem, l * (NE + 1) + i * 2 + (p + 2))
                        ac.activation(x_pT[1 - p], bank(7)[:, 0:T], ACT.Copy).then_inc(pt_ready.sem, 1)
                        for n in range(2):
                            ac.wait_ge(xy_done.sem, l * 2 * NE + i * 4 + (2 * p + n + 1))
                            ac.activation(x_y[:, n * 512:(n + 1) * 512], bank(5 + n), ACT.Copy)\
                              .then_inc(xy_ready.sem, 1)
                ac.wait_ge(spill_known.sem, spill_known.at(l, 1))
                ac.sem_inc(spill_asked.sem, 1)
                spilled = ac.value_load(spill[0:1, 0:1], min_val=0, max_val=1)
                with ac.If(spilled > 0):
                    with ac.Fori(0, NE // 2) as i:
                        for p in range(2):
                            ac.wait_ge(wb_done.sem, l * 16 + i * 2 + (p + 1))
                            ac.wait_ge(gu_ready.sem, l * 64 + i * 8 + (4 * p + 4))
                            ac.activation(wb, bank(6)[:, 0:T], ACT.Copy).then_inc(wb_ready.sem, 1)
                            for f in range(4):
                                ac.wait_ge(ab_done.sem, l * 64 + i * 8 + (4 * p + f + 1))
                                ac.wait_ge(gu_ready.sem, l * 64 + i * 8 + (4 * p + f + 3))
                                ac.activation(e_t[:, f % 2, :], bank(f % 2)[:, 0:T], ACT.Silu).then_inc(a_exp.sem, 1)
                with ac.Else():
                    for s in (wb_ready, a_exp):
                        ac.sem_inc(s.sem, s.per_layer)
            assert chain.n == ACT_STEPS, chain.n
            ac.wait_ge(x_ready.sem, 2 * DEPTH + 1)
            squares()
            ac.wait_ge(sumsq_done.sem, 2 * DEPTH + 1)
            ac.activation(rstd[:, :], bank(0)[:, 0:T], ACT.Ln, scale=1.0 / D, bias=eps[:, 0:1]).then_inc(final_s.sem, 1)
            ac.wait_ge(final_s.sem, 1)
            ac.activation(rstd[:, :], rstd[:, :], ACT.Exp, scale=-0.5).then_inc(final_s.sem, 1)

        @block.vector
        def _(ve):
            chain = Chain(ve, dve_chain, DVE_STEPS)
            for s, n in ((params_free, 1), (mod_used, 1), (merged_s, 2), (out_used, 2), (ht_copied, 2), (back_used, 2), (gu_ready, 4), (y_used, 2)):
                ve.sem_inc(s.sem, n)
            ve.memset(mva[:, :, :, DV:DV + 1], 1.0)
            ve.memset(gaT[32:33, :], 1.0)
            ve.memset(eps[:, :], EPS)
            ve.memset(rw[:, :, NE:NE + 1], 0.0)
            ve.memset(rk[:, :, NE:NE + 1], 0.0)
            ve.wait_ge(loaded.sem, 32)
            ve.sem_inc(x_ready.sem, 1)
            ve.wait_ge(setup_s.sem, 1)
            ve.tensor_scalar(small[:, 0:16], small[:, 0:16], 1.0, None, ALU.add).then_inc(setup_s.sem, 1)
            ve.wait_ge(setup_s.sem, 2)
            ve.reciprocal(small[:, 0:16], small[:, 0:16]).then_inc(setup_s.sem, 1)
            ve.wait_ge(setup_s.sem, 3)
            ve.tensor_tensor(cc("cond"), cc("cond"), small[:, 0:16], ALU.mult).then_inc(setup_s.sem, 1)
            ve.wait_ge(setup_s.sem, 4)
            ve.memset(rows[:, :, :], 0.0).then_inc(setup_s.sem, 1)
            ve.memset(merged[:, :, :], 0.0).then_inc(setup_s.sem, 1)
            ve.memset(small[:, 60:62], 0.0).then_inc(setup_s.sem, 1)
            ve.wait_ge(setup_s.sem, 7)

            def step(o):
                chain.step(o)

            def scaled(l, which):
                for k in range(KD):
                    if k == 0:
                        ve.wait_ge(rstd_ready.sem, l * 2 + (which + 1))
                    ve.tensor_tensor(hT[:, k, :], xT[:, k, :], rstd[:, :], ALU.mult).then_inc(xn_ready.sem, 1)

            def finish_sums(l, b):
                step(ve.tensor_tensor(scrB, ytok[:, :, :].rearrange("p t n -> p (t n)"),
                                      ytok[:, :, :].rearrange("p t n -> p (t n)"), ALU.mult))
                chain.settle()
                o = ve.tensor_reduce(small[:, 0:12], scrB.rearrange("p (a n) -> p a n", n=P), AX.X, ALU.add)
                o.then_inc(fin_sq.sem, 1)
                ve.wait_ge(fin_rs.sem, fin_rs.at(l, b + 1))
                yv = ytok[:, :, :].rearrange("p t (h n) -> p (t h) n", h=H)
                ve.tensor_tensor(yv, yv, small[:, 12:24].rearrange("p (a b) -> p a b", b=1)
                                 .to_broadcast([P, 12, P]), ALU.mult).then_inc(fin_n.sem, 1)

            with ve.Fori(0, DEPTH) as l:
                chain.layer, chain.n = l, 0
                with ve.Fori(0, NMOD // RING) as i:
                    for j in range(RING):
                        ve.wait_ge(mod_done.sem, l * NMOD + i * RING + (j + 1))
                        ve.tensor_copy(mod_rows[:, j * W:(j + 1) * W], bank(5 + j)[0:2, :]).then_inc(mod_row.sem, 1)
                    ve.wait_ge(params_in.sem, params_in.at(l, 32))
                    ve.wait_ge(mod_turned.sem, l * (NMOD // RING) + i + 1)
                    bias = par[:, bass.ds(i * 12 + PAR["bmod"][0], 12)]
                    ve.tensor_tensor(mod[:, bass.ds(i * 12, 12), :],
                                     bank(4)[:, 0:24].rearrange("p (a b) -> p a b", b=2),
                                     bias.rearrange("p (a b) -> p a b", b=1).to_broadcast([P, 12, 2]), ALU.add)\
                      .then_inc(mod_used.sem, 1)
                ve.wait_ge(mod_used.sem, mod_used.at(l, NMOD // RING))
                for w, nm in enumerate(("norm1", "norm2")):
                    g = pp(nm).rearrange("p (a b) -> p a b", b=1).to_broadcast([P, KD, 2])
                    step(ve.scalar_tensor_tensor(amp[:, w, :, :], mod[:, 24 * w + 8:24 * w + 16, :], 1.0, g,
                                                 ALU.add, ALU.mult))
                ve.tensor_tensor(small[0:64, 40:42], pp("lam")[0:64, 0:4:2], pp("lam")[0:64, 1:4:2], ALU.mult)\
                  .then_inc(lamp_ready.sem, 1)
                scaled(l, 0)

                ve.wait_ge(ga_ready.sem, ga_ready.at(l, 1))
                step(ve.scalar_tensor_tensor(rows[:, R_F, :], rows[:, R_F, :], 0.0, rows[:, R_T, :],
                                             ALU.min, ALU.subtract))
                chain.settle()

                def scans(fn):
                    for d in range(2):
                        rs = slice(32 * d, 32 * d + 4)
                        for grp, (a, b) in enumerate(((0, SEQ), (SEQ, T))):
                            back = slice(b - 1, a - 1 if a else None, -1)
                            fn(rs, grp, slice(a, b) if d == 0 else back)
                scans(lambda rs, grp, s: step(ve.tensor_tensor_scan(
                    rows[rs, R_B, s], ones[rs, 0:1].to_broadcast([4, (P, DEC)[grp]]), rows[rs, R_F, s], 0.0, ALU.mult, ALU.add)))
                chain.settle()
                step(ve.tensor_tensor(rows[0:36, R_U, :], rows[0:36, R_I, :], rows[0:36, R_B, :], ALU.subtract))
                chain.settle()
                scans(lambda rs, grp, s: step(ve.tensor_tensor_scan(
                    rows[rs, R_T, s], cc("zero")[rs, 0:1].to_broadcast([4, (P, DEC)[grp]]), rows[rs, R_U, s],
                    0.0 if grp == 0 else pp("m0")[rs, :], ALU.add, ALU.max)))
                chain.settle()
                step(ve.tensor_scalar(rows[0:36, R_NG, :], rows[0:36, R_T, :], -1.0, None, ALU.mult))
                step(ve.tensor_tensor(rows[0:36, R_EM, :], rows[0:36, R_T, :], rows[0:36, R_B, :], ALU.add))
                chain.settle()
                for d in range(2):
                    rs, last = slice(32 * d, 32 * d + 4), SEQ - 1 if d == 0 else 0
                    step(ve.tensor_copy(small[rs, 60:61], rows[rs, R_EM, last:last + 1]))
                    o = ve.tensor_copy(small[rs, 61:62], rows[rs, R_NG, last:last + 1])
                    if d == 0:
                        step(o)
                o.then_inc(rows_ready.sem, 1)

                ve.wait_ge(cb_sig.sem, cb_sig.at(l, 1))
                step(ve.tensor_tensor(upad[:, :, PAD:PAD + SEQ], pc[:, CA, :, CTX], pc[:, CB, :, CTX], ALU.mult))
                step(ve.tensor_tensor(upad[:, :, 2 * PAD + SEQ:2 * PAD + T], pc[:, CA, :, LAT], pc[:, CB, :, LAT],
                                      ALU.mult))
                for z in (0, PAD + SEQ, 2 * PAD + T):
                    step(ve.memset(upad[:, :, z:z + PAD], 0.0))
                chain.settle()
                for j in range(CW):
                    for c in range(4):
                        for first, g in ((0, CTX), (PAD, LAT)):
                            src = upad[:, c, g.start + first + j:g.stop + first + j]
                            dst = pc[:, CA, c, g]
                            if j == 0:
                                step(ve.tensor_scalar(dst, src, taps[:, c, 0:1], None, ALU.mult))
                                continue
                            chain.settle(but=7)
                            o = ve.scalar_tensor_tensor(dst, src, taps[:, c, j:j + 1], dst, ALU.mult, ALU.add)
                            if j == CW - 1 and c == 3 and g is LAT:
                                o.then_inc(conv_acc.sem, 1)
                            else:
                                step(o)

                ve.wait_ge(lame_ready.sem, lame_ready.at(l, 1))
                chain.settle()
                step(ve.tensor_tensor(small[:, 44:45], small[:, 42:43], small[:, 43:44], ALU.subtract))
                chain.settle()
                step(ve.tensor_tensor(small[:, 44:45], small[:, 44:45],
                                      cst[:, bass.ds(l + CST["lam_init"][0], 1)], ALU.add))

                ve.wait_ge(cols_done.sem, cols_done.at(l, 1))
                ve.tensor_copy(cols[:, :, :], bank(4)[:, 0:360].rearrange("p (a b) -> p a b", a=10))\
                  .then_inc(cols_ready.sem, 1)
                ve.wait_ge(kt_done.sem, kt_done.at(l, 1))
                ve.tensor_copy(mktok, bank(5).rearrange("p (h n) -> p h n", h=H)).then_inc(kt_ready.sem, 1)
                for i in range(9):
                    if i < 8:
                        ve.wait_ge(mexp_ready.sem, mexp_ready.at(l, i + 1))
                        ve.wait_ge(qk_done.sem, qk_done.at(l, i + 1))
                        if i >= 2:
                            ve.wait_ge(pv_done.sem, pv_done.at(l, i - 1))
                        ve.scalar_tensor_tensor(m_s[i % 2], bank(2 + i % 2), M_SCALE, m_exp[i % 2],
                                                ALU.mult, ALU.mult).then_inc(s_ready.sem, 1)
                    if i >= 1:
                        n, N = i - 1, DV + 1
                        d, h = divmod(n, H)
                        r = bflip(d, h)
                        ve.wait_ge(inter_ready.sem, inter_ready.at(l, n + 1))
                        V = bank(4 + n % 2)
                        if n >= 1:
                            ve.wait_ge(m_out.sem, m_out.at(l, n))
                        step(ve.tensor_copy(m_nd[:, 0, :], V[:, 0:N]))
                        step(ve.tensor_tensor(m_nd[:, 1:3, :], V[:, N:3 * N].rearrange("p (t n) -> p t n", t=2),
                                              m_x[:, n % 2, :].rearrange("p (t n) -> p t n", t=2), ALU.add))
                        chain.settle()
                        den = m_nd[:, :, DV:N].rearrange("p t n -> p (t n)")
                        step(ve.scalar_tensor_tensor(small[:, 45:48], den, -1.0, den, ALU.mult, ALU.max))
                        chain.settle()
                        step(ve.tensor_tensor(small[:, 45:48], small[:, 45:48],
                                              cols[:, 6:9, r:r + 1].rearrange("p t n -> p (t n)"), ALU.max))
                        chain.settle()
                        step(ve.reciprocal(small[:, 45:48], small[:, 45:48]))
                        chain.settle()
                        for t in range(NT):
                            y = ytok[:, t, h * P:(h + 1) * P]
                            if d == 0:
                                o = ve.tensor_scalar(y, m_nd[:, t, 0:DV], small[:, 45 + t:46 + t], None, ALU.mult)
                            else:
                                o = ve.scalar_tensor_tensor(y, m_nd[:, t, 0:DV], small[:, 45 + t:46 + t], y,
                                                            ALU.mult, ALU.add)
                            if t < NT - 1:
                                step(o)
                        o.then_inc(m_out.sem, 1)
                        chain.settle()
                for i in range(8):
                    d, h = divmod(i, H)
                    r = bflip(d, h)
                    if i >= 1:
                        ve.wait_ge(st_done.sem, st_done.at(l, i))
                    ve.tensor_scalar(kstate, mktok[:, h, :], cols[:, 9, r:r + 1], M_SCALE,
                                     ALU.mult, ALU.mult).then_inc(kw_ready.sem, 1)
                    if i == 1:
                        ve.wait_ge(conv_sum.sem, conv_sum.at(l, 1))
                        step(ve.tensor_scalar(cmean, bank(1)[:, 0:T], 1.0 / W, None, ALU.mult))
                        chain.settle()
                        ve.tensor_tensor(pc[:, CA, :, :], pc[:, CA, :, :],
                                         cmean.rearrange("p (a b) -> p a b", a=1).to_broadcast([P, 4, T]),
                                         ALU.subtract).then_inc(conv_mean.sem, 1)
                    if i == 5:
                        ve.wait_ge(conv_rs.sem, conv_rs.at(l, 1))
                        ve.tensor_tensor(pc[:, CA, :, :], pc[:, CA, :, :],
                                         rstd[:, :].rearrange("p (a b) -> p a b", a=1).to_broadcast([P, 4, T]),
                                         ALU.mult).then_inc(conv_n.sem, 1)
                ve.wait_ge(m_out.sem, m_out.at(l, 8))
                ve.wait_ge(kw_ready.sem, kw_ready.at(l, 8))
                finish_sums(l, 0)
                ve.wait_ge(fin_t.sem, fin_t.at(l, 1))
                chain.settle()
                for h in range(H):
                    o = ve.scalar_tensor_tensor(pc[:, MO, h, :], bank(h)[:, 0:T], pp("hn_m")[:, h:h + 1],
                                                pc[:, MO, h, :], ALU.mult, ALU.mult)
                o.then_inc(fin_done.sem, 1)

                for n in range(8):
                    slot, h = (DQ, DKK)[n // 4], n % 4
                    v = pc[:, slot, h, LAT]
                    ve.wait_ge(rot_done.sem, rot_done.at(l, n + 1))
                    step(ve.tensor_tensor(rstd[:, 0:DEC], bank(n % 2)[:, 0:DEC], cc("sin"), ALU.mult))
                    step(ve.tensor_tensor(v, v, cc("cos"), ALU.mult))
                    chain.settle()
                    ve.tensor_tensor(v, v, rstd[:, 0:DEC], ALU.add).then_inc(rot_used.sem, 1)
                    ve.wait_ge(rot_used.sem, rot_used.at(l, n + 1))

                ve.wait_ge(la_exp.sem, la_exp.at(l, 1))
                for t in range(NT):
                    o = ve.scalar_tensor_tensor(la[:, t, :], bank(4 + t), 0.0, scrB[:, t * 512:(t + 1) * 512],
                                                ALU.min, ALU.subtract)
                o.then_inc(la_ready.sem, 1)

                def differences(u):
                    for lv in range(LEVELS):
                        w = 1 << lv
                        sums = gT[:, u, :].rearrange("p (b w) -> p b w", w=2 * w)
                        mid = w - 1 if u % 2 == 0 else w
                        o = ve.tensor_tensor(g_zl[u % 2][lv].rearrange("p (b w) -> p b w", w=2 * w), sums,
                                             sums[:, :, mid:mid + 1].to_broadcast([P, T // (2 * w), 2 * w]),
                                             ALU.subtract)
                    o.then_inc(gd_ready.sem, 1)

                def scale(u):
                    pair, d = divmod(u, 2)
                    ve.wait_ge(gx_ready.sem, gx_ready.at(l, u + 1))
                    for lv in range(LEVELS):
                        w = 1 << lv
                        z = g_zl[u % 2][lv].rearrange("p (b w) -> p b w", w=2 * w)
                        for half, c in enumerate((2 + pair, pair) if d == 0 else (pair, 2 + pair)):
                            s = slice(half * w, half * w + w)
                            src = pc[:, GQK, c, :].rearrange("p (b w) -> p b w", w=2 * w)
                            o = ve.tensor_tensor(z[:, :, s], src[:, :, s], z[:, :, s], ALU.mult)
                    o.then_inc(gz_ready.sem, 1)

                ve.wait_ge(g_ready.sem, g_ready.at(l, 4))
                differences(0)

                def d_weights(v):
                    h, t = divmod(v, 3)
                    nk = P if t == 0 else T
                    q = (v % 2) * 2
                    dp = d_p[v % 2]
                    ve.wait_ge(p_ready.sem, p_ready.at(l, 2 * v + 2))
                    step(ve.reciprocal(small[:, 32:34], small[:, 28 + q:30 + q]))
                    chain.settle()
                    step(ve.tensor_tensor(small[:, 34:35], small[:, 33:34], small[:, 44:45], ALU.mult))
                    chain.settle()
                    step(ve.tensor_scalar(dp[:, 1, 0:nk], dp[:, 1, 0:nk], small[:, 34:35], None, ALU.mult))
                    if v >= 1:
                        ve.wait_ge(dwt_done.sem, dwt_done.at(l, v))
                    chain.settle()
                    ve.scalar_tensor_tensor(d_w[:, 0:nk], dp[:, 0, 0:nk], small[:, 32:33], dp[:, 1, 0:nk],
                                            ALU.mult, ALU.subtract).then_inc(dw_ready.sem, 1)
                    ve.wait_ge(dwt_done.sem, dwt_done.at(l, v + 1))
                    if v >= 1:
                        ve.wait_ge(dpv_done.sem, dpv_done.at(l, v))
                    ve.tensor_copy(d_wt[:, 0:nk], bank(2)[:, 0:nk]).then_inc(dwt_ready.sem, 1)

                for u in range(24):
                    h, t, c = u // 6, (u // 2) % 3, u % 2
                    nk = P if t == 0 else T
                    ve.wait_ge(sc_done.sem, sc_done.at(l, u + 1))
                    if u >= 4:
                        ve.wait_ge(p_ready.sem, p_ready.at(l, u - 3))
                    step(ve.tensor_reduce(small[:, 35:36], bank(u % 2)[:, 0:nk], AX.X, ALU.max))
                    chain.settle()
                    ve.tensor_scalar(small[:, 24 + u % 4:25 + u % 4], small[:, 35:36], -D_SCALE, None, ALU.mult)\
                      .then_inc(negmax.sem, 1)
                    ve.wait_ge(negmax.sem, negmax.at(l, u + 1))
                    if u % 2 and u >= 3:
                        d_weights(u // 2 - 1)
                    if u == 19:
                        ve.wait_ge(ch_copied.sem, ch_copied.at(l, 36))
                        step(ve.tensor_scalar(pc[:, GQK, 0:2, :], pc[:, GQK, 0:2, :], G_SCALE, None, ALU.mult))
                        chain.settle()
                        scale(0)
                d_weights(11)
                ve.wait_ge(dpv_copied.sem, dpv_copied.at(l, 12))
                finish_sums(l, 1)
                step(ve.tensor_scalar(small[:, 36:40], pp("hn_d"), cst[:, bass.ds(l + CST["one_less"][0], 1)], None,
                                      ALU.mult))
                ve.wait_ge(fin_t.sem, fin_t.at(l, 2))
                chain.settle()
                for h in range(H):
                    o = ve.tensor_scalar(pc[:, DQ, h, :], bank(h)[:, 0:T], small[:, 36 + h:37 + h], None, ALU.mult)
                o.then_inc(fin_done.sem, 1)

                ve.wait_ge(outs.sem, l * outs.per_layer + 16 * 12)
                for d in range(2):
                    step(ve.memset(g_att[d], 0.0))

                def cross_differences(u):
                    ref = 2 * P - 1 if u % 2 == 0 else 2 * P
                    last = SEQ - 1 if u % 2 == 0 else 0
                    gr = gT[:, u, :]
                    step(ve.tensor_tensor(g_xx, gr[:, LAT], gr[:, ref:ref + 1].to_broadcast([P, DEC]), ALU.subtract))
                    ve.tensor_tensor(g_kd, gr[:, CTX], gr[:, last:last + 1].to_broadcast([P, P]), ALU.subtract)\
                      .then_inc(gcd_ready.sem, 1)

                cross_differences(0)
                for u in range(4):
                    pair, d = divmod(u, 2)
                    q, k = pc[:, GQK, pair, :], pc[:, GQK, 2 + pair, :]
                    tq, tk = (2, 1) if d == 0 else (1, 2)
                    if u < 3:
                        if u >= 1:
                            ve.wait_ge(ga_done.sem, ga_done.at(l, 2 * u))
                        differences(u + 1)
                    ve.wait_ge(gcx_ready.sem, gcx_ready.at(l, u + 1))
                    step(ve.tensor_tensor(g_qx, q[:, tok(tq)], g_xx[:, tok(tq - 1)], ALU.mult))
                    step(ve.tensor_tensor(g_kx, k[:, tok(tk)], g_xx[:, tok(tk - 1)], ALU.mult))
                    step(ve.tensor_tensor(g_kd, k[:, CTX], g_kd, ALU.mult))
                    ve.tensor_tensor(g_qs[d], q[:, LAT], g_qs[d], ALU.mult).then_inc(gcq_ready.sem, 1)
                    if u < 3:
                        scale(u + 1)
                    if u >= 1:
                        ve.wait_ge(gsum_ready.sem, gsum_ready.at(l, u))
                    gm = g_m.rearrange("p (h t n) -> p h t n", h=2, t=NT)
                    for phase, (t0, t1, column) in enumerate(((0, 2, 0), (2, 3, 512))):
                        mask = lev[d].rearrange("p (a n) -> p a n", a=1).to_broadcast([P, t1 - t0, NLEV * SUB])
                        ve.wait_ge(ga_done.sem, ga_done.at(l, u * 2 + phase + 1))
                        for hh in range(2):
                            ve.tensor_tensor(gm[:, hh, t0:t1, :],
                                             psum[hh][:, column:column + (t1 - t0) * NLEV * SUB]
                                             .rearrange("p (t n) -> p t n", t=t1 - t0), mask, ALU.mult)\
                              .then_inc(gm_ready.sem, 1)
                    ve.wait_ge(gm_ready.sem, gm_ready.at(l, u * 4 + 4))
                    if u >= 1:
                        ve.wait_ge(gatt_ready.sem, gatt_ready.at(l, u))
                    ve.tensor_reduce(g_c, g_m.rearrange("p (x l t) -> p x t l", x=6, l=NLEV), AX.X, ALU.add)\
                      .then_inc(gsum_ready.sem, 1)
                    if u < 3:
                        ve.wait_ge(gc_done.sem, gc_done.at(l, 2 * u + 2))
                        ve.wait_ge(gs_t.sem, gs_t.at(l, u + 1))
                        cross_differences(u + 1)
                ve.wait_ge(go_copied.sem, go_copied.at(l, 4))
                step(ve.memset(mva[:, :, :, DV:DV + 1], 1.0))
                finish_sums(l, 2)
                ve.wait_ge(fin_t.sem, fin_t.at(l, 3))
                chain.settle()
                for h in range(H):
                    o = ve.scalar_tensor_tensor(pc[:, GR, h, :], bank(h)[:, 0:T], pp("hn_g")[:, h:h + 1],
                                                pc[:, GR, h, :], ALU.mult, ALU.mult)
                o.then_inc(fin_done.sem, 1)

                step(ve.memset(merged[:, :, :], 0.0))
                with ve.Fori(0, 4) as i:
                    for n in range(8):
                        e = e_t[:, n % 2, :]
                        gg = e_t[:, 2 + n % 2, :]
                        ve.wait_ge(gate_sig.sem, l * 32 + i * 8 + (n + 3))
                        ve.wait_ge(br_done.sem, l * 32 + i * 8 + (n + 1))
                        ve.tensor_tensor(gg, e, bank(2 + n % 2)[:, 0:T], ALU.mult).then_inc(merge_x.sem, 1)
                        ve.wait_ge(merge_x.sem, l * 32 + i * 8 + (n + 1))
                        ve.wait_ge(merged_s.sem, l * 32 + i * 8 + (n + 2))
                        ve.tensor_tensor(merged[:, n, :], merged[:, n, :], gg, ALU.add).then_inc(merged_s.sem, 1)
                for n in range(8):
                    ve.wait_ge(out_done.sem, out_done.at(l, n + 1))
                    for c, s in enumerate((CTX, LAT)):
                        o = ve.scalar_tensor_tensor(xT[:, n, s], bank(4 + n % 2)[:, s], mod[:, 16 + n, c:c + 1],
                                                    xT[:, n, s], ALU.mult, ALU.add)
                        if c == 0:
                            step(o)
                    o.then_inc(out_used.sem, 1)
                ve.wait_ge(out_used.sem, out_used.at(l, 8))
                ve.sem_inc(x_ready.sem, 1)
                scaled(l, 1)

                ve.wait_ge(rt_done.sem, rt_done.at(l, 1))
                step(ve.tensor_copy(rt[:, 0:60], bank(6)[:, 0:60]))
                chain.settle()

                def first_best(score, best, sel, tmp):
                    step(ve.tensor_reduce(best, score, AX.X, ALU.max))
                    chain.settle()
                    step(ve.scalar_tensor_tensor(sel, score, best, cc("order"), ALU.is_equal, ALU.mult))
                    chain.settle()
                    step(ve.tensor_reduce(tmp, sel, AX.X, ALU.max))
                    chain.settle()
                    step(ve.tensor_scalar(sel, sel, tmp, None, ALU.is_equal))
                    chain.settle()

                for t in range(NT):
                    gl, el = rt[:, t * 20:t * 20 + 4], rt[:, t * 20 + 4:t * 20 + 20]
                    best, gsel, tmp = rt[:, 60:61], rt[:, 61:65], rt[:, 65:66]
                    first_best(gl, best, gsel, tmp)
                    ve.tensor_scalar(rt[:, 100:104], gl, best, None, ALU.subtract).then_inc(rt_step.sem, 1)
                    g3 = gsel.rearrange("p (a b) -> p a b", b=1).to_broadcast([P, NG, EPG])
                    step(ve.tensor_tensor(rt[:, 70:86].rearrange("p (a b) -> p a b", a=NG),
                                          el.rearrange("p (a b) -> p a b", a=NG), g3, ALU.mult))
                    chain.settle()
                    es = rt[:, 86:90]
                    step(ve.tensor_reduce(es, rt[:, 70:86].rearrange("p (a b) -> p b a", a=NG), AX.X, ALU.add))
                    chain.settle()
                    v1, s1, v2, s2 = rt[:, 90:91], rt[:, 106:110], rt[:, 91:92], rt[:, 110:114]
                    first_best(es, v1, s1, tmp)
                    step(ve.scalar_tensor_tensor(es, s1, -3e38, es, ALU.mult, ALU.add))
                    chain.settle()
                    first_best(es, v2, s2, tmp)
                    ve.wait_ge(rt_exp.sem, rt_exp.at(l, 2 * t + 1))
                    ve.tensor_tensor(rt[:, 105:106], v2, v1, ALU.subtract).then_inc(rt_step.sem, 1)
                    ve.wait_ge(rt_exp.sem, rt_exp.at(l, 2 * t + 2))
                    step(ve.scalar_tensor_tensor(rt[:, 92:93], rt[:, 105:106], 1.0, rt[:, 104:105],
                                                 ALU.add, ALU.mult))
                    chain.settle()
                    step(ve.reciprocal(rt[:, 92:93], rt[:, 92:93]))
                    chain.settle()
                    step(ve.scalar_tensor_tensor(s1, s2, rt[:, 105:106], s1, ALU.mult, ALU.add))
                    chain.settle()
                    step(ve.tensor_scalar(s1, s1, rt[:, 92:93], None, ALU.mult))
                    chain.settle()
                    o = ve.tensor_tensor(rw[:, t, 0:NE].rearrange("p (a b) -> p a b", a=NG), g3,
                                         s1.rearrange("p (a b) -> p a b", a=1).to_broadcast([P, NG, EPG]), ALU.mult)
                    if t < NT - 1:
                        step(o)
                        chain.settle()
                o.then_inc(rt_ready.sem, 1)
                ve.wait_ge(rt_ready.sem, rt_ready.at(l, 1))
                ve.tensor_scalar(sel[:, :, :], rw[:, :, 0:NE], 0.0, None, ALU.not_equal).then_inc(sel_ready.sem, 1)
                for n in range(6):
                    half, t = divmod(n, 3)
                    ve.wait_ge(ht_done.sem, l * 6 + n + 1)
                    ve.tensor_copy(htok[half][:, t, :], bank(2 + n % 2)).then_inc(ht_copied.sem, 1)
                ve.wait_ge(rank_done.sem, rank_done.at(l, 1))
                step(ve.scalar_tensor_tensor(rk[:, :, 0:NE], bank(7)[:, 0:NT * NE].rearrange("p (t e) -> p t e", t=NT),
                                             16.0, sel[:, :, :], ALU.mult, ALU.mult))
                step(ve.tensor_reduce(rt[0:1, 120:121], bank(7)[0:1, NT * NE:(NT + 1) * NE], AX.X, ALU.max))
                chain.settle()
                ve.tensor_scalar(spill[0:1, 0:1], rt[0:1, 120:121], float(P), None, ALU.is_gt)\
                  .then_inc(spill_known.sem, 1)

                def build_slots(x):
                    for t in range(NT):
                        ve.tensor_scalar(x_p[:, t, :], cc("slots"), rk[:, t, bass.ds(x, 1)], None, ALU.is_equal)
                        o = ve.tensor_scalar(x_pw[:, t, :], cc("slots"), rk[:, t, bass.ds(x, 1)],
                                             rw[:, t, bass.ds(x, 1)], ALU.is_equal, ALU.mult)
                    o.then_inc(p_built.sem, 1)

                build_slots(0)
                with ve.Fori(0, NE // 2) as i:
                    for p in range(2):
                        ve.wait_ge(pt_done.sem, l * (NE + 1) + i * 2 + (p + 1))
                        build_slots(i * 2 + (p + 1))
                        ve.wait_ge(xs_ready.sem, l * NE + i * 2 + (p + 1))
                        ve.tensor_tensor(x_g, x_s, bank(3), ALU.mult).then_inc(xg_ready.sem, 1)
                        for n in range(KD):
                            ve.wait_ge(back_done.sem, l * 128 + i * 16 + (8 * p + n + 1))
                            for c, s in enumerate((CTX, LAT)):
                                o = ve.scalar_tensor_tensor(xT[:, n, s], bank(n % 2)[:, s],
                                                            mod[:, 40 + n, c:c + 1], xT[:, n, s], ALU.mult, ALU.add)
                            o.then_inc(back_used.sem, 1)
                ve.wait_ge(spill_known.sem, spill_known.at(l, 1))
                ve.sem_inc(spill_asked.sem, 1)
                spilled = ve.value_load(spill[0:1, 0:1], min_val=0, max_val=1)
                with ve.If(spilled > 0):
                    ve.wait_ge(back_used.sem, l * 128 + (128 + 2))
                    ve.tensor_scalar(sel[:, :, :], rk[:, :, 0:NE], float(P), None, ALU.is_gt).then_inc(sp_free.sem, 1)
                    ve.wait_ge(sp_free.sem, sp_free.at(l, 1))
                    ve.tensor_tensor(rw[:, :, 0:NE], rw[:, :, 0:NE], sel[:, :, :], ALU.mult).then_inc(sp_rw.sem, 1)
                    ve.wait_ge(rtt_done.sem, rtt_done.at(l, 1))
                    ve.tensor_copy(wT, bank(7)[0:NE, 0:T]).then_inc(wT_ready.sem, 1)
                    ve.wait_ge(wT_ready.sem, wT_ready.at(l, 1))
                    ve.tensor_scalar(wm, wT, ident[0:NE, 0:1], None, ALU.mult).then_inc(wm_ready.sem, 1)
                    with ve.Fori(0, NE // 2) as i:
                        for p in range(2):
                            for f in range(4):
                                e, s = e_t[:, f % 2, :], e_t[:, 2 + f % 2, :]
                                ve.wait_ge(a_exp.sem, l * 64 + i * 8 + (4 * p + f + 1))
                                ve.tensor_tensor(s, e, bank(2 + f % 2)[:, 0:T], ALU.mult).then_inc(e_x.sem, 1)
                                ve.wait_ge(e_x.sem, l * 64 + i * 8 + (4 * p + f + 1))
                                if f == 0:
                                    ve.wait_ge(wb_ready.sem, l * 16 + i * 2 + (p + 1))
                                    ve.wait_ge(y_used.sem, l * 128 + i * 16 + (8 * p + 2))
                                ve.tensor_tensor(gu[:, f, :], s, wb, ALU.mult).then_inc(gu_ready.sem, 1)
                            ve.tensor_scalar(wm, wT, cst[0:NE, bass.ds(i * 2 + (p + 1 + CST["ident"][0]), 1)], None,
                                             ALU.mult).then_inc(wm_ready.sem, 1)
                            for n in range(KD):
                                ve.wait_ge(y_done.sem, l * 128 + i * 16 + (8 * p + n + 1))
                                for c, s in enumerate((CTX, LAT)):
                                    o = ve.scalar_tensor_tensor(xT[:, n, s], bank(4 + n % 2)[:, s],
                                                                mod[:, 40 + n, c:c + 1], xT[:, n, s],
                                                                ALU.mult, ALU.add)
                                o.then_inc(y_used.sem, 1)
                with ve.Else():
                    ve.wait_ge(back_used.sem, l * 128 + (128 + 2))
                    for s in (sp_free, sp_rw, wT_ready, wm_ready, e_x, gu_ready, y_used):
                        ve.sem_inc(s.sem, s.per_layer)
                ve.wait_ge(y_used.sem, l * 128 + (128 + 2))
                ve.sem_inc(x_ready.sem, 1)
                ve.sem_inc(params_free.sem, 1)
            assert chain.n == DVE_STEPS, chain.n
            ve.wait_ge(final_s.sem, 2)
            for k in range(KD):
                o = ve.tensor_tensor(hT[:, k, :], xT[:, k, :], rstd[:, :], ALU.mult)
            o.then_inc(final_s.sem, 1)
            ve.wait_ge(final_s.sem, 3)
            for k in range(KD):
                o = ve.tensor_scalar(hT[:, k, :], hT[:, k, :], cc("final")[:, k:k + 1], None, ALU.mult)
            o.then_inc(final_s.sem, 1)


_STARTS = {GR: 4656, CA: 5168, CB: 5680, GQK: 3600, DQ: 2064, DKK: 2576, MO: 1536, MQ: 0, MK: 512}
_TOKEN_STARTS = (1024, 3088, 4112)
_MERGE_ORDER = (2, 3, 1, 0)


def _by_partition(w, n):
    import numpy as np
    k, cols = w.shape
    return np.ascontiguousarray(w.reshape(k // P, P, cols // n, n).transpose(2, 1, 0, 3)).reshape(cols // n, P, -1)


def _constants(inputs):
    import numpy as np
    c = np.zeros((P, NCST), np.float32)

    def put(name, v):
        c[:, CST[name][0]:CST[name][1]] = np.asarray(v, np.float32).reshape(P, -1)

    s, t = np.arange(P)[:, None], np.arange(P)[None, :]
    put("ident", s == t)
    put("swap", (s // 64 == t // 64) & (s % 32 == t % 32) & (s != t))
    n_freq = DQK // 4
    inv = 10000.0 ** (-np.arange(n_freq, dtype=np.float32) / n_freq)
    r, col = np.divmod(np.arange(DEC), 64)
    ang = np.concatenate([r[:, None] * inv, col[:, None] * inv], axis=1).astype(np.float32)
    part = np.arange(P)
    put("cos", np.cos(ang).T[part % 32])
    put("sin", np.sin(ang).T[part % 32] * np.where(part % 64 < 32, -1.0, 1.0)[:, None])
    put("tri_f", (s <= t) / 16.0)
    put("tri_b", (s >= t) / 16.0)
    put("sixteenth", np.full((P, P), 1 / 16.0))
    put("ones", np.ones((P, P)))
    put("neg_f", np.where(s <= t, 0.0, MASKED))
    put("neg_b", np.where(s >= t, 0.0, MASKED))
    i, j = s % SUB, np.arange(SUB)[None, :]
    for name, a, b in (("lev_f", i, j), ("lev_b", j, i)):
        m = np.zeros((P, NLEV, SUB))
        for lv in range(NLEV - 1):
            w = 1 << lv
            m[:, lv] = (i // (2 * w) == j // (2 * w)) & (a % (2 * w) < w) & (b % (2 * w) >= w)
        m[:, NLEV - 1] = i == j
        put(name, m)
    put("slots", np.tile(np.arange(1, P + 1), (P, 1)))
    put("order", np.tile(np.arange(NG, 0, -1), (P, 1)))
    lam = [0.8 - 0.6 * math.exp(-0.3 * l) for l in range(DEPTH)]
    put("lam_init", np.tile(lam, (P, 1)))
    put("one_less", np.tile([1.0 - v for v in lam], (P, 1)))
    put("final", inputs["final_norm"].reshape(KD, P).T)
    put("cond", np.stack([inputs["c_ctx"].reshape(KD, P).T, inputs["c"][0].reshape(KD, P).T], axis=2))
    return c


def _parameters(inputs, l):
    import numpy as np
    a = np.zeros((P, NPAR), np.float32)

    def view(name):
        return a[:, PAR[name][0]:PAR[name][1]]

    def chunks(v):
        return v.reshape(-1, P).T

    for name, key in (("norm1", "norm1"), ("norm2", "norm2"), ("bmod", "b_mod"), ("ln_g", "conv_ln_g"),
                      ("ln_b", "conv_ln_b"), ("hn_m", "hnorm_m"), ("hn_d", "hnorm_d"), ("hn_g", "hnorm_g")):
        view(name)[:] = chunks(inputs[key][l])
    view("taps")[:] = inputs["w_dw"][l].reshape(CW, 4, P).transpose(2, 1, 0).reshape(P, -1)
    for i, key in enumerate(("lam_q1", "lam_k1", "lam_q2", "lam_k2")):
        view("lam")[0:64, i] = inputs[key][l]
    w = inputs["w_in"][l]
    rows, bi, bf = np.zeros((D, P), np.float32), inputs["b_m_i"][l], inputs["b_m_f"][l]
    for d in range(2):
        rows[:, 32 * d:32 * d + 4] = w[:, 2048 + 4 * d:2052 + 4 * d]
        rows[:, 64 + 32 * d:68 + 32 * d] = w[:, 2056 + 4 * d:2060 + 4 * d]
        view("b_i")[32 * d:32 * d + 4, 0] = bi[4 * d:4 * d + 4]
        view("b_f")[64 + 32 * d:68 + 32 * d, 0] = bf[4 * d:4 * d + 4]
        view("m0")[32 * d:32 * d + 4, 0] = inputs["state_mlstm_m"][0, l, d]
    early = np.concatenate([_by_partition(rows, P)[0], _by_partition(w[:, 4624:4656], 32)[0]], axis=1)
    view("router")[:] = _by_partition(np.concatenate([inputs["w_group_router"][l], inputs["w_expert_router"][l]], 1), 20)[0]
    for d in range(2):
        view("w_up")[16 * d:16 * d + 16, 256 * d:256 * d + 256] = inputs["w_gla_up"][l, d]
        view("w_up")[32, 256 * d:256 * d + 256] = inputs["b_gla_gate"][l, d]
    view("S0")[:] = inputs["state_gla_S"][0, l].reshape(2, 2, 2, 64, P).transpose(2, 3, 0, 1, 4).reshape(P, -1)
    cn = np.concatenate([inputs["state_mlstm_C"][0, l], inputs["state_mlstm_n"][0, l][..., None]], axis=3)
    view("C0")[:] = cn.transpose(2, 0, 1, 3).reshape(P, -1)
    view("k_cache")[:] = inputs["cache_diff_k"][0, l].transpose(2, 1, 0).reshape(P, -1)
    view("v_cache")[:] = inputs["cache_diff_v"][0, l].reshape(P, -1)
    return a, early


def kernel(**inputs):
    import numpy as np
    import concourse.bacc as bacc
    from concourse.bass_utils import run_bass_kernel_spmd

    inputs = {k: np.asarray(v) for k, v in inputs.items()}
    L = range(DEPTH)
    w_in = inputs["w_in"]
    x = np.concatenate([inputs["x_prompt"][0], inputs["x_sample"][0]], axis=0)
    arrays = {
        "par": np.stack([_parameters(inputs, l)[0] for l in L]),
        "early": np.stack([_parameters(inputs, l)[1] for l in L]),
        "cst": _constants(inputs),
        "x": np.ascontiguousarray(x.T.reshape(KD, P, T).transpose(1, 0, 2)),
        "wmod": np.concatenate([_by_partition(inputs["w_mod"][l], W) for l in L]),
        "wch": np.concatenate([_by_partition(w_in[l][:, _STARTS[s]:_STARTS[s] + W], W) for l in L for s in (*range(2, NCH), 0, 1)]),
        "wtok": np.concatenate([_by_partition(w_in[l][:, s:s + W], W) for l in L for s in _TOKEN_STARTS]),
        "wgate": np.concatenate([_by_partition(w_in[l][:, 6192 + n * D:6192 + (n + 1) * D], W)
                                 for l in L for n in _MERGE_ORDER]),
        "wbr": np.concatenate([_by_partition(inputs["w_branch"][l, n], D) for l in L for n in _MERGE_ORDER]),
        "wout": np.concatenate([_by_partition(inputs["w_out"][l], W) for l in L]),
        "we13": np.concatenate([_by_partition(inputs[k][l, e // EPG, e % EPG], W)
                                for l in L for e in range(NE) for k in ("w_e1", "w_e3")]),
        "we2": np.concatenate([_by_partition(inputs["w_e2"][l, e // EPG, e % EPG], D) for l in L for e in range(NE)]),
    }
    outputs = {"y": (P, KD, T), "ko": (DEPTH, P, H, P), "vo": (DEPTH, P, W), "co": (DEPTH * 8, P, DV + 1),
               "mo": (DEPTH * 2, H, 1), "so": (DEPTH * 8, 64, P)}
    nc = bacc.Bacc("TRN2", target_bir_lowering=False, num_devices=1)
    args = [nc.dram_tensor(f"{n}_in", a.shape, F32, kind="ExternalInput").ap() for n, a in arrays.items()]
    args += [nc.dram_tensor(f"{n}_out", s, F32, kind="ExternalOutput").ap() for n, s in outputs.items()]
    hybrid_step(nc, *args)
    r = run_bass_kernel_spmd(nc, [{f"{n}_in": a for n, a in arrays.items()}], core_ids=[0]).results[0]
    y = r["y_out"].transpose(1, 0, 2).reshape(D, T).T
    ko = r["ko_out"].transpose(0, 3, 2, 1)
    vo = r["vo_out"].reshape(DEPTH, SEQ, H, DV)
    co = r["co_out"].reshape(DEPTH, 2, H, P, DV + 1)
    so = r["so_out"].reshape(DEPTH, 2, 2, 2, 64, P).transpose(0, 2, 1, 3, 4, 5).reshape(DEPTH, 2, H, 64, P)
    out = (y[:SEQ], y[SEQ:], ko, vo, co[..., :DV], co[..., DV], r["mo_out"].reshape(DEPTH, 2, H), so)
    return tuple(np.ascontiguousarray(v)[None] for v in out)
```
